# Optimizing a Trainium2 kernel written in Bass

```python
import jax, jax.numpy as jnp
from jax import lax
import numpy as np
import math

D_MODEL = 1024
BATCH = 1
SEQ = 256
DEPTH = 2

HEAD_DIM = 64
A_Q_HEADS = 8
A_KV_HEADS = 2
A_BLOCK = 128
WINDOW = 128
ROPE_THETA = 10000.0
B_HEADS = 8
GRID_W = 64
NA_MAX_KH = 8
NA_KW = 16
NA_QBLOCK_W = 16
NA_SPAN_W = 2 * NA_KW
A_Q_DIM = A_Q_HEADS * HEAD_DIM
A_KV_DIM = A_KV_HEADS * HEAD_DIM
B_DIM = B_HEADS * HEAD_DIM
ATTN_IN = A_Q_DIM + 2 * A_KV_DIM + 3 * B_DIM
ATTN_OUT = A_Q_DIM + B_DIM
SSM_D_INNER = 2 * D_MODEL
SSM_HEAD_DIM = 64
SSM_HEADS = SSM_D_INNER // SSM_HEAD_DIM
SSM_GROUPS = 8
SSM_STATE = 128
SSM_CONV = 5
SSM_CHUNK = 128
SSM_CONV_DIM = SSM_D_INNER + 2 * SSM_GROUPS * SSM_STATE
SSM_IN = SSM_D_INNER + SSM_CONV_DIM + 2 * SSM_HEADS
D_FF = 4 * D_MODEL
DN_ALPHA = (2 * DEPTH) ** 0.25
DN_BETA = (8 * DEPTH) ** -0.25
LN_EPS = 1e-5
RMS_EPS = 1e-5
NEG_INF = -1e30
N_ATTN_LAYERS = (DEPTH + 1) // 2
N_SSM_LAYERS = DEPTH // 2


def layer_norm(x, g, b):
    xf = x.astype(jnp.float32)
    mu = jnp.mean(xf, -1, keepdims=True)
    var = jnp.mean(jnp.square(xf - mu), -1, keepdims=True)
    return ((xf - mu) * lax.rsqrt(var + LN_EPS)).astype(x.dtype) * g + b

def rope(x, pos):
    half = HEAD_DIM // 2
    inv = ROPE_THETA ** (-jnp.arange(half, dtype=jnp.float32) / half)
    ang = pos.astype(jnp.float32)[:, None] * inv[None, :]
    cos = jnp.cos(ang)[None, :, None, :].astype(x.dtype)
    sin = jnp.sin(ang)[None, :, None, :].astype(x.dtype)
    x1, x2 = x[..., :half], x[..., half:]
    return jnp.concatenate([x1 * cos - x2 * sin, x2 * cos + x1 * sin], axis=-1)

def windowed_gqa_sink(q, k, v, sink):
    bsz, t = q.shape[:2]
    nb = t // A_BLOCK
    rep = A_Q_HEADS // A_KV_HEADS
    qb = q.reshape(bsz, nb, A_BLOCK, A_KV_HEADS, rep, HEAD_DIM)

    def band(u):
        ub = u.reshape(bsz, nb, A_BLOCK, A_KV_HEADS, HEAD_DIM)
        up = jnp.pad(ub, ((0, 0), (1, 1), (0, 0), (0, 0), (0, 0)))
        return jnp.concatenate([up[:, :-2], up[:, 1:-1], up[:, 2:]], axis=2)

    kb, vb = band(k), band(v)
    s = jnp.einsum('bnqgrd,bnkgd->bngrqk', qb, kb).astype(jnp.float32) * (HEAD_DIM ** -0.5)
    qi = np.arange(A_BLOCK)[:, None] + A_BLOCK
    ki = np.arange(3 * A_BLOCK)[None, :]
    kabs = (np.arange(nb)[:, None, None] - 1) * A_BLOCK + ki[None]
    valid = (np.abs(qi - ki) <= WINDOW)[None] & (kabs >= 0) & (kabs < t)
    s = jnp.where(jnp.asarray(valid)[None, :, None, None], s, NEG_INF)
    sink_l = jnp.broadcast_to(sink.astype(jnp.float32).reshape(A_KV_HEADS, rep)[None, None, :, :, None, None],
                              s.shape[:-1] + (1,))
    p = jax.nn.softmax(jnp.concatenate([s, sink_l], axis=-1), axis=-1)[..., :-1]
    o = jnp.einsum('bngrqk,bnkgd->bnqgrd', p.astype(v.dtype), vb)
    return o.reshape(bsz, t, A_Q_DIM)

def _na_static():
    ncb = GRID_W // NA_QBLOCK_W
    starts = [min(max(j * NA_QBLOCK_W - NA_KW // 2, 0), GRID_W - NA_SPAN_W) for j in range(ncb)]
    c = np.arange(GRID_W).reshape(ncb, NA_QBLOCK_W)
    cs = np.clip(c - NA_KW // 2, 0, GRID_W - NA_KW)
    kc = np.array(starts)[:, None] + np.arange(NA_SPAN_W)[None, :]
    mask = (kc[:, None, :] >= cs[:, :, None]) & (kc[:, None, :] < cs[:, :, None] + NA_KW)
    dc = np.clip(kc[:, None, :] - c[:, :, None] + NA_KW - 1, 0, 2 * NA_KW - 2)
    return starts, mask, dc

def neighborhood_attention(q, k, v, rpb):
    bsz, t = q.shape[:2]
    rows = t // GRID_W
    kh = min(NA_MAX_KH, rows)
    ncb = GRID_W // NA_QBLOCK_W
    starts, mask, dc = _na_static()
    qg = q.reshape(bsz, rows, ncb, NA_QBLOCK_W, B_HEADS, HEAD_DIM)
    kg = k.reshape(bsz, rows, GRID_W, B_HEADS, HEAD_DIM)
    vg = v.reshape(bsz, rows, GRID_W, B_HEADS, HEAD_DIM)
    mask_j = jnp.asarray(mask)[:, :, None, :]
    scale = HEAD_DIM ** -0.5

    def row_step(r):
        rs = jnp.clip(r - kh // 2, 0, rows - kh)
        k_rows = lax.dynamic_slice_in_dim(kg, rs, kh, axis=1)
        v_rows = lax.dynamic_slice_in_dim(vg, rs, kh, axis=1)
        k_blk = jnp.stack([k_rows[:, :, s0:s0 + NA_SPAN_W] for s0 in starts], axis=1)
        v_blk = jnp.stack([v_rows[:, :, s0:s0 + NA_SPAN_W] for s0 in starts], axis=1)
        q_r = lax.dynamic_index_in_dim(qg, r, axis=1, keepdims=False)
        s = jnp.einsum('bjqhd,bjakhd->bhjqak', q_r, k_blk).astype(jnp.float32) * scale
        dr = rs + jnp.arange(kh) - r + NA_MAX_KH - 1
        bias = rpb[:, dr][:, :, dc].transpose(0, 2, 3, 1, 4)
        s = jnp.where(mask_j, s + bias.astype(jnp.float32), NEG_INF)
        p = jax.nn.softmax(s.reshape(s.shape[:-2] + (kh * NA_SPAN_W,)), axis=-1).reshape(s.shape)
        o = jnp.einsum('bhjqak,bjakhd->bjqhd', p.astype(v.dtype), v_blk)
        return o.reshape(bsz, GRID_W, B_DIM)

    out = lax.map(row_step, jnp.arange(rows))
    return out.transpose(1, 0, 2, 3).reshape(bsz, t, B_DIM)

def attention_mixer(x, w_in, sink, rpb, w_out):
    bsz, t, _ = x.shape
    h = x @ w_in
    qa, ka, va, qb, kb, vb = jnp.split(
        h, [A_Q_DIM, A_Q_DIM + A_KV_DIM, A_Q_DIM + 2 * A_KV_DIM,
            A_Q_DIM + 2 * A_KV_DIM + B_DIM, A_Q_DIM + 2 * A_KV_DIM + 2 * B_DIM], axis=-1)
    pos = jnp.arange(t)
    qa = rope(qa.reshape(bsz, t, A_Q_HEADS, HEAD_DIM), pos)
    ka = rope(ka.reshape(bsz, t, A_KV_HEADS, HEAD_DIM), pos)
    va = va.reshape(bsz, t, A_KV_HEADS, HEAD_DIM)
    oa = windowed_gqa_sink(qa, ka, va, sink)
    shp = (bsz, t, B_HEADS, HEAD_DIM)
    ob = neighborhood_attention(qb.reshape(shp), kb.reshape(shp), vb.reshape(shp), rpb)
    return jnp.concatenate([oa, ob], axis=-1) @ w_out

def depthwise_conv_centred(u, w, b):
    c = u.shape[-1]
    pad = SSM_CONV // 2
    out = lax.conv_general_dilated(u, w[:, None, :].astype(u.dtype), window_strides=(1,),
                                   padding=[(pad, pad)], dimension_numbers=('NWC', 'WIO', 'NWC'),
                                   feature_group_count=c)
    return out + b

def ssd_chunked(x, dt, a_neg, bm, cm):
    bsz, t = x.shape[:2]
    nc, L, G, R = t // SSM_CHUNK, SSM_CHUNK, SSM_GROUPS, SSM_HEADS // SSM_GROUPS
    x = x.astype(jnp.float32)
    dt = dt.astype(jnp.float32)
    xc = (x * dt[..., None]).reshape(bsz, nc, L, G, R, SSM_HEAD_DIM)
    a = (dt * a_neg.astype(jnp.float32)).reshape(bsz, nc, L, G, R).transpose(0, 1, 3, 4, 2)
    acum = jnp.cumsum(a, axis=-1)
    bc = bm.astype(jnp.float32).reshape(bsz, nc, L, G, SSM_STATE)
    cc = cm.astype(jnp.float32).reshape(bsz, nc, L, G, SSM_STATE)
    tri = jnp.tril(jnp.ones((L, L), dtype=bool))
    lmat = jnp.exp(jnp.where(tri, acum[..., :, None] - acum[..., None, :], -jnp.inf))
    cb = jnp.einsum('bclgn,bcsgn->bcgls', cc, bc)
    y_diag = jnp.einsum('bcgrls,bcsgrp->bclgrp', cb[:, :, :, None] * lmat, xc)
    decay_states = jnp.exp(acum[..., -1:] - acum)
    states = jnp.einsum('bcsgn,bcgrs,bcsgrp->bcgrpn', bc, decay_states, xc)
    chunk_decay = jnp.exp(acum[..., -1])

    def step(h, inp):
        st, dec = inp
        return h * dec[..., None, None] + st, h

    h0 = jnp.zeros((bsz, G, R, SSM_HEAD_DIM, SSM_STATE), jnp.float32)
    _, prev = lax.scan(step, h0, (jnp.moveaxis(states, 1, 0), jnp.moveaxis(chunk_decay, 1, 0)))
    prev = jnp.moveaxis(prev, 0, 1)
    y_off = jnp.einsum('bclgn,bcgrpn,bcgrl->bclgrp', cc, prev, jnp.exp(acum))
    return (y_diag + y_off).reshape(bsz, t, SSM_HEADS, SSM_HEAD_DIM)

def mamba2_bidir_mixer(x, w_in, conv_w, conv_b, dt_bias, a_log, d_skip, norm_w, w_out):
    bsz, t, _ = x.shape
    zxbcdt = x @ w_in
    z, xbc, dt = jnp.split(zxbcdt, [SSM_D_INNER, SSM_D_INNER + SSM_CONV_DIM], axis=-1)
    xbc = jax.nn.silu(depthwise_conv_centred(xbc, conv_w, conv_b))
    xs, bm, cm = jnp.split(xbc, [SSM_D_INNER, SSM_D_INNER + SSM_GROUPS * SSM_STATE], axis=-1)
    xs = xs.reshape(bsz, t, SSM_HEADS, SSM_HEAD_DIM)
    bm = bm.reshape(bsz, t, SSM_GROUPS, SSM_STATE)
    cm = cm.reshape(bsz, t, SSM_GROUPS, SSM_STATE)
    dt = jax.nn.softplus((dt + dt_bias).astype(jnp.float32))
    dt_f, dt_b = dt[..., :SSM_HEADS], dt[..., SSM_HEADS:]
    a_neg = -jnp.exp(a_log.astype(jnp.float32))
    y_f = ssd_chunked(xs, dt_f, a_neg[0], bm, cm)
    flip = lambda u: jnp.flip(u, axis=1)
    y_b = flip(ssd_chunked(flip(xs), flip(dt_b), a_neg[1], flip(bm), flip(cm)))
    y = (y_f + y_b).astype(x.dtype) + xs * d_skip[:, None]
    y = y.reshape(bsz, t, SSM_D_INNER) * jax.nn.silu(z)
    yg = y.astype(jnp.float32).reshape(bsz, t, SSM_GROUPS, SSM_D_INNER // SSM_GROUPS)
    yg = yg * lax.rsqrt(jnp.mean(jnp.square(yg), -1, keepdims=True) + RMS_EPS)
    y = yg.reshape(bsz, t, SSM_D_INNER).astype(x.dtype) * norm_w
    return y @ w_out

def squared_relu_mlp(x, w1, w2):
    return jnp.square(jax.nn.relu(x @ w1)) @ w2

def first_inputs(seed: int = 0) -> dict:
    key = jax.random.key(seed)
    ks = jax.random.split(key, 20)
    f32 = jnp.float32
    nrm = lambda k, shp, sc: jax.random.normal(k, shp, f32) * sc
    dt0 = jnp.exp(jax.random.uniform(ks[9], (N_SSM_LAYERS, 2 * SSM_HEADS), f32,
                                     jnp.log(1e-3), jnp.log(1e-1)))
    return {
        "x": nrm(ks[0], (BATCH, SEQ, D_MODEL), 1.0),
        "attn_w_in": nrm(ks[1], (N_ATTN_LAYERS, D_MODEL, ATTN_IN), D_MODEL ** -0.5),
        "attn_sink": nrm(ks[2], (N_ATTN_LAYERS, A_Q_HEADS), 1.0),
        "attn_rpb": nrm(ks[3], (N_ATTN_LAYERS, B_HEADS, 2 * NA_MAX_KH - 1, 2 * NA_KW - 1), 0.1),
        "attn_w_out": nrm(ks[4], (N_ATTN_LAYERS, ATTN_OUT, D_MODEL), ATTN_OUT ** -0.5 * DN_BETA),
        "ssm_w_in": nrm(ks[5], (N_SSM_LAYERS, D_MODEL, SSM_IN), D_MODEL ** -0.5),
        "ssm_conv_w": nrm(ks[6], (N_SSM_LAYERS, SSM_CONV, SSM_CONV_DIM), SSM_CONV ** -0.5),
        "ssm_conv_b": nrm(ks[7], (N_SSM_LAYERS, SSM_CONV_DIM), 0.02),
        "ssm_dt_bias": dt0 + jnp.log(-jnp.expm1(-dt0)),
        "ssm_A_log": jnp.log(jax.random.uniform(ks[10], (N_SSM_LAYERS, 2, SSM_HEADS), f32, 1.0, 16.0)),
        "ssm_D": 1.0 + nrm(ks[11], (N_SSM_LAYERS, SSM_HEADS), 0.05),
        "ssm_norm_w": 1.0 + nrm(ks[12], (N_SSM_LAYERS, SSM_D_INNER), 0.05),
        "ssm_w_out": nrm(ks[13], (N_SSM_LAYERS, SSM_D_INNER, D_MODEL), SSM_D_INNER ** -0.5 * DN_BETA),
        "mlp_w1": nrm(ks[14], (DEPTH, D_MODEL, D_FF), D_MODEL ** -0.5),
        "mlp_w2": nrm(ks[15], (DEPTH, D_FF, D_MODEL), D_FF ** -0.5 * DN_BETA),
        "ln1_g": 1.0 + nrm(ks[16], (DEPTH, D_MODEL), 0.05),
        "ln1_b": nrm(ks[17], (DEPTH, D_MODEL), 0.02),
        "ln2_g": 1.0 + nrm(ks[18], (DEPTH, D_MODEL), 0.05),
        "ln2_b": nrm(ks[19], (DEPTH, D_MODEL), 0.02),
    }

def first_block(x, attn_w_in, attn_sink, attn_rpb, attn_w_out, ssm_w_in, ssm_conv_w, ssm_conv_b,
              ssm_dt_bias, ssm_A_log, ssm_D, ssm_norm_w, ssm_w_out, mlp_w1, mlp_w2,
              ln1_g, ln1_b, ln2_g, ln2_b):
    for i in range(DEPTH):
        j = i // 2
        if i % 2 == 0:
            mix = attention_mixer(x, attn_w_in[j], attn_sink[j], attn_rpb[j], attn_w_out[j])
        else:
            mix = mamba2_bidir_mixer(x, ssm_w_in[j], ssm_conv_w[j], ssm_conv_b[j], ssm_dt_bias[j],
                                     ssm_A_log[j], ssm_D[j], ssm_norm_w[j], ssm_w_out[j])
        x = layer_norm(DN_ALPHA * x + mix, ln1_g[i], ln1_b[i])
        x = layer_norm(DN_ALPHA * x + squared_relu_mlp(x, mlp_w1[i], mlp_w2[i]), ln2_g[i], ln2_b[i])
    return x


MIX_WIDTH = D_MODEL
CONV_CH = MIX_WIDTH // 2
CONV_GROUPS = 8
CONV_K = 31
DIFF_WIDTH = MIX_WIDTH - CONV_CH
N_DIFF_HEADS = DIFF_WIDTH // (2 * HEAD_DIM)
D_FF_2 = 2816
NUM_BUCKETS = 32
MAX_DISTANCE = 128
BLOCK_Q = 128
EPS = 1e-6
IN_COLS = 2 * CONV_CH + 3 * DIFF_WIDTH


def rms_norm(x, g):
    xf = x.astype(jnp.float32)
    y = xf * lax.rsqrt(jnp.mean(xf * xf, axis=-1, keepdims=True) + EPS)
    return (y * g.astype(jnp.float32)).astype(x.dtype)

def swiglu(h, w_gate, w_up, w_down):
    return (jax.nn.silu(h @ w_gate) * (h @ w_up)) @ w_down

def lambda_init_fn(layer_idx):
    return 0.8 - 0.6 * math.exp(-0.3 * layer_idx)

def rel_bucket(n):
    max_exact = NUM_BUCKETS // 2
    nf = jnp.maximum(n, 1).astype(jnp.float32)
    large = max_exact + (jnp.log(nf / max_exact) / math.log(MAX_DISTANCE / max_exact)
                         * (NUM_BUCKETS - max_exact)).astype(jnp.int32)
    large = jnp.minimum(large, NUM_BUCKETS - 1)
    return jnp.where(n < max_exact, n, large)

def conv_module(a, g, conv_w, conv_b, conv_norm):
    u = a * jax.nn.sigmoid(g)
    rhs = conv_w[:, None, :].astype(u.dtype)
    y = lax.conv_general_dilated(u, rhs, window_strides=(1,), padding=[(CONV_K - 1, 0)],
                                 dimension_numbers=("NWC", "WIO", "NWC"),
                                 feature_group_count=CONV_CH)
    y = y + conv_b
    return jax.nn.silu(rms_norm(y, conv_norm))

def diff_attention(q, k, v, rel_bias, lam, lam_init, subln_g):
    B, H, _, S, d = q.shape
    nb = S // BLOCK_Q
    scale = 1.0 / math.sqrt(d)
    qb = q.reshape(B, H, 2, nb, BLOCK_Q, d).transpose(3, 0, 1, 2, 4, 5)
    k_pos = jnp.arange(S, dtype=jnp.int32)
    bias_tab = rel_bias.astype(jnp.float32)

    def block(args):
        qi, i = args
        q_pos = i * BLOCK_Q + jnp.arange(BLOCK_Q, dtype=jnp.int32)
        dist = q_pos[:, None] - k_pos[None, :]
        bias = bias_tab[rel_bucket(jnp.maximum(dist, 0))].transpose(2, 0, 1)
        s = jnp.einsum("bhmqd,bhmkd->bhmqk", qi, k).astype(jnp.float32) * scale
        s = s + bias[None, :, None]
        s = jnp.where((dist >= 0)[None, None, None], s, -1e30)
        p = jax.nn.softmax(s, axis=-1)
        a = p[:, :, 0] - lam * p[:, :, 1]
        return jnp.einsum("bhqk,bhkd->bhqd", a.astype(v.dtype), v)

    o = lax.map(block, (qb, jnp.arange(nb, dtype=jnp.int32)))
    o = o.transpose(1, 0, 3, 2, 4).reshape(B, S, H, 2 * d)
    o = rms_norm(o, subln_g) * (1.0 - lam_init)
    return o.reshape(B, S, H * 2 * d)

def second_inputs(seed: int = 0) -> dict:
    key = jax.random.key(seed)
    ks = jax.random.split(key, 24)
    f32 = jnp.float32

    def nrm(k, shape, scale):
        return jax.random.normal(k, shape, f32) * scale

    def gain(k, shape):
        return 1.0 + 0.02 * jax.random.normal(k, shape, f32)

    L = DEPTH
    return {
        "x": jax.random.normal(ks[0], (BATCH, SEQ, D_MODEL), f32),
        "rel_bias": nrm(ks[1], (NUM_BUCKETS, N_DIFF_HEADS), 0.5),
        "ffn1_norm": gain(ks[2], (L, D_MODEL)),
        "ffn1_w_gate": nrm(ks[3], (L, D_MODEL, D_FF_2), D_MODEL ** -0.5),
        "ffn1_w_up": nrm(ks[4], (L, D_MODEL, D_FF_2), D_MODEL ** -0.5),
        "ffn1_w_down": nrm(ks[5], (L, D_FF_2, D_MODEL), D_FF_2 ** -0.5),
        "mix_norm": gain(ks[6], (L, D_MODEL)),
        "w_in": nrm(ks[7], (L, D_MODEL, IN_COLS), D_MODEL ** -0.5),
        "conv_w": nrm(ks[8], (L, CONV_K, CONV_CH), CONV_K ** -0.5),
        "conv_b": nrm(ks[9], (L, CONV_CH), 0.02),
        "conv_norm": gain(ks[10], (L, CONV_CH)),
        "q_norm": gain(ks[11], (L, HEAD_DIM)),
        "k_norm": gain(ks[12], (L, HEAD_DIM)),
        "lambda_q1": nrm(ks[13], (L, HEAD_DIM), 0.1),
        "lambda_k1": nrm(ks[14], (L, HEAD_DIM), 0.1),
        "lambda_q2": nrm(ks[15], (L, HEAD_DIM), 0.1),
        "lambda_k2": nrm(ks[16], (L, HEAD_DIM), 0.1),
        "subln_norm": gain(ks[17], (L, 2 * HEAD_DIM)),
        "w_out": nrm(ks[18], (L, MIX_WIDTH, D_MODEL), MIX_WIDTH ** -0.5),
        "ffn2_norm": gain(ks[19], (L, D_MODEL)),
        "ffn2_w_gate": nrm(ks[20], (L, D_MODEL, D_FF_2), D_MODEL ** -0.5),
        "ffn2_w_up": nrm(ks[21], (L, D_MODEL, D_FF_2), D_MODEL ** -0.5),
        "ffn2_w_down": nrm(ks[22], (L, D_FF_2, D_MODEL), D_FF_2 ** -0.5),
    }

def second_block(x, rel_bias, ffn1_norm, ffn1_w_gate, ffn1_w_up, ffn1_w_down, mix_norm, w_in,
              conv_w, conv_b, conv_norm, q_norm, k_norm, lambda_q1, lambda_k1, lambda_q2,
              lambda_k2, subln_norm, w_out, ffn2_norm, ffn2_w_gate, ffn2_w_up, ffn2_w_down):
    B, S, _ = x.shape
    H, d = N_DIFF_HEADS, HEAD_DIM
    splits = np.cumsum([CONV_CH, CONV_CH, DIFF_WIDTH, DIFF_WIDTH]).tolist()
    for l in range(DEPTH):
        x = x + 0.5 * swiglu(rms_norm(x, ffn1_norm[l]), ffn1_w_gate[l], ffn1_w_up[l], ffn1_w_down[l])

        h = rms_norm(x, mix_norm[l])
        a, g, q, k, v = jnp.split(h @ w_in[l], splits, axis=-1)

        conv_out = conv_module(a, g, conv_w[l], conv_b[l], conv_norm[l])

        q = q.reshape(B, S, H, 2, d).transpose(0, 2, 3, 1, 4)
        k = k.reshape(B, S, H, 2, d).transpose(0, 2, 3, 1, 4)
        q = rms_norm(q, q_norm[l])
        k = rms_norm(k, k_norm[l])
        v = v.reshape(B, S, H, 2 * d).transpose(0, 2, 1, 3)
        lam_init = lambda_init_fn(l)
        lam = (jnp.exp(jnp.sum(lambda_q1[l].astype(jnp.float32) * lambda_k1[l].astype(jnp.float32)))
               - jnp.exp(jnp.sum(lambda_q2[l].astype(jnp.float32) * lambda_k2[l].astype(jnp.float32)))
               + lam_init)
        diff_out = diff_attention(q, k, v, rel_bias, lam, lam_init, subln_norm[l])

        x = x + jnp.concatenate([conv_out, diff_out], axis=-1) @ w_out[l]

        x = x + 0.5 * swiglu(rms_norm(x, ffn2_norm[l]), ffn2_w_gate[l], ffn2_w_up[l], ffn2_w_down[l])
    return x


def setup_inputs(seed=0):
    out = dict(first_inputs(seed))
    for name, value in second_inputs(seed + 1).items():
        if name != "x":
            out[name + "_2"] = value
    return out


def reference(
    x, attn_w_in, attn_sink, attn_rpb, attn_w_out, ssm_w_in, ssm_conv_w, ssm_conv_b,
    ssm_dt_bias, ssm_A_log, ssm_D, ssm_norm_w, ssm_w_out, mlp_w1, mlp_w2, ln1_g, ln1_b, ln2_g,
    ln2_b, rel_bias_2, ffn1_norm_2, ffn1_w_gate_2, ffn1_w_up_2, ffn1_w_down_2, mix_norm_2,
    w_in_2, conv_w_2, conv_b_2, conv_norm_2, q_norm_2, k_norm_2, lambda_q1_2, lambda_k1_2,
    lambda_q2_2, lambda_k2_2, subln_norm_2, w_out_2, ffn2_norm_2, ffn2_w_gate_2, ffn2_w_up_2,
    ffn2_w_down_2,
):
    x = first_block(
        x, attn_w_in, attn_sink, attn_rpb, attn_w_out, ssm_w_in, ssm_conv_w, ssm_conv_b,
        ssm_dt_bias, ssm_A_log, ssm_D, ssm_norm_w, ssm_w_out, mlp_w1, mlp_w2, ln1_g, ln1_b,
        ln2_g, ln2_b,
    )
    return second_block(
        x, rel_bias_2, ffn1_norm_2, ffn1_w_gate_2, ffn1_w_up_2, ffn1_w_down_2, mix_norm_2,
        w_in_2, conv_w_2, conv_b_2, conv_norm_2, q_norm_2, k_norm_2, lambda_q1_2, lambda_k1_2,
        lambda_q2_2, lambda_k2_2, subln_norm_2, w_out_2, ffn2_norm_2, ffn2_w_gate_2,
        ffn2_w_up_2, ffn2_w_down_2,
    )


_drawn_inputs = setup_inputs


def setup_inputs(seed=0):
    import zlib

    import numpy as np

    out = dict(_drawn_inputs(seed))
    spreads = {}
    factors = {'attn_sink': 8.0,
     'attn_rpb': 8.0,
     'ssm_conv_b': 4.026,
     'ssm_D': 4.839,
     'ffn1_norm_2': 4.919,
     'mix_norm_2': 2.914,
     'conv_norm_2': 20.475,
     'q_norm_2': 6.886,
     'k_norm_2': 7.37,
     'lambda_q2_2': 6.746,
     'lambda_k2_2': 3.6,
     'subln_norm_2': 18.095,
     'ffn2_norm_2': 6.152,
     'conv_b_2': 5.845,
     'lambda_q1_2': 5.435}
    for name, (base, spread) in spreads.items():
        noise = np.random.default_rng([zlib.crc32(name.encode()), seed]).standard_normal(out[name].shape)
        drawn = base * np.exp(spread * noise) if base else spread * noise
        out[name] = __import__('jax').numpy.asarray(drawn.astype(out[name].dtype))
    for name, factor in factors.items():
        out[name] = (out[name] * factor).astype(out[name].dtype)
    return out
```

```python
from contextlib import ExitStack
import math

import numpy as np

import concourse.bass as bass
from concourse import mybir

F32 = mybir.dt.float32
F32R = mybir.dt.float32r
ACT = mybir.ActivationFunctionType
ALU = mybir.AluOpType
AX = mybir.AxisListType

P = 128
T = 256
TT = T // P
D = 1024
KC = D // P
HD = 64
DEPTH = 2
ALPHA = float((2 * DEPTH) ** 0.25)
LN_EPS = 1e-5
NEG = -1e30
SCALE = HD ** -0.5

AQ, AKV, BH = 8, 2, 8
A_COLS = (AQ + 2 * AKV + 3 * BH) * HD
GRID_W, NA_KW, NA_KH = 64, 16, 8
WINDOW = 128
RPB_R, RPB_C = 2 * NA_KH - 1, 2 * NA_KW - 1
DI = 2 * D
SH = DI // HD
SG, SN = 8, 128
GH = SH // SG
CONV = 5
F1 = 4 * D
CCH = 512
CK = 31
DH = 4
F2 = 2816
BUCKETS = 32
EPS2 = 1e-6

U = 256
UN = KC * U
RING = 3

A_UNITS = A_COLS // U
Z_UNITS = DI // U
OUT_UNITS = D // U
SSM_COLS = [2 * DI + i * U for i in range(2)] + [2 * DI + 2 * SG * SN] + [2 * DI + i * U for i in range(2, 8)] \
    + [DI + i * U for i in range(Z_UNITS)] + [i * U for i in range(Z_UNITS)]
DT_AT = 2
G1, G2 = F1 // U, F2 // U
MIX_COLS = [2 * U, 0, 3 * U, U] + [2 * CCH + i * U for i in range(6)]
U_ATT = 0
U_ATT_OUT = U_ATT + A_UNITS
U_MLP = [U_ATT_OUT + OUT_UNITS, 0]
U_SSM = U_MLP[0] + 2 * G1
U_SSM_OUT = U_SSM + len(SSM_COLS)
U_MLP[1] = U_SSM_OUT + DI // U
U_SECOND = U_MLP[1] + 2 * G1
U_FFN, U_MIX, U_MIX_OUT = [], [], []
_u = U_SECOND
for _l in range(DEPTH):
    U_FFN.append(_u)
    U_MIX.append(_u + 3 * G2)
    U_MIX_OUT.append(U_MIX[-1] + len(MIX_COLS))
    U_FFN.append(U_MIX_OUT[-1] + OUT_UNITS)
    _u = U_FFN[-1] + 3 * G2
N_UNITS = _u
HG_MLP = [0, G1]
HG_FFN = [2 * G1 + i * G2 for i in range(2 * DEPTH)]

TURNS = ["x", "ln1_0", "ln2_0", "y", "ln1_1"] + [f"{s}_{l}" for l in range(DEPTH) for s in ("ffn1", "mix", "ffn2")]
TURN_CHUNKS = [DI // P if n == "y" else KC for n in TURNS]
TURN_BANK = [sum(TURN_CHUNKS[:i]) // 2 for i in range(len(TURNS) + 1)]

COL = {"ln1_g": 0, "ln1_b": 16, "ln2_g": 32, "ln2_b": 48, "ffn1": 64, "mix": 80, "ffn2": 96, "ssm_norm": 112,
       "ssm_conv_w": 128, "ssm_conv_b": 288, "conv_b": 320, "conv_norm": 328, "subln": 336, "q_norm": 338,
       "k_norm": 340, "conv_w": 384}
ROW_BLOCKS = [128, 128, 86, 124, 124]
COL["conv_w1"] = 512

CONST = {}
_at = 0
for _n, _w in (("ident", P), ("rot", P), ("dup0", P), ("rdup0", P), ("dup1", P), ("rdup1", P), ("na_flip", P),
               ("cos", T), ("sin", T), ("mask_a", 2 * T), ("mask_na", 2 * T),
               ("mask_ssm", 256), ("select", 64), ("nselect", 64),
               ("flip", P), ("halves", P), ("causal", 384), ("buckets", 384)):
    CONST[_n] = (_at, _w)
    _at += _w
CONST_W = _at


def shape_constants():
    c = np.zeros((P, CONST_W), np.float32)

    def put(name, a):
        at, w = CONST[name]
        assert a.shape[1] == w
        c[:a.shape[0], at:at + w] = a

    eye = np.eye(P, dtype=np.float32)
    put("ident", eye)
    half = HD // 2
    rot = np.zeros((P, P), np.float32)
    for b in range(0, P, HD):
        for i in range(half):
            rot[b + half + i, b + i] = -1.0
            rot[b + i, b + half + i] = 1.0
    put("rot", rot)
    for j in range(2):
        dup = np.zeros((P, P), np.float32)
        for b in range(0, P, HD):
            for i in range(HD):
                dup[j * HD + i, b + i] = 1.0
        put(f"dup{j}", dup)
        put(f"rdup{j}", dup @ rot)
    flip = eye[::-1].copy()
    put("flip", flip)
    na = np.zeros((P, P), np.float32)
    for b in range(0, P, 64):
        for i in range(64):
            na[b + 63 - i, b + i] = 1.0
    put("na_flip", na)
    inv = (10000.0 ** (-np.arange(half, dtype=np.float32) / half)).astype(np.float32)
    ang = (np.arange(T, dtype=np.float32)[:, None] * inv[None, :]).astype(np.float32)
    put("cos", np.tile(np.cos(ang).T, (P // half, 1)).astype(np.float32))
    put("sin", np.tile(np.sin(ang).T, (P // half, 1)).astype(np.float32))
    q = np.arange(T)
    far = np.abs(q[:, None] - q[None, :]) > WINDOW
    put("mask_a", np.where(far, np.float32(NEG), np.float32(0)).reshape(2, P, T).transpose(1, 0, 2).reshape(P, 2 * T))
    col = q % GRID_W
    lo = np.clip(col - NA_KW // 2, 0, GRID_W - NA_KW)
    inside = (col[None, :] >= lo[:, None]) & (col[None, :] < lo[:, None] + NA_KW)
    put("mask_na", np.where(inside, np.float32(0), np.float32(NEG)).reshape(2, P, T).transpose(1, 0, 2)
        .reshape(P, 2 * T))
    s, l = np.arange(P)[:, None], np.arange(P)[None, :]
    put("mask_ssm", np.where(np.concatenate([s > l, s < l], 1), np.float32(NEG), np.float32(0)))
    sel = np.concatenate([np.eye(64), np.eye(64)]).astype(np.float32)
    put("select", sel)
    put("nselect", -sel)
    put("halves", np.kron(np.eye(2), np.ones((64, 64))).astype(np.float32))
    k0, k1 = np.arange(P)[None, :], np.arange(T)[None, :]
    put("causal", np.where(np.concatenate([k0 > s, k1 > s + P], 1), np.float32(NEG), np.float32(0)))
    dist = np.maximum(255 - np.arange(384), 0)
    exact = BUCKETS // 2
    nf = np.maximum(dist, 1).astype(np.float32)
    large = exact + (np.log(nf / np.float32(exact)) / np.float32(math.log(128 / exact))
                     * np.float32(BUCKETS - exact)).astype(np.int32)
    bucket = np.where(dist < exact, dist, np.minimum(large, BUCKETS - 1))
    put("buckets", (bucket[None, :] == np.arange(BUCKETS)[:, None]).astype(np.float32))
    return c


XN2 = [[8, 10, 12], [14, 16, 18]]
N_XNEW = 20
STD2 = [[5, 6, 7], [8, 9, 10]]
N_PAR = 20


def lambda_init(l):
    return 0.8 - 0.6 * math.exp(-0.3 * l)


def two_blocks(nc, A, out):
    with ExitStack() as ctx:
        def sb(name, shape, dt=F32):
            return ctx.enter_context(nc.sbuf_tensor(name, shape, dt))

        def sem(name):
            return ctx.enter_context(nc.semaphore(name))

        w_raw = sb("w_raw", [P, RING, UN])
        w_hi = sb("w_hi", [P, RING, UN], F32R)
        w_lo = sb("w_lo", [P, RING, UN], F32R)
        op_hi = sb("op_hi", [P, 16, T], F32R)
        op_lo = sb("op_lo", [P, 16, T], F32R)
        X = sb("X", [P, TT, D])
        xn = sb("xn", [P, TT, D])
        turn_buf = sb("turn_buf", [P, 2, 2, T])
        act_buf = sb("act_buf", [P, 2 * T])
        h32 = sb("h32", [P, 2 * T])
        gain_row = sb("gain_row", [P, D])
        bias_row = sb("bias_row", [P, D])
        prow = sb("prow", [P, 5, P])
        pcol = sb("pcol", [P, 5 * P])
        ident = sb("ident", [P, P])
        stats = sb("stats", [P, TT, 2, 6])
        mv = sb("mv", [P, TT, 2])
        std = sb("std", [P, TT])
        rstd = sb("rstd", [P, TT])
        ssum = sb("ssum", [P, TT])
        lnb = sb("lnb", [P, 4])
        zeros = sb("zeros", [P, 512], mybir.dt.bfloat16)
        select = sb("select", [P, 64], F32R)
        nselect = sb("nselect", [P, 64], F32R)
        neg_tri = sb("neg_tri", [P, 2, P], F32R)
        ident_r = sb("ident_r", [P, P], F32R)
        g_pair = sb("g_pair", [P, T], F32R)
        AR = 15872
        arena = sb("arena", [P, AR])

        acc = ctx.enter_context(nc.psum_tensor("acc", [P, 4, 512], F32))
        pg = ctx.enter_context(nc.psum_tensor("pg", [P, 4, 512], F32))

        class Carve:
            def __init__(self, at=0):
                self.at = at

            def __call__(self, *shape):
                n = int(np.prod(shape))
                v = arena[:, self.at:self.at + n]
                self.at += n
                assert self.at <= AR, self.at
                if len(shape) == 2:
                    v = v.rearrange("p (a b) -> p a b", a=shape[0])
                elif len(shape) == 3:
                    v = v.rearrange("p (a b c) -> p a b c", a=shape[0], b=shape[1])
                return v

        cv = Carve()
        n_att = CONST["mask_ssm"][0] - P
        att_c = cv(n_att)

        def att_const(name):
            at, w = CONST[name]
            return att_c[:, at - P:at - P + w]

        q_raw = cv(2, 2 * T)
        r_tmp = cv(2, 2 * T)
        k_raw = cv(T)
        QT = cv(8, T)
        KT = cv(6, T)
        va = cv(TT, AKV * HD)
        vb = cv(TT, BH * HD)
        na_bias = cv(BH, 2, T)
        prob = cv(3, 2, T)
        probT = turn_buf
        sink = cv(16)
        mx = cv(16, 2)
        nmx = cv(16, 2)
        psm = cv(16, 2)
        pes = cv(16, 2)
        pden = cv(16, 2)
        cv = Carve()
        BT = cv(SG, T)
        CT = cv(SG, T)
        xs = cv(TT, DI)
        silz = cv(TT, DI)
        ssd_at = cv.at
        E = cv(2, 768)
        CB = cv(2, 768)
        conv_in = Carve(ssd_at)
        over = Carve(ssd_at)
        conv_in = over(2, 2, T + CONV - 1)
        xsT = over(2, 2, T)
        conv_sum = over(2, 2, T)
        assert over.at <= cv.at + 40
        cv.at = max(cv.at, over.at)
        ssm_c = prow[:, :, :].rearrange("p a n -> p (a n)")[:, 0:384]
        dt_bias = cv(64)
        d_skip = cv(SH)
        a_col = cv(1)
        dt_tok = cv(TT, 64)
        one_col = cv(1)
        aT, gT = act_buf[:, 0:T], act_buf[:, T:2 * T]
        dt_v, dt_a = (h32[:, i * P:i * P + P].rearrange("p (t n) -> p t n", t=TT) for i in range(2))
        xD = [b[:, :].rearrange("p (t n) -> p t n", t=TT) for b in (act_buf, h32)]
        ysq = cv(TT, SG)
        yrs = cv(TT, SG)
        xdt = xn[:, :, :].rearrange("p a (b c) -> p (a b) c", b=4)
        cv = Carve()
        blk_c = cv(CONST_W - CONST["flip"][0])

        def blk_const(name):
            at, w = CONST[name]
            at -= CONST["flip"][0]
            return blk_c[:, at:at + w]

        ones_m = cv(P)
        rbias = cv(DH, 384)
        rel = cv(DH)
        rvec = cv(384)
        lam_q = cv(4, HD)
        lam_k = cv(4, HD)
        lam_s = cv(4)
        lam_e = cv(4)
        nlam = cv(2)
        sub_g = cv(2)
        gate = cv(2, T)
        uu = cv(4, T + CK - 1)
        cacc = cv(4, T)
        ptmp = cv(T)
        sq = turn_buf[:, :, :, :].rearrange("p a b t -> p a (b t)")
        sdev = cv(2, 2 * T)
        Q2 = cv(DH, T)
        K2 = cv(DH, T)
        V2 = cv(TT, 2 * T)
        prob2 = cv(4, 384)
        pmix = cv(2, 384)
        pmixT = cv(2, 384)
        O2 = cv(DH, T)
        osq = cv(4, T)
        odev = xn[:, 0, :].rearrange("p (a t) -> p a t", a=4)
        c32 = xn[:, 1, :].rearrange("p (a t) -> p a t", a=4)
        m2 = cv(8, 2)
        n2 = cv(8, 2)
        s2 = cv(8, 2)
        r2 = cv(8, 2)

        rel_dram = nc.dram_tensor("rel_scratch", (DH, 384), F32, kind="Internal").ap()

        raw_ready = [sem(f"raw_ready{i}") for i in range(RING)]
        hi_ready = sem("hi_ready")
        lo_ready = sem("lo_ready")
        unit_done = sem("unit_done")
        x_in = sem("x_in")
        par_in = sem("par_in")
        const_in = sem("const_in")
        small_in = sem("small_in")
        bias_in = sem("bias_in")
        par_turned = sem("par_turned")
        par_ready = sem("par_ready")
        fixed_ready = sem("fixed_ready")
        bias_flipped = sem("bias_flipped")
        bias_ready = sem("bias_ready")
        norm_ready = sem("norm_ready")
        turned = sem("turned")
        gained = sem("gained")
        xt_ready = sem("xt_ready")
        x_new = sem("x_new")
        var_ready = sem("var_ready")
        std_ready = sem("std_ready")
        rows_in = sem("rows_in")
        x_settled = sem("x_settled")
        dve_link = sem("dve_link")
        act_link = sem("act_link")
        pool_link = sem("pool_link")
        attn_evac = sem("attn_evac")
        rot_done = sem("rot_done")
        rope_done = sem("rope_done")
        score_done = sem("score_done")
        score_taken = sem("score_taken")
        max_ready = sem("max_ready")
        exp_done = sem("exp_done")
        p_ready = sem("p_ready")
        pT_done = sem("pT_done")
        pt_ready = sem("pt_ready")
        pv_done = sem("pv_done")
        ot_hi = sem("ot_hi")
        ot_ready = sem("ot_ready")
        act_done = sem("act_done")
        h32_ready = sem("h32_ready")
        h_hi = sem("h_hi")
        h_ready = sem("h_ready")
        stored = sem("stored")
        dt_sum = sem("dt_sum")
        dt_soft = sem("dt_soft")
        dt_ready = sem("dt_ready")
        dtT_done = sem("dtT_done")
        g_ready = sem("g_ready")
        sel_ready = sem("sel_ready")
        conv_evac = sem("conv_evac")
        conv_done = sem("conv_done")
        conv_silu = sem("conv_silu")
        xsT_done = sem("xsT_done")
        xs_ready = sem("xs_ready")
        z_ready = sem("z_ready")
        cb_done = sem("cb_done")
        cb_ready = sem("cb_ready")
        xdt_ready = sem("xdt_ready")
        diff_done = sem("diff_done")
        e_ready = sem("e_ready")
        m_ready = sem("m_ready")
        head_done = sem("head_done")
        y_gated = sem("y_gated")
        y_sq = sem("y_sq")
        y_std = sem("y_std")
        lam_in = sem("lam_in")
        lam_sum = sem("lam_sum")
        lam_exp = sem("lam_exp")
        rel_sum = sem("rel_sum")
        rel_row = sem("rel_row")
        rel_out = sem("rel_out")
        gate_ready = sem("gate_ready")
        u_ready = sem("u_ready")
        qk_sq = sem("qk_sq")
        qk_sum = sem("qk_sum")
        qk_std = sem("qk_std")
        qk_ready = sem("qk_ready")
        v_ready = sem("v_ready")
        sc2_done = sem("sc2_done")
        sc2_taken = sem("sc2_taken")
        mx2_ready = sem("mx2_ready")
        ex2_done = sem("ex2_done")
        mix_ready = sem("mix_ready")
        mixT_done = sem("mixT_done")
        mixT_ready = sem("mixT_ready")
        o2_done = sem("o2_done")
        o2_evac = sem("o2_evac")
        osq_sum = sem("osq_sum")
        osq_std = sem("osq_std")
        o2_norm = sem("o2_norm")
        o2_hi = sem("o2_hi")
        o2_ready = sem("o2_ready")
        pconv = sem("pconv")
        cconv = sem("cconv")
        csq = sem("csq")
        csum = sem("csum")
        cstd = sem("cstd")
        cnorm = sem("cnorm")
        c_hi = sem("c_hi")
        c_ready = sem("c_ready")

        def at(base, it, per):
            return base if it is None else base + it * per

        class Link:
            def __init__(self, eng, s):
                self.eng, self.s, self.n = eng, s, 0

            def __call__(self, ins):
                self.n += 1
                ins.then_inc(self.s, 1)
                self.eng.wait_ge(self.s, self.n)

        def cols_view(w):
            return w.rearrange("(k p) n -> p k n", p=P)

        v_att = cols_view(A["attn_w_in"][0])
        v_ssm = cols_view(A["ssm_w_in"][0])
        v_att_out = cols_view(A["attn_w_out"][0])
        v_ssm_out = cols_view(A["ssm_w_out"][0])
        v_w1 = [cols_view(A["mlp_w1"][l]) for l in range(DEPTH)]
        v_w2 = [cols_view(A["mlp_w2"][l]) for l in range(DEPTH)]
        ffn = [(cols_view(A[f"ffn{s}_w_gate_2"][l]), cols_view(A[f"ffn{s}_w_up_2"][l]),
                cols_view(A[f"ffn{s}_w_down_2"][l])) for l in range(DEPTH) for s in (1, 2)]
        v_mix = [cols_view(A["w_in_2"][l]) for l in range(DEPTH)]
        v_mix_out = [cols_view(A["w_out_2"][l]) for l in range(DEPTH)]

        n_par = [0]
        n_rows = [0]
        block = ctx.enter_context(nc.Block())

        @block.sync
        def _(sp):
            def load(u, src, it=None, per=0, width=UN):
                if u >= RING:
                    sp.wait_ge(lo_ready, at(u - RING + 1, it, per))
                dst = w_raw[:, u % RING, 0:width].rearrange("p (k n) -> p k n", k=src.shape[1])
                sp.dma_start(dst, src).then_inc(raw_ready[u % RING], 16)

            def columns(v, c):
                return v[:, :, c:c + U]

            def rows(v, g):
                return v[:, 2 * g:2 * g + 2, :]

            def mlp(u0, w1, w2):
                load(u0, columns(w1, 0))
                with sp.Fori(0, (G1 - 1) // 3) as it:
                    for j in range(3):
                        load(u0 + 1 + 2 * j, w1[:, :, bass.ds(it * (3 * U) + (1 + j) * U, U)], it, 6)
                        load(u0 + 2 + 2 * j, w2[:, bass.ds(it * 6 + 2 * j, 2), :], it, 6)
                load(u0 + 2 * G1 - 1, rows(w2, G1 - 1))

            def swiglu(u0, w):
                load(u0, columns(w[0], 0))
                load(u0 + 1, columns(w[1], 0))
                with sp.Fori(0, G2 - 1) as it:
                    load(u0 + 2, w[0][:, :, bass.ds(it * U + U, U)], it, 3)
                    load(u0 + 3, w[1][:, :, bass.ds(it * U + U, U)], it, 3)
                    load(u0 + 4, w[2][:, bass.ds(it * 2, 2), :], it, 3)
                load(u0 + 3 * G2 - 1, rows(w[2], G2 - 1))

            sp.dma_start(X[:, :, :], A["x"][0].rearrange("(t p) d -> p t d", p=P)).then_inc(x_in, 16)
            for n in range(A_UNITS):
                load(U_ATT + n, columns(v_att, n * U))
            for n in range(OUT_UNITS):
                load(U_ATT_OUT + n, rows(v_att_out, n))
            mlp(U_MLP[0], v_w1[0], v_w2[0])
            for n, c in enumerate(SSM_COLS):
                if n == DT_AT:
                    load(U_SSM + n, v_ssm[:, :, c:c + 64], width=KC * 64)
                else:
                    load(U_SSM + n, columns(v_ssm, c))
            for n in range(DI // U):
                load(U_SSM_OUT + n, rows(v_ssm_out, n))
            mlp(U_MLP[1], v_w1[1], v_w2[1])
            for l in range(DEPTH):
                swiglu(U_FFN[2 * l], ffn[2 * l])
                for n, c in enumerate(MIX_COLS):
                    load(U_MIX[l] + n, columns(v_mix[l], c))
                for n in range(OUT_UNITS):
                    load(U_MIX_OUT[l] + n, rows(v_mix_out[l], (n + 2) % 4))
                swiglu(U_FFN[2 * l + 1], ffn[2 * l + 1])
            sp.wait_ge(x_new, N_XNEW)
            sp.dma_start(out[0].rearrange("(t p) d -> p t d", p=P), X[:, :, :]).then_inc(stored, 16)
            sp.wait_ge(stored, 16)

        @block.gpsimd
        def _(pool):
            link = Link(pool, pool_link)

            def par(dst, src):
                pool.dma_start(dst, src).then_inc(par_in, 16)
                n_par[0] += 1

            def rows_of(v):
                return v.rearrange("l (c p) -> (l c) p", p=P)

            for i, n in enumerate(("ln1_g", "ln1_b", "ln2_g", "ln2_b", "ffn1_norm_2", "mix_norm_2", "ffn2_norm_2",
                                   "ssm_norm_w")):
                par(prow[16 * i:16 * i + 16, 0, :], rows_of(A[n]))
            cw = A["ssm_conv_w"][0].rearrange("k (c p) -> (k c) p", p=P)
            par(prow[:, 1, :], cw[0:128, :])
            par(prow[0:32, 2, :], cw[128:160, :])
            par(prow[32:64, 2, :], rows_of(A["ssm_conv_b"]))
            par(prow[64:72, 2, :], rows_of(A["conv_b_2"]))
            par(prow[72:80, 2, :], rows_of(A["conv_norm_2"]))
            par(prow[80:82, 2, :], A["subln_norm_2"])
            for h in range(2):
                par(prow[82:84, 2, h * HD:h * HD + HD], A["q_norm_2"])
                par(prow[84:86, 2, h * HD:h * HD + HD], A["k_norm_2"])
            for l in range(DEPTH):
                par(prow[0:CK * 4, 3 + l, :], A["conv_w_2"][l].rearrange("k (c p) -> (k c) p", p=P))

            rpb = A["attn_rpb"]
            for h in range(BH):
                for qt in range(TT):
                    for r in range(2):
                        src = bass.AP(rpb.tensor, rpb.offset + h * RPB_R * RPB_C + (NA_KH - 1 - 2 * qt - r) * RPB_C
                                      + NA_KW - 1 - (GRID_W - 1), [[1, 64], [RPB_C, 4], [1, GRID_W]])
                        pool.dma_start(na_bias[r * 64:r * 64 + 64, h, qt, :].rearrange("p (a k) -> p a k", a=4),
                                       src).then_inc(bias_in, 16)
            pool.dma_start(sink[:, 0:AQ], A["attn_sink"].broadcast_to([P, AQ])).then_inc(small_in, 16)

            lns = [("ln1", 0), ("ln2", 0), ("ln1", 1), ("ln2", 1)]

            def rows_load(i):
                n, l = lns[i]
                pool.dma_start(gain_row[:, :], A[n + "_g"][l:l + 1, :].broadcast_to([P, D])).then_inc(rows_in, 16)
                pool.dma_start(bias_row[:, :], A[n + "_b"][l:l + 1, :].broadcast_to([P, D])).then_inc(rows_in, 16)

            def settle(i, ready):
                pool.wait_ge(rows_in, 32 * (i + 1))
                pool.wait_ge(norm_ready, ready)
                for t in range(TT):
                    link(pool.tensor_tensor(X[:, t, :], xn[:, t, :], gain_row[:, :], ALU.mult))
                for t in range(TT):
                    ins = pool.tensor_tensor(X[:, t, :], X[:, t, :], bias_row[:, :], ALU.add)
                    ins.then_inc(x_settled, 1)
                pool.wait_ge(x_settled, 2 * (i + 1))

            rows_load(0)
            settle(0, 2)
            rows_load(1)
            settle(1, 4)
            rows_load(2)

            pool.wait_ge(h_ready, HG_MLP[0] + G1)
            pool.dma_start(dt_bias, A["ssm_dt_bias"].broadcast_to([P, 64])).then_inc(small_in, 16)
            pool.dma_start(d_skip, A["ssm_D"].broadcast_to([P, SH])).then_inc(small_in, 16)
            pool.dma_start(a_col[0:64, :], A["ssm_A_log"].rearrange("a d (h o) -> (a d h) o", o=1)) \
                .then_inc(small_in, 16)
            pool.wait_ge(dt_ready, 1)
            pool.wait_ge(small_in, 64)
            for g in range(SG):
                b = g % 2
                pool.wait_ge(xs_ready, g + 1)
                if g >= 2:
                    pool.wait_ge(head_done, GH * (g - 1))
                for t in range(TT):
                    xg = xs[:, t, g * U:g * U + U].rearrange("p (h e) -> p h e", h=GH)
                    for d in range(2):
                        dts = dt_tok[:, t, d * SH + g * GH:d * SH + (g + 1) * GH]
                        pool.tensor_tensor(xdt[:, b * 4 + d * 2 + t, :].rearrange("p (h e) -> p h e", h=GH), xg,
                                           dts.unsqueeze(2).broadcast_to([P, GH, HD]), ALU.mult)
                if g >= 2:
                    pool.wait_ge(y_gated, g - 1)
                for t in range(TT):
                    xg = xs[:, t, g * U:g * U + U].rearrange("p (h e) -> p h e", h=GH)
                    ds = d_skip[:, g * GH:(g + 1) * GH]
                    ins = pool.tensor_tensor(xD[b][:, t, :].rearrange("p (h e) -> p h e", h=GH), xg,
                                             ds.unsqueeze(2).broadcast_to([P, GH, HD]), ALU.mult)
                ins.then_inc(xdt_ready, 1)
            settle(2, 8)
            rows_load(3)
            settle(3, 10)

            pool.dma_start(rel[0:BUCKETS, :], A["rel_bias_2"]).then_inc(lam_in, 16)
            for i, n in enumerate(("lambda_q1_2", "lambda_q2_2")):
                pool.dma_start(lam_q[:, 2 * i:2 * i + 2, :], A[n].unsqueeze(0).broadcast_to([P, DEPTH, HD])) \
                    .then_inc(lam_in, 16)
            for i, n in enumerate(("lambda_k1_2", "lambda_k2_2")):
                pool.dma_start(lam_k[:, 2 * i:2 * i + 2, :], A[n].unsqueeze(0).broadcast_to([P, DEPTH, HD])) \
                    .then_inc(lam_in, 16)
            pool.wait_ge(rel_row, 1)
            pool.dma_start(rel_dram, rvec[0:DH, :]).then_inc(rel_out, 16)
            pool.wait_ge(rel_out, 16)
            for h in range(DH):
                for off, k0, n in ((128, 0, 128), (0, 128, 256)):
                    src = bass.AP(rel_dram.tensor, rel_dram.offset + h * 384 + off, [[1, P], [1, n]])
                    pool.dma_start(rbias[:, h, k0:k0 + n], src).then_inc(bias_in, 16)
            for l in range(DEPTH):
                pool.wait_ge(u_ready, 4 * l + 4)
                if l:
                    pool.wait_ge(cnorm, 1)
                wc = COL["conv_w"] + l * P
                c = 3
                link(pool.tensor_scalar(cacc[:, c, :], uu[:, c, 0:T], pcol[:, wc + c:wc + c + 1],
                                        pcol[:, COL["conv_b"] + 4 * l + c:COL["conv_b"] + 4 * l + c + 1],
                                        ALU.mult, ALU.add))
                for k in range(1, CK):
                    link(pool.tensor_scalar(ptmp, uu[:, c, k:k + T], pcol[:, wc + 4 * k + c:wc + 4 * k + c + 1],
                                            None, ALU.mult))
                    ins = pool.tensor_tensor(cacc[:, c, :], cacc[:, c, :], ptmp, ALU.add)
                    if k < CK - 1:
                        link(ins)
                ins.then_inc(pconv, 1)

        @block.scalar
        def _(act):
            link = Link(act, act_link)

            def split(u, it=None, per=0):
                if u >= N_UNITS:
                    return
                act.wait_ge(raw_ready[u % RING], at(16 * (u // RING + 1), it, 16 * per // RING))
                if u >= RING:
                    act.wait_ge(unit_done, at(u - RING + 1, it, per))
                act.copy(w_hi[:, u % RING, :], w_raw[:, u % RING, :]).then_inc(hi_ready, 1)

            def turn(name, gain, bias):
                n = TURNS.index(name)
                for b in range(TURN_CHUNKS[n] // 2):
                    k = TURN_BANK[n] + b
                    act.wait_ge(turned, k + 1)
                    if k >= 2:
                        act.wait_ge(xt_ready, k - 1)
                    for c in range(2):
                        j = 2 * b + c
                        ins = act.activation(turn_buf[:, k % 2, c, :], pg[:, k % 4, c * T:(c + 1) * T], ACT.Identity,
                                             scale=1.0 if gain is None else pcol[:, gain + j:gain + j + 1],
                                             bias=0.0 if bias is None else pcol[:, bias + j:bias + j + 1])
                    ins.then_inc(gained, 1)

            def ln_std(k):
                act.wait_ge(var_ready, k)
                act.activation(std[:, :], mv[:, :, 1], ACT.Sqrt, bias=lnb[:, 0:1]).then_inc(std_ready, 1)

            def rms_std(k):
                if k == 8:
                    act.wait_ge(x_settled, 8)
                else:
                    act.wait_ge(x_new, k)
                for t in range(TT):
                    ins = act.activation(xn[:, t, :], X[:, t, :], ACT.Square, accum_out=ssum[:, t:t + 1])
                link(ins)
                act.activation(std[:, :], ssum[:, :], ACT.Sqrt, bias=lnb[:, 1:2], scale=1.0 / D) \
                    .then_inc(std_ready, 1)

            def hidden(h, u_in, func, src, it=None, per_h=0, per_u=0):
                act.wait_ge(unit_done, at(u_in + 1, it, per_u))
                act.activation(act_buf[:, :], src, func).then_inc(act_done, 1)

            def hidden_hi(h, u_free, it=None, per_h=0, per_u=0):
                act.wait_ge(h32_ready, at(h + 1, it, per_h))
                if u_free is not None:
                    act.wait_ge(unit_done, at(u_free + 1, it, per_u))
                act.copy(op_hi[:, 8:10, :], h32[:, :].rearrange("p (c t) -> p c t", c=2)).then_inc(h_hi, 1)

            def mlp(u0, h0):
                split(u0 + 2)
                hidden(h0, u0, ACT.Relu, pg[:, 0, :])
                hidden_hi(h0, None)
                with act.Fori(0, (G1 - 1) // 3) as it:
                    for j in range(3):
                        u = u0 + 1 + 2 * j
                        split(u + 2, it, 6)
                        hidden(h0 + 1 + j, u, ACT.Relu, pg[:, (1 + j) % 3, :], it, 3, 6)
                        split(u + 3, it, 6)
                        hidden_hi(h0 + 1 + j, u + 1, it, 3, 6)
                split(u0 + 2 * G1 + 1)

            def swiglu(u0, h0):
                split(u0 + 2)
                hidden(h0, u0, ACT.Silu, pg[:, 0, :])
                split(u0 + 3)
                hidden_hi(h0, None)

                def group(u, h, it=None):
                    split(u + 2, it, 3)
                    hidden(h, u, ACT.Silu, pg[:, 0, :], it, 1, 3)
                    split(u + 3, it, 3)
                    split(u + 4, it, 3)
                    hidden_hi(h, u + 2, it, 1, 3)

                last = u0 + 3 * G2 == N_UNITS
                with act.Fori(0, G2 - 1 - last) as it:
                    group(u0 + 2, h0 + 1, it)
                if last:
                    group(u0 + 3 * G2 - 4, h0 + G2 - 1)
                split(u0 + 3 * G2 + 1)

            def o2_out(act, l, h):
                i = DH * l + h
                act.wait_ge(o2_done, i + 1)
                act.copy(O2[:, h, :], acc[:, h % 2, 0:T])
                act.activation(osq[:, h, :], acc[:, h % 2, 0:T], ACT.Square).then_inc(o2_evac, 1)

            act.dma_start(ident[:, :], A["consts"][:, 0:P]).then_inc(const_in, 16)
            act.dma_start(att_c, A["consts"][:, P:P + n_att]).then_inc(const_in, 16)
            split(0)
            split(1)
            turn("x", None, None)

            for n in range(A_UNITS):
                u = U_ATT + n
                split(u + 2)
                act.wait_ge(unit_done, u + 1)
                bank = pg[:, n % 4, :]
                pair = bank.rearrange("p (c t) -> p c t", c=2)
                if n < 2:
                    ins = act.copy(q_raw[:, n, :], bank)
                elif n == 2:
                    act.copy(k_raw, bank[:, 0:T])
                    ins = act.copy(va, bank[:, T:2 * T].rearrange("p (t n) -> p t n", t=TT))
                elif n < 5:
                    ins = act.copy(QT[:, 4 + 2 * (n - 3):6 + 2 * (n - 3), :], pair)
                elif n < 7:
                    ins = act.copy(KT[:, 2 + 2 * (n - 5):4 + 2 * (n - 5), :], pair)
                else:
                    ins = act.copy(vb[:, :, (n - 7) * U:(n - 6) * U], pair)
                ins.then_inc(attn_evac, 1)
            for s in range(AQ + BH + 4):
                if s < AQ + BH:
                    act.wait_ge(max_ready, s + 1)
                    for qt in range(TT):
                        act.activation(prob[:, s % 3, qt, :], prob[:, s % 3, qt, :], ACT.Exp,
                                       bias=nmx[:, s, qt:qt + 1], accum_out=psm[:, s, qt:qt + 1])
                    act.activation(pes[:, s, :], nmx[:, s, :], ACT.Exp, bias=sink[:, s:s + 1]).then_inc(exp_done, 1)
                h = s - 1
                if 0 <= h < AQ + BH:
                    act.wait_ge(pT_done, h + 1)
                    if h >= 2:
                        act.wait_ge(pv_done, h - 1)
                    act.copy(probT[:, h % 2, :, :], pg[:, 2 + h % 2, :].rearrange("p (c t) -> p c t", c=2)) \
                        .then_inc(pt_ready, 1)
                if s >= 4 and s % 2 == 0:
                    c = (s - 4) // 2
                    act.wait_ge(pv_done, 2 * c + 2)
                    act.copy(op_hi[:, 8 + c, :], acc[:, c % 4, 0:T]).then_inc(ot_hi, 1)
            for n in range(OUT_UNITS):
                split(U_ATT_OUT + n + 2)
            ln_std(1)
            turn("ln1_0", COL["ln1_g"], COL["ln1_b"])
            mlp(U_MLP[0], HG_MLP[0])
            act.wait_ge(h_ready, HG_MLP[0] + G1)
            c0 = CONST["mask_ssm"][0]
            act.dma_start(ssm_c, A["consts"][:, c0:c0 + 384]).then_inc(const_in, 16)
            ln_std(2)
            act.wait_ge(const_in, 48)
            act.copy(select[:, :], ssm_c[:, 256:320])
            act.copy(neg_tri[:, :, :], ssm_c[:, 0:256].rearrange("p (d n) -> p d n", d=2))
            act.copy(ident_r[:, :], ident[:, :])
            act.copy(nselect[:, :], ssm_c[:, 320:384]).then_inc(sel_ready, 1)
            turn("ln2_0", COL["ln2_g"], COL["ln2_b"])

            def conv_act(i):
                act.wait_ge(conv_done, i + 1)
                bias = COL["ssm_conv_b"]
                for c in range(2):
                    ch = (16 + 2 * i + c) % 32
                    if i < 8:
                        dst = (BT if i < 4 else CT)[:, 2 * (i % 4) + c, :]
                    else:
                        if i >= 10 and c == 0:
                            act.wait_ge(xsT_done, i - 9)
                        dst = xsT[:, i % 2, c, :]
                    ins = act.activation(dst, conv_sum[:, i % 2, c, :], ACT.Silu,
                                         bias=pcol[:, bias + ch:bias + ch + 1])
                ins.then_inc(conv_silu, 1)

            i = 0
            for n in range(len(SSM_COLS)):
                u = U_SSM + n
                split(u + 2)
                if n == DT_AT:
                    act.wait_ge(dt_sum, 1)
                    link(act.activation(dt_a, dt_v, ACT.Abs))
                    link(act.activation(dt_a, dt_a, ACT.Exp, scale=-1.0))
                    act.activation(dt_a, dt_a, ACT.Ln, bias=1.0).then_inc(dt_soft, 1)
                    act.activation(a_col[0:64, :], a_col[0:64, :], ACT.Exp).then_inc(dt_soft, 1)
                    continue
                act.wait_ge(unit_done, u + 1)
                pair = pg[:, n % 4, :].rearrange("p (c t) -> p c t", c=2)
                if n < len(SSM_COLS) - Z_UNITS:
                    if i >= 2:
                        act.wait_ge(conv_done, i - 1)
                    act.copy(conv_in[:, i % 2, :, 2:2 + T], pair).then_inc(conv_evac, 1)
                    if i >= 1:
                        conv_act(i - 1)
                    i += 1
                else:
                    if i == 16:
                        conv_act(15)
                        i += 1
                    z = n - (len(SSM_COLS) - Z_UNITS)
                    act.activation(silz[:, :, z * U:z * U + U], pair, ACT.Silu).then_inc(z_ready, 1)
            for h in range(SH):
                b = h % 2
                act.wait_ge(diff_done, h + 1)
                if h >= 2:
                    act.wait_ge(head_done, h - 1)
                act.activation(E[:, b, :], pg[:, 2 * b:2 * b + 2, :].rearrange("p a n -> p (a n)")[:, 0:768],
                               ACT.Exp).then_inc(e_ready, 1)
                if h % GH == 1 and h > GH:
                    g = h // GH - 1
                    act.wait_ge(y_gated, g + 1)
                    for t in range(TT):
                        ins = act.activation(turn_buf[:, 0, t, :], xs[:, t, g * U:g * U + U], ACT.Square,
                                             accum_out=ysq[:, t, g:g + 1])
                    ins.then_inc(y_sq, 1)
            act.wait_ge(y_gated, SG)
            for t in range(TT):
                ins = act.activation(turn_buf[:, 0, t, :], xs[:, t, (SG - 1) * U:SG * U], ACT.Square,
                                     accum_out=ysq[:, t, SG - 1:SG])
            link(ins)
            act.activation(yrs, ysq, ACT.Sqrt, bias=lnb[:, 0:1], scale=1.0 / U).then_inc(y_std, 1)
            turn("y", COL["ssm_norm"], None)
            for n in range(DI // U):
                split(U_SSM_OUT + n + 2)
            ln_std(3)
            turn("ln1_1", COL["ln1_g"] + 8, COL["ln1_b"] + 8)
            mlp(U_MLP[1], HG_MLP[1])
            act.wait_ge(h_ready, HG_MLP[1] + G1)
            act.dma_start(blk_c, A["consts"][:, CONST["flip"][0]:CONST_W]).then_inc(const_in, 16)
            ln_std(4)
            act.wait_ge(lam_sum, 1)
            act.activation(lam_e, lam_s, ACT.Exp).then_inc(lam_exp, 1)

            for l in range(DEPTH):
                rms_std(XN2[l][0])
                turn(f"ffn1_{l}", COL["ffn1"] + 8 * l, None)
                swiglu(U_FFN[2 * l], HG_FFN[2 * l])
                rms_std(XN2[l][1])
                turn(f"mix_{l}", COL["mix"] + 8 * l, None)
                for n in range(len(MIX_COLS)):
                    u = U_MIX[l] + n
                    split(u + 2)
                    bank = pg[:, n % 4, :]
                    pair = bank.rearrange("p (c t) -> p c t", c=2)
                    if n in (0, 2):
                        act.wait_ge(unit_done, u + 1)
                        if n == 2:
                            act.wait_ge(u_ready, 4 * l + 2)
                        act.activation(gate, pair, ACT.Sigmoid).then_inc(gate_ready, 1)
                    elif 4 <= n < 8:
                        i = 4 * l + n - 4
                        act.wait_ge(unit_done, u + 1)
                        if i >= 2:
                            act.wait_ge(qk_sum, i - 1)
                        act.activation(sq[:, i % 2, :], bank, ACT.Square).then_inc(qk_sq, 1)
                        act.wait_ge(qk_sum, i + 1)
                        if i >= 2:
                            act.wait_ge(qk_ready, i - 1)
                        act.activation(sdev[:, i % 2, :], acc[:, i % 2, :], ACT.Sqrt, bias=lnb[:, 1:2],
                                       scale=1.0 / HD).then_inc(qk_std, 1)
                    elif n >= 8:
                        act.wait_ge(unit_done, u + 1)
                        act.copy(V2[:, :, (n - 8) * U:(n - 7) * U], pair).then_inc(v_ready, 1)
                for s in range(2 * DH + 1):
                    i = 8 * l + s
                    if s < 2 * DH:
                        act.wait_ge(mx2_ready, i + 1)
                        b = s % 4
                        act.activation(prob2[:, b, 0:P], prob2[:, b, 0:P], ACT.Exp, bias=n2[:, s, 0:1],
                                       accum_out=s2[:, s, 0:1])
                        act.activation(prob2[:, b, P:384], prob2[:, b, P:384], ACT.Exp, bias=n2[:, s, 1:2],
                                       accum_out=s2[:, s, 1:2]).then_inc(ex2_done, 1)
                    if s >= 2 and s % 2 == 0:
                        h = DH * l + (s - 2) // 2
                        act.wait_ge(mixT_done, h + 1)
                        if h >= 2:
                            act.wait_ge(o2_done, h - 1)
                        act.copy(pmixT[:, h % 2, :], pg[:, 2 + h % 2, 0:384]).then_inc(mixT_ready, 1)
                    if s >= 4 and s % 2 == 0:
                        o2_out(act, l, (s - 4) // 2)
                o2_out(act, l, DH - 1)
                act.wait_ge(osq_sum, l + 1)
                act.activation(odev, acc[:, 2:4, :].rearrange("p a (b n) -> p (a b) n", b=2), ACT.Sqrt,
                               bias=lnb[:, 1:2], scale=1.0 / P).then_inc(osq_std, 1)
                act.wait_ge(o2_norm, l + 1)
                act.copy(op_hi[:, 12:16, :], O2).then_inc(o2_hi, 1)
                act.wait_ge(pconv, l + 1)
                act.wait_ge(cconv, l + 1)
                act.activation(osq, cacc, ACT.Square).then_inc(csq, 1)
                act.wait_ge(csum, l + 1)
                act.activation(odev[:, 0, :], pg[:, 0, 0:T], ACT.Sqrt, bias=lnb[:, 1:2],
                               scale=1.0 / CCH).then_inc(cstd, 1)
                act.wait_ge(cnorm, l + 1)
                for c in range(4):
                    k = COL["conv_norm"] + 4 * l + c
                    ins = act.activation(c32[:, c, :], osq[:, c, :], ACT.Silu, scale=pcol[:, k:k + 1])
                link(ins)
                act.copy(op_hi[:, 8:12, :], c32).then_inc(c_hi, 1)
                for n in range(OUT_UNITS):
                    split(U_MIX_OUT[l] + n + 2)
                rms_std(XN2[l][2])
                turn(f"ffn2_{l}", COL["ffn2"] + 8 * l, None)
                swiglu(U_FFN[2 * l + 1], HG_FFN[2 * l + 1])

        @block.vector
        def _(dve):
            link = Link(dve, dve_link)

            def split(u, it=None, per=0):
                if u >= N_UNITS:
                    return
                dve.wait_ge(hi_ready, at(u + 1, it, per))
                s = u % RING
                dve.tensor_tensor(w_lo[:, s, :], w_raw[:, s, :], w_hi[:, s, :].bitcast(F32), ALU.subtract) \
                    .then_inc(lo_ready, 1)

            def turn(name, off=0):
                n = TURNS.index(name)
                for b in range(TURN_CHUNKS[n] // 2):
                    k = TURN_BANK[n] + b
                    dve.wait_ge(gained, k + 1)
                    dst = slice(off + 2 * b, off + 2 * b + 2)
                    link(dve.tensor_copy(op_hi[:, dst, :], turn_buf[:, k % 2, :, :]))
                    dve.tensor_tensor(op_lo[:, dst, :], turn_buf[:, k % 2, :, :], op_hi[:, dst, :].bitcast(F32),
                                      ALU.subtract).then_inc(xt_ready, 1)

            def ln(u_last, k):
                dve.wait_ge(unit_done, u_last + 1)
                if k > 1:
                    dve.wait_ge(x_settled, 2 * (k - 1))
                for t in range(TT):
                    dve.scalar_tensor_tensor(out=X[:, t, :].rearrange("p (a n) -> p a n", a=2),
                                             in0=X[:, t, :].rearrange("p (a n) -> p a n", a=2), scalar=ALPHA,
                                             in1=acc[:, 2 * t:2 * t + 2, :],
                                             op0=ALU.mult, op1=ALU.add).then_inc(x_new, 1)
                for t in range(TT):
                    dve.wait_ge(x_new, 2 * (k - 1) + t + 1)
                    for a in range(2):
                        ins = dve.bn_stats(stats[:, t, a, :], X[:, t, a * 512:(a + 1) * 512])
                    link(ins)
                    ins = dve.bn_aggr(mv[:, t, :], stats[:, t, :, :].rearrange("p a n -> p (a n)"))
                ins.then_inc(var_ready, 1)
                dve.wait_ge(std_ready, k)
                link(dve.reciprocal(rstd[:, :], std[:, :]))
                for t in range(TT):
                    ins = dve.tensor_scalar(xn[:, t, :], X[:, t, :], mv[:, t, 0:1], rstd[:, t:t + 1],
                                            ALU.subtract, ALU.mult)
                    ins.then_inc(norm_ready, 1)

            def rms(k_std):
                dve.wait_ge(std_ready, k_std)
                link(dve.reciprocal(rstd[:, :], std[:, :]))
                for t in range(TT):
                    dve.tensor_scalar(xn[:, t, :], X[:, t, :], rstd[:, t:t + 1], None, ALU.mult) \
                        .then_inc(norm_ready, 1)

            def residual(u_last, factor):
                dve.wait_ge(unit_done, u_last + 1)
                for t in range(TT):
                    dve.scalar_tensor_tensor(out=X[:, t, :].rearrange("p (a n) -> p a n", a=2),
                                             in0=acc[:, 2 * t:2 * t + 2, :], scalar=factor,
                                             in1=X[:, t, :].rearrange("p (a n) -> p a n", a=2),
                                             op0=ALU.mult, op1=ALU.add).then_inc(x_new, 1)

            def hidden(h, u_in, make, it=None, per_h=0, per_u=0):
                dve.wait_ge(act_done, at(h + 1, it, per_h))
                if h:
                    dve.wait_ge(h_ready, at(h, it, per_h))
                if u_in is not None:
                    dve.wait_ge(unit_done, at(u_in + 1, it, per_u))
                make().then_inc(h32_ready, 1)

            def hidden_lo(h, it=None, per_h=0):
                dve.wait_ge(h_hi, at(h + 1, it, per_h))
                dve.tensor_tensor(op_lo[:, 8:10, :], h32[:, :].rearrange("p (c t) -> p c t", c=2),
                                  op_hi[:, 8:10, :].bitcast(F32), ALU.subtract).then_inc(h_ready, 1)

            def square():
                return dve.tensor_tensor(h32[:, :], act_buf[:, :], act_buf[:, :], ALU.mult)

            def gated():
                return dve.tensor_tensor(h32[:, :], act_buf[:, :], pg[:, 1, :], ALU.mult)

            def mlp(u0, h0):
                split(u0 + 2)
                hidden(h0, None, square)
                hidden_lo(h0)
                with dve.Fori(0, (G1 - 1) // 3) as it:
                    for j in range(3):
                        u = u0 + 1 + 2 * j
                        split(u + 2, it, 6)
                        hidden(h0 + 1 + j, None, square, it, 3, 6)
                        split(u + 3, it, 6)
                        hidden_lo(h0 + 1 + j, it, 3)
                split(u0 + 2 * G1 + 1)

            def swiglu(u0, h0):
                split(u0 + 2)
                split(u0 + 3)
                hidden(h0, u0 + 1, gated)
                hidden_lo(h0)

                def group(u, h, it=None):
                    split(u + 2, it, 3)
                    split(u + 3, it, 3)
                    hidden(h, u + 1, gated, it, 1, 3)
                    split(u + 4, it, 3)
                    hidden_lo(h, it, 1)

                last = u0 + 3 * G2 == N_UNITS
                with dve.Fori(0, G2 - 1 - last) as it:
                    group(u0 + 2, h0 + 1, it)
                if last:
                    group(u0 + 3 * G2 - 4, h0 + G2 - 1)
                split(u0 + 3 * G2 + 1)

            def xs_evac(dve, j):
                dve.wait_ge(xsT_done, j + 1)
                dve.tensor_copy(xs[:, :, j * U:j * U + U], acc[:, 2 + j % 2, :].rearrange("p (t n) -> p t n", t=TT)) \
                    .then_inc(xs_ready, 1)

            dve.memset(lnb[:, 0:1], LN_EPS)
            dve.memset(lnb[:, 1:2], EPS2)
            dve.memset(zeros[:, :], 0.0)
            dve.memset(sink[:, AQ:16], NEG).then_inc(fixed_ready, 1)
            split(0)
            split(1)
            turn("x")
            def na_bias_make(h):
                dve.wait_ge(bias_flipped, h + 1)
                dve.tensor_tensor(na_bias[:, h, :, :].rearrange("p a n -> p (a n)"), acc[:, h % 2, :],
                                  att_const("mask_na"), ALU.add).then_inc(bias_ready, 1)

            def rope_sum(dst, plain, turned_ps, width):
                c = width // T
                cos = att_const("cos").unsqueeze(1).broadcast_to([P, c, T])
                sin = att_const("sin").unsqueeze(1).broadcast_to([P, c, T])
                a, b = r_tmp[:, 0, 0:width], r_tmp[:, 1, 0:width]
                v = lambda z: z.rearrange("p (c t) -> p c t", c=c)
                dve.tensor_tensor(v(a), v(turned_ps), sin, ALU.mult)
                link(dve.tensor_tensor(v(b), v(plain), cos, ALU.mult))
                return dve.tensor_tensor(dst, v(a), v(b), ALU.add)

            dve.wait_ge(const_in, 32)
            for n in range(A_UNITS):
                split(U_ATT + n + 2)
                if 5 <= n < 9:
                    na_bias_make(2 * n - 10)
                    na_bias_make(2 * n - 9)
                if n in (1, 2):
                    i = n - 1
                    dve.wait_ge(rot_done, i + 1)
                    link(rope_sum(QT[:, 2 * i:2 * i + 2, :], q_raw[:, i, :], acc[:, i, :], 2 * T))
                if n == 3:
                    dve.wait_ge(rot_done, 3)
                    for j in range(AKV):
                        ins = rope_sum(KT[:, j:j + 1, :], acc[:, 2 + j, 0:T], acc[:, 2 + j, T:2 * T], T)
                        if j == 0:
                            link(ins)
                    ins.then_inc(rope_done, 1)
            for b in range(5):
                dve.wait_ge(par_turned, b + 1)
                dve.tensor_copy(pcol[:, b * P:b * P + ROW_BLOCKS[b]], acc[:, b % 4, 0:ROW_BLOCKS[b]]) \
                    .then_inc(par_ready, 1)
            dve.wait_ge(small_in, 16)
            dve.wait_ge(bias_ready, BH)
            dve.wait_ge(fixed_ready, 1)
            for s in range(AQ + BH + 4):
                h = s
                if h < AQ + BH:
                    dve.wait_ge(score_done, h + 1)
                    if h >= 3:
                        dve.wait_ge(pT_done, h - 2)
                    p = prob[:, h % 3, :, :]
                    mask = att_const("mask_a") if h < AQ else na_bias[:, h - AQ, :, :].rearrange("p a n -> p (a n)")
                    dve.scalar_tensor_tensor(out=p.rearrange("p a n -> p (a n)"), in0=pg[:, h % 2, :], scalar=SCALE,
                                             in1=mask, op0=ALU.mult, op1=ALU.add).then_inc(score_taken, 1)
                    dve.wait_ge(score_taken, h + 1)
                    link(dve.tensor_reduce(mx[:, h, :], p, AX.X, ALU.max))
                    dve.tensor_scalar(nmx[:, h, :], mx[:, h, :], sink[:, h:h + 1], -1.0, ALU.max, ALU.mult) \
                        .then_inc(max_ready, 1)
                h = s - 1
                if 0 <= h < AQ + BH:
                    dve.wait_ge(exp_done, h + 1)
                    link(dve.tensor_tensor(pden[:, h, :], psm[:, h, :], pes[:, h, :], ALU.add))
                    link(dve.reciprocal(pden[:, h, :], pden[:, h, :]))
                    for qt in range(TT):
                        ins = dve.tensor_scalar(prob[:, h % 3, qt, :], prob[:, h % 3, qt, :], pden[:, h, qt:qt + 1],
                                                None, ALU.mult)
                    ins.then_inc(p_ready, 1)
                if s >= 4 and s % 2 == 0:
                    c = (s - 4) // 2
                    dve.wait_ge(ot_hi, c + 1)
                    dve.tensor_tensor(op_lo[:, 8 + c, :], acc[:, c % 4, 0:T], op_hi[:, 8 + c, :].bitcast(F32),
                                      ALU.subtract).then_inc(ot_ready, 1)
            for n in range(OUT_UNITS):
                split(U_ATT_OUT + n + 2)
            ln(U_MLP[0] - 1, 1)
            turn("ln1_0")
            mlp(U_MLP[0], HG_MLP[0])
            ln(U_SSM - 1, 2)
            turn("ln2_0")

            dve.memset(one_col, 1.0)
            dve.memset(conv_in[:, :, :, 0:2], 0.0)
            link(dve.memset(conv_in[:, :, :, 2 + T:], 0.0))
            i = 0
            for n in range(len(SSM_COLS)):
                split(U_SSM + n + 2)
                if n == DT_AT:
                    dve.wait_ge(unit_done, U_SSM + n + 1)
                    dve.wait_ge(small_in, 64)
                    dve.tensor_tensor(dt_v, pg[:, n % 4, 0:128].rearrange("p (t n) -> p t n", t=TT),
                                      dt_bias.unsqueeze(1).broadcast_to([P, TT, 64]), ALU.add).then_inc(dt_sum, 1)
                    dve.wait_ge(dt_soft, 2)
                    dve.scalar_tensor_tensor(out=dt_tok, in0=dt_v, scalar=0.0, in1=dt_a, op0=ALU.max,
                                             op1=ALU.add).then_inc(dt_ready, 1)
                    continue
                if n == DT_AT + 2:
                    dve.wait_ge(dtT_done, 1)
                    link(dve.tensor_scalar(aT[0:64, :], acc[0:64, 0, 0:T], a_col[0:64, :], -1.0, ALU.mult, ALU.mult))
                    link(dve.tensor_tensor_scan(gT[0:64, :], one_col[0:64, :].broadcast_to([64, T]), aT[0:64, :], 0.0, ALU.mult, ALU.add))
                    link(dve.tensor_tensor(gT[32:64, :], aT[32:64, :], gT[32:64, :], ALU.subtract))
                    link(dve.tensor_copy(g_pair[0:64, :], gT[0:64, :]))
                    link(dve.tensor_tensor(gT[0:64, :], gT[0:64, :], g_pair[0:64, :].bitcast(F32), ALU.subtract))
                    dve.tensor_copy(g_pair[64:128, :], gT[0:64, :]).then_inc(g_ready, 1)
                if n < len(SSM_COLS) - Z_UNITS:
                    dve.wait_ge(conv_evac, i + 1)
                    if i >= 2:
                        dve.wait_ge(conv_silu, i - 1)
                    for k in range(CONV):
                        for c in range(2):
                            wc = COL["ssm_conv_w"] + 32 * k + (16 + 2 * i + c) % 32
                            src = conv_in[:, i % 2, c, k:k + T]
                            dst = conv_sum[:, i % 2, c, :]
                            if k == 0:
                                ins = dve.tensor_scalar(dst, src, pcol[:, wc:wc + 1], None, ALU.mult)
                            else:
                                ins = dve.scalar_tensor_tensor(out=dst, in0=src, scalar=pcol[:, wc:wc + 1], in1=dst,
                                                               op0=ALU.mult, op1=ALU.add)
                        if k < CONV - 1:
                            link(ins)
                    ins.then_inc(conv_done, 1)
                    i += 1
                    if i >= 11:
                        xs_evac(dve, i - 11)
                elif i == 16:
                    xs_evac(dve, 6)
                    xs_evac(dve, 7)
                    i += 1
            dve.wait_ge(const_in, 48)

            def cb_make(g):
                dve.wait_ge(cb_done, g + 1)
                src = acc[:, 2 + g % 2, :]
                for a, z, o in ((0, 256, 0), (384, 512, 256), (0, 128, 384), (256, 512, 512)):
                    ins = dve.tensor_copy(CB[:, g % 2, o:o + z - a], src[:, a:z])
                ins.then_inc(cb_ready, 1)
                dve.wait_ge(cb_ready, g + 1)

            def y_make(g):
                dve.wait_ge(head_done, GH * (g + 1))
                dve.wait_ge(xdt_ready, g + 1)
                yg = xs[:, :, g * U:g * U + U]
                link(dve.tensor_tensor(yg, acc[:, g % 2, :].rearrange("p (t n) -> p t n", t=TT), xD[g % 2],
                                       ALU.add))
                dve.wait_ge(z_ready, Z_UNITS)
                dve.tensor_tensor(yg, yg, silz[:, :, g * U:g * U + U], ALU.mult).then_inc(y_gated, 1)

            for h in range(SH):
                g, b = h // GH, h % 2
                if h % GH == 0:
                    cb_make(g)
                dve.wait_ge(e_ready, h + 1)
                dve.tensor_tensor(E[:, b, :], E[:, b, :], CB[:, g % 2, :], ALU.mult).then_inc(m_ready, 1)
                if h % GH == 0 and g:
                    y_make(g - 1)
            y_make(SG - 1)
            dve.wait_ge(y_std, 1)
            link(dve.reciprocal(yrs, yrs))
            for t in range(TT):
                for g in range(SG):
                    ins = dve.tensor_scalar(xs[:, t, g * U:g * U + U], xs[:, t, g * U:g * U + U],
                                            yrs[:, t, g:g + 1], None, ALU.mult)
                ins.then_inc(norm_ready, 1)
            turn("y")
            for n in range(DI // U):
                split(U_SSM_OUT + n + 2)
            ln(U_MLP[1] - 1, 3)
            turn("ln1_1")
            mlp(U_MLP[1], HG_MLP[1])
            ln(U_SECOND - 1, 4)

            dve.wait_ge(lam_in, 80)
            dve.wait_ge(const_in, 64)
            link(dve.tensor_tensor(lam_q, lam_q, lam_k, ALU.mult))
            dve.tensor_reduce(lam_s, lam_q, AX.X, ALU.add).then_inc(lam_sum, 1)
            dve.wait_ge(rel_sum, 1)
            dve.tensor_copy(rvec[0:DH, :], acc[0:DH, 0, 0:384]).then_inc(rel_row, 1)
            dve.memset(ones_m, 1.0)
            dve.memset(uu[:, :, 0:CK - 1], 0.0)
            dve.wait_ge(lam_exp, 1)
            for l in range(DEPTH):
                link(dve.tensor_tensor(nlam[:, l:l + 1], lam_e[:, 2 + l:3 + l], lam_e[:, l:l + 1], ALU.subtract))
                link(dve.tensor_scalar(nlam[:, l:l + 1], nlam[:, l:l + 1], -lambda_init(l), None, ALU.add))
                link(dve.tensor_scalar(sub_g[:, l:l + 1], pcol[:, COL["subln"] + l:COL["subln"] + l + 1],
                                       1.0 - lambda_init(l), None, ALU.mult))
            for h in range(DH):
                dve.wait_ge(bias_flipped, BH + h + 1)
                ins = dve.tensor_tensor(rbias[:, h, :], acc[:, h, 0:384], blk_const("causal"), ALU.add)
                ins.then_inc(bias_ready, 1)
            dve.wait_ge(bias_ready, BH + DH)
            dve.wait_ge(x_settled, 8)

            for l in range(DEPTH):
                rms(STD2[l][0])
                turn(f"ffn1_{l}")
                swiglu(U_FFN[2 * l], HG_FFN[2 * l])
                residual(U_MIX[l] - 1, 0.5)
                rms(STD2[l][1])
                turn(f"mix_{l}")
                for n in range(len(MIX_COLS)):
                    u = U_MIX[l] + n
                    split(u + 2)
                    bank = pg[:, n % 4, :]
                    pair = bank.rearrange("p (c t) -> p c t", c=2)
                    if n in (1, 3):
                        dve.wait_ge(unit_done, u + 1)
                        dve.wait_ge(gate_ready, 2 * l + (n + 1) // 2)
                        if l and n == 1:
                            dve.wait_ge(pconv, l)
                        dve.tensor_tensor(uu[:, n - 1:n + 1, CK - 1:], pair, gate, ALU.mult).then_inc(u_ready, 2)
                    elif 4 <= n < 8:
                        i = 4 * l + n - 4
                        dve.wait_ge(qk_std, i + 1)
                        link(dve.reciprocal(sdev[:, i % 2, :], sdev[:, i % 2, :]))
                        gc = (COL["q_norm"] if n < 6 else COL["k_norm"]) + l
                        c = 2 * (n % 2)
                        dst = (Q2 if n < 6 else K2)[:, c:c + 2, :]
                        dve.scalar_tensor_tensor(out=dst, in0=pair, scalar=pcol[:, gc:gc + 1],
                                                 in1=sdev[:, i % 2, :].rearrange("p (c t) -> p c t", c=2),
                                                 op0=ALU.mult, op1=ALU.mult).then_inc(qk_ready, 1)
                for s in range(2 * DH + 1):
                    i = 8 * l + s
                    if s < 2 * DH:
                        h = s // 2
                        dve.wait_ge(sc2_done, i + 1)
                        b = s % 4
                        dve.scalar_tensor_tensor(out=prob2[:, b, :], in0=pg[:, s % 2, 0:384], scalar=SCALE,
                                                 in1=rbias[:, h, :], op0=ALU.mult, op1=ALU.add) \
                            .then_inc(sc2_taken, 1)
                        dve.wait_ge(sc2_taken, i + 1)
                        dve.tensor_reduce(m2[:, s, 0:1], prob2[:, b, 0:P], AX.X, ALU.max)
                        link(dve.tensor_reduce(m2[:, s, 1:2], prob2[:, b, P:384], AX.X, ALU.max))
                        dve.tensor_scalar(n2[:, s, :], m2[:, s, :], -1.0, None, ALU.mult).then_inc(mx2_ready, 1)
                    if s >= 2 and s % 2 == 0:
                        h = (s - 2) // 2
                        k = DH * l + h
                        dve.wait_ge(ex2_done, 8 * l + 2 * h + 2)
                        link(dve.reciprocal(r2[:, 2 * h:2 * h + 2, :], s2[:, 2 * h:2 * h + 2, :]))
                        link(dve.tensor_scalar(r2[:, 2 * h + 1, :], r2[:, 2 * h + 1, :], nlam[:, l:l + 1], None,
                                               ALU.mult))
                        if k >= 2:
                            dve.wait_ge(mixT_done, k - 1)
                        b0, b1 = (2 * h) % 4, (2 * h + 1) % 4
                        for a, z, qt in ((0, P, 0), (P, 384, 1)):
                            ins = dve.tensor_scalar(pmix[:, k % 2, a:z], prob2[:, b0, a:z],
                                                    r2[:, 2 * h, qt:qt + 1], None, ALU.mult)
                        link(ins)
                        for a, z, qt in ((0, P, 0), (P, 384, 1)):
                            ins = dve.scalar_tensor_tensor(out=pmix[:, k % 2, a:z], in0=prob2[:, b1, a:z],
                                                           scalar=r2[:, 2 * h + 1, qt:qt + 1],
                                                           in1=pmix[:, k % 2, a:z], op0=ALU.mult, op1=ALU.add)
                        ins.then_inc(mix_ready, 1)
                dve.wait_ge(osq_std, l + 1)
                link(dve.reciprocal(odev, odev))
                flat = lambda z: z.rearrange("p a n -> p (a n)")
                dve.scalar_tensor_tensor(out=flat(O2), in0=flat(O2), scalar=sub_g[:, l:l + 1], in1=flat(odev),
                                         op0=ALU.mult, op1=ALU.mult).then_inc(o2_norm, 1)
                dve.wait_ge(o2_hi, l + 1)
                dve.tensor_tensor(op_lo[:, 12:16, :], O2, op_hi[:, 12:16, :].bitcast(F32), ALU.subtract) \
                    .then_inc(o2_ready, 1)
                wc = COL["conv_w"] + l * P
                for k in range(CK):
                    for c in range(3):
                        w = pcol[:, wc + 4 * k + c:wc + 4 * k + c + 1]
                        if k == 0:
                            bc = COL["conv_b"] + 4 * l + c
                            ins = dve.tensor_scalar(cacc[:, c, :], uu[:, c, 0:T], w, pcol[:, bc:bc + 1],
                                                    ALU.mult, ALU.add)
                        else:
                            ins = dve.scalar_tensor_tensor(out=cacc[:, c, :], in0=uu[:, c, k:k + T], scalar=w,
                                                           in1=cacc[:, c, :], op0=ALU.mult, op1=ALU.add)
                    if k < CK - 1:
                        link(ins)
                ins.then_inc(cconv, 1)
                dve.wait_ge(cstd, l + 1)
                link(dve.reciprocal(odev[:, 0, :], odev[:, 0, :]))
                dve.tensor_tensor(osq, cacc, odev[:, 0:1, :].broadcast_to([P, 4, T]), ALU.mult).then_inc(cnorm, 1)
                dve.wait_ge(c_hi, l + 1)
                dve.tensor_tensor(op_lo[:, 8:12, :], c32, op_hi[:, 8:12, :].bitcast(F32), ALU.subtract) \
                    .then_inc(c_ready, 1)
                for n in range(OUT_UNITS):
                    split(U_MIX_OUT[l] + n + 2)
                residual(U_FFN[2 * l + 1] - 1, 1.0)
                rms(STD2[l][2])
                turn(f"ffn2_{l}")
                swiglu(U_FFN[2 * l + 1], HG_FFN[2 * l + 1])
                residual((U_FFN + [N_UNITS])[2 * l + 2] - 1, 0.5)

        @block.tensor
        def _(pe):
            def take(u, it=None, per=0):
                pe.wait_ge(lo_ready, at(u + 1, it, per))

            def three(psum, w, x, first, last, swap=False):
                terms = ((0, 0), (1, 0), (0, 1))
                for i, (a, b) in enumerate(terms):
                    l, r = (x[b], w[a]) if swap else (w[a], x[b])
                    ins = pe.matmul(psum, l, r, start=first and i == 0, stop=last and i == 2)
                return ins

            def wslice(u, a, z):
                s = u % RING
                return w_hi[:, s, a:z], w_lo[:, s, a:z]

            def feature_chunk(u, bank, c, step=U):
                for k in range(KC):
                    o = k * step + c * P
                    ins = three(bank, wslice(u, o, o + P), (op_hi[:, k, :], op_lo[:, k, :]), k == 0, k == KC - 1)
                return ins

            def token_tile(u, bank, t, c0, width, step=U):
                for k in range(KC):
                    o = k * step + c0
                    ts = slice(t * P, t * P + P)
                    ins = three(bank, wslice(u, o, o + width), (op_hi[:, k, ts], op_lo[:, k, ts]), k == 0,
                                k == KC - 1, swap=True)
                return ins

            def project(u, bank, tokens=False, it=None, per=0):
                take(u, it, per)
                for c in range(2):
                    o = bank[:, c * T:(c + 1) * T]
                    ins = token_tile(u, o, c, 0, U) if tokens else feature_chunk(u, o, c)
                ins.then_inc(unit_done, 1)

            def output(u, chunk, first, last, it=None, per=0):
                take(u, it, per)
                for k in range(2):
                    for t in range(TT):
                        ts = slice(t * P, t * P + P)
                        for h in range(2):
                            o = k * D + h * 512
                            ins = three(acc[:, 2 * t + h, :], wslice(u, o, o + 512),
                                        (op_hi[:, chunk + k, ts], op_lo[:, chunk + k, ts]),
                                        first and k == 0, last and k == 1, swap=True)
                ins.then_inc(unit_done, 1)

            def turn(name, src, ready):
                n = TURNS.index(name)
                if ready:
                    pe.wait_ge(norm_ready, ready)
                for b in range(TURN_CHUNKS[n] // 2):
                    k = TURN_BANK[n] + b
                    if k >= 4:
                        pe.wait_ge(gained, k - 3)
                    for c in range(2):
                        for t in range(TT):
                            j = (2 * b + c) * P
                            ins = pe.transpose(pg[:, k % 4, c * T + t * P:c * T + t * P + P], src[:, t, j:j + P],
                                               ident[:, :])
                    ins.then_inc(turned, 1)

            def turned_in(name):
                pe.wait_ge(xt_ready, TURN_BANK[TURNS.index(name) + 1])

            def mlp(u0, h0):
                project(u0, pg[:, 0, :])
                with pe.Fori(0, (G1 - 1) // 3) as it:
                    for j in range(3):
                        project(u0 + 1 + 2 * j, pg[:, (1 + j) % 3, :], False, it, 6)
                        pe.wait_ge(h_ready, at(h0 + j + 1, it, 3))
                        output(u0 + 2 + 2 * j, 8, False, False, it, 6)
                pe.wait_ge(h_ready, h0 + G1)
                output(u0 + 2 * G1 - 1, 8, False, True)

            def swiglu(u0, h0):
                project(u0, pg[:, 0, :])
                project(u0 + 1, pg[:, 1, :])
                with pe.Fori(0, G2 - 1) as it:
                    pe.wait_ge(act_done, at(h0 + 1, it, 1))
                    project(u0 + 2, pg[:, 0, :], False, it, 3)
                    pe.wait_ge(h32_ready, at(h0 + 1, it, 1))
                    project(u0 + 3, pg[:, 1, :], False, it, 3)
                    pe.wait_ge(h_ready, at(h0 + 1, it, 1))
                    output(u0 + 4, 8, False, False, it, 3)
                pe.wait_ge(h_ready, h0 + G2)
                output(u0 + 3 * G2 - 1, 8, False, True)

            def clear_sums():
                for b in range(4):
                    pe.matmul(acc[:, b, :], zeros[:, 0:P], zeros[:, :], start=True, stop=False)

            def qk_sums(pe, i):
                pe.wait_ge(qk_sq, i + 1)
                if i >= 2:
                    pe.wait_ge(qk_std, i - 1)
                pe.matmul(acc[:, i % 2, :], blk_const("halves"), sq[:, i % 2, :], start=True, stop=True) \
                    .then_inc(qk_sum, 1)

            def o2(pe, l, h):
                k = DH * l + h
                pe.wait_ge(mixT_ready, k + 1)
                if k >= 2:
                    pe.wait_ge(o2_evac, k - 1)
                pe.matmul(acc[:, h % 2, 0:T], V2[:, 0, h * P:h * P + P], pmixT[:, k % 2, 0:T], start=True, stop=False)
                pe.matmul(acc[:, h % 2, P:T], V2[:, 1, h * P:h * P + P], pmixT[:, k % 2, T:384], start=False,
                          stop=True).then_inc(o2_done, 1)

            pe.wait_ge(x_in, 16)
            pe.wait_ge(const_in, 32)
            turn("x", X, 0)
            turned_in("x")
            for n in range(A_UNITS):
                u = U_ATT + n
                if n >= 4:
                    pe.wait_ge(attn_evac, n - 3)
                bank = pg[:, n % 4, :]
                if n == 2:
                    take(u)
                    feature_chunk(u, bank[:, 0:T], 0)
                    for t in range(TT):
                        ins = token_tile(u, bank[:, T + t * P:T + t * P + P], t, P, P)
                    ins.then_inc(unit_done, 1)
                else:
                    project(u, bank, tokens=n >= 7)
                if n in (1, 2):
                    i = n - 1
                    pe.wait_ge(attn_evac, i + 1)
                    pe.matmul(acc[:, i, :], att_const("rot"), q_raw[:, i, :], start=True, stop=True) \
                        .then_inc(rot_done, 1)
                if 4 <= n < 8:
                    if n == 4:
                        pe.wait_ge(bias_in, 16 * BH * 4)
                        pe.wait_ge(rope_done, 1)
                    for h in (2 * n - 8, 2 * n - 7):
                        if h >= 2:
                            pe.wait_ge(bias_ready, h - 1)
                        pe.matmul(acc[:, h % 2, :], att_const("na_flip"),
                                  na_bias[:, h, :, :].rearrange("p a n -> p (a n)"), start=True, stop=True) \
                            .then_inc(bias_flipped, 1)
                if n == 8:
                    pe.wait_ge(par_in, 16 * N_PAR)
                    pe.wait_ge(bias_ready, BH)
                    for b in range(5):
                        r = ROW_BLOCKS[b]
                        if b >= 4:
                            pe.wait_ge(par_ready, b - 3)
                        pe.transpose(acc[:, b % 4, 0:r], prow[0:r, b, :], ident[0:r, 0:r]).then_inc(par_turned, 1)
                if n == 3:
                    pe.wait_ge(attn_evac, 3)
                    for j in range(AKV):
                        pe.matmul(acc[:, 2 + j, 0:T], att_const(f"dup{j}"), k_raw, start=True, stop=True)
                        ins = pe.matmul(acc[:, 2 + j, T:2 * T], att_const(f"rdup{j}"), k_raw, start=True, stop=True)
                    ins.then_inc(rot_done, 1)
            pe.wait_ge(par_ready, 5)
            pe.wait_ge(attn_evac, A_UNITS)
            for s in range(AQ + BH + 2):
                h = s
                if h < AQ + BH:
                    if h >= 2:
                        pe.wait_ge(score_taken, h - 1)
                    p0 = (h % 2) * HD
                    ki = h // 4 if h < AQ else 2 + (h - AQ) // 2
                    for qt in range(TT):
                        ins = pe.matmul(pg[:, h % 2, qt * T:(qt + 1) * T],
                                        QT[p0:p0 + HD, h // 2, qt * P:qt * P + P], KT[p0:p0 + HD, ki, :],
                                        start=True, stop=True)
                    ins.then_inc(score_done, 1)
                h = s - 1
                if 0 <= h < AQ + BH:
                    pe.wait_ge(p_ready, h + 1)
                    if h >= 2:
                        pe.wait_ge(pt_ready, h - 1)
                    for kt in range(TT):
                        for qt in range(TT):
                            ins = pe.transpose(pg[:, 2 + h % 2, kt * T + qt * P:kt * T + qt * P + P],
                                               prob[:, h % 3, qt, kt * P:kt * P + P], ident[:, :])
                    ins.then_inc(pT_done, 1)
                h = s - 2
                if 0 <= h < AQ + BH:
                    pe.wait_ge(pt_ready, h + 1)
                    c = h // 2
                    if c >= 4 and h % 2 == 0:
                        pe.wait_ge(ot_ready, c - 3)
                    p0 = (h % 2) * HD
                    for kt in range(TT):
                        v = va[:, kt, (h // 4) * HD:(h // 4 + 1) * HD] if h < AQ \
                            else vb[:, kt, (h - AQ) * HD:(h - AQ + 1) * HD]
                        ins = pe.matmul(acc[p0:p0 + HD, c % 4, 0:T], v, probT[:, h % 2, kt, :], start=kt == 0,
                                        stop=kt == TT - 1)
                    ins.then_inc(pv_done, 1)
            pe.wait_ge(ot_ready, 8)
            for n in range(OUT_UNITS):
                output(U_ATT_OUT + n, 8 + 2 * n, n == 0, n == OUT_UNITS - 1)
            turn("ln1_0", xn, 2)
            turned_in("ln1_0")
            clear_sums()
            mlp(U_MLP[0], HG_MLP[0])
            turn("ln2_0", xn, 4)
            turned_in("ln2_0")

            i = 0
            for n in range(len(SSM_COLS)):
                u = U_SSM + n
                bank = pg[:, n % 4, :]
                if n >= 4:
                    m = n - 4
                    if m < DT_AT:
                        pe.wait_ge(conv_evac, m + 1)
                    elif m == DT_AT:
                        pe.wait_ge(dt_sum, 1)
                    elif m < 17:
                        pe.wait_ge(conv_evac, m)
                    else:
                        pe.wait_ge(z_ready, m - 16)
                if n == DT_AT:
                    take(u)
                    for t in range(TT):
                        ins = token_tile(u, bank[:, t * 64:t * 64 + 64], t, 0, 64, step=64)
                    ins.then_inc(unit_done, 1)
                    continue
                project(u, bank, tokens=n >= 17)
                if n == DT_AT + 1:
                    pe.wait_ge(dt_ready, 1)
                    for t in range(TT):
                        ins = pe.transpose(acc[0:64, 0, t * P:t * P + P], dt_tok[:, t, :], ident[:, :])
                    ins.then_inc(dtT_done, 1)
                if n >= 11 and n < 19:
                    j = n - 11
                    pe.wait_ge(conv_silu, j + 9)
                    if j >= 2:
                        pe.wait_ge(xs_ready, j - 1)
                    for t in range(TT):
                        for c in range(2):
                            ins = pe.transpose(acc[:, 2 + j % 2, t * U + c * P:t * U + c * P + P],
                                               xsT[:, j % 2, c, t * P:t * P + P], ident[:, :])
                    ins.then_inc(xsT_done, 1)

            def cb(g):
                if g >= 2:
                    pe.wait_ge(cb_ready, g - 1)
                for st in range(TT):
                    ins = pe.matmul(acc[:, 2 + g % 2, st * T:(st + 1) * T], BT[:, g, st * P:st * P + P], CT[:, g, :],
                                    start=True, stop=True)
                ins.then_inc(cb_done, 1)

            def diff(h):
                b = h % 2
                if h >= 2:
                    pe.wait_ge(e_ready, h - 1)
                o = pg[:, 2 * b:2 * b + 2, :].rearrange("p a n -> p (a n)")
                for at_, w, r, st, l0, d0 in ((0, 256, h, 0, 0, 0), (256, 128, h, 1, 128, 256),
                                              (384, 128, SH + h, 0, 0, 384), (512, 256, SH + h, 1, 0, 640)):
                    pe.matmul(o[:, at_:at_ + w], select[:, r:r + 1].broadcast_to([P, P]), g_pair[:, l0:l0 + w],
                              start=True, stop=False)
                    pe.matmul(o[:, at_:at_ + w], g_pair[:, st * P:st * P + P],
                                    nselect[:, r:r + 1].broadcast_to([P, w]), start=False, stop=False)
                    ins = pe.matmul(o[:, d0:d0 + P], ident_r[:, :], neg_tri[:, r // SH, :], start=False, stop=True)
                ins.then_inc(diff_done, 1)

            def y(h):
                g, b = h // GH, h % 2
                e0 = (h % GH) * HD
                pe.wait_ge(m_ready, h + 1)
                if h % GH == 0:
                    pe.wait_ge(xdt_ready, g + 1)
                    if g >= 2:
                        pe.wait_ge(y_gated, g - 1)
                x4 = lambda d, t: xdt[:, (g % 2) * 4 + d * 2 + t, e0:e0 + HD]
                terms = [[(0, 0, 0), (384, 1, 0), (512, 1, 1)], [(128, 0, 0), (256, 0, 1), (640, 1, 1)]]
                for lt in range(TT):
                    for i_, (o, d, st) in enumerate(terms[lt]):
                        ins = pe.matmul(acc[:, g % 2, lt * U + e0:lt * U + e0 + HD], E[:, b, o:o + P], x4(d, st),
                                        start=i_ == 0, stop=i_ == 2)
                ins.then_inc(head_done, 1)

            pe.wait_ge(z_ready, Z_UNITS)
            pe.wait_ge(xs_ready, 8)
            pe.wait_ge(g_ready, 1)
            pe.wait_ge(sel_ready, 1)
            cb(0)
            diff(0)
            for h in range(SH):
                if h + 1 < SH:
                    if (h + 1) % GH == 0:
                        cb((h + 1) // GH)
                    diff(h + 1)
                y(h)
            turn("y", xs, 6)
            turned_in("y")
            for n in range(DI // U):
                output(U_SSM_OUT + n, 2 * n, n == 0, n == DI // U - 1)
            turn("ln1_1", xn, 8)
            turned_in("ln1_1")
            clear_sums()
            mlp(U_MLP[1], HG_MLP[1])

            pe.wait_ge(var_ready, 4)
            pe.wait_ge(lam_in, 80)
            pe.wait_ge(const_in, 64)
            pe.matmul(acc[0:DH, 0, 0:384], rel[0:BUCKETS, :], blk_const("buckets")[0:BUCKETS, :], start=True,
                      stop=True).then_inc(rel_sum, 1)
            pe.wait_ge(bias_in, 16 * (BH * 4 + DH * 2))
            pe.wait_ge(rel_row, 1)
            for h in range(DH):
                pe.matmul(acc[:, h, 0:384], blk_const("flip"), rbias[:, h, :], start=True, stop=True) \
                    .then_inc(bias_flipped, 1)
            for l in range(DEPTH):
                turn(f"ffn1_{l}", xn, 10 + 6 * l + 2)
                turned_in(f"ffn1_{l}")
                pe.wait_ge(bias_ready, BH + DH)
                clear_sums()
                swiglu(U_FFN[2 * l], HG_FFN[2 * l])
                turn(f"mix_{l}", xn, 10 + 6 * l + 4)
                turned_in(f"mix_{l}")
                for n in range(len(MIX_COLS)):
                    u = U_MIX[l] + n
                    m = n - 4
                    if m in (0, 1):
                        pe.wait_ge(u_ready, 4 * l + 2)
                    elif m in (2, 3):
                        pe.wait_ge(u_ready, 4 * l + 4)
                    elif m >= 4:
                        pe.wait_ge(qk_ready, 4 * l + m - 3)
                    project(u, pg[:, n % 4, :], tokens=n >= 8)
                    if 5 <= n < 9:
                        qk_sums(pe, 4 * l + n - 5)
                pe.wait_ge(qk_ready, 4 * l + 4)
                pe.wait_ge(v_ready, 2 * l + 2)
                for s in range(2 * DH + 2):
                    i = 8 * l + s
                    if s < 2 * DH:
                        h, m = s // 2, s % 2
                        if s >= 2:
                            pe.wait_ge(sc2_taken, i - 1)
                        p0 = m * HD
                        pe.matmul(pg[:, s % 2, 0:P], Q2[p0:p0 + HD, h, 0:P], K2[p0:p0 + HD, h, 0:P], start=True,
                                  stop=True)
                        pe.matmul(pg[:, s % 2, P:384], Q2[p0:p0 + HD, h, P:T], K2[p0:p0 + HD, h, :], start=True,
                                  stop=True).then_inc(sc2_done, 1)
                    if s >= 2 and s % 2 == 0:
                        k = DH * l + (s - 2) // 2
                        pe.wait_ge(mix_ready, k + 1)
                        if k >= 2:
                            pe.wait_ge(mixT_ready, k - 1)
                        for o, a in ((0, 0), (P, P), (2 * P, 2 * P)):
                            ins = pe.transpose(pg[:, 2 + k % 2, o:o + P], pmix[:, k % 2, a:a + P], ident[:, :])
                        ins.then_inc(mixT_done, 1)
                    if s >= 3 and s % 2 == 1:
                        o2(pe, l, (s - 3) // 2)
                pe.wait_ge(o2_evac, DH * l + DH)
                for a in range(2):
                    ins = pe.matmul(acc[:, 2 + a, :], ones_m, osq[:, 2 * a:2 * a + 2, :].rearrange("p a n -> p (a n)"),
                                    start=True, stop=True)
                ins.then_inc(osq_sum, 1)
                pe.wait_ge(o2_ready, l + 1)
                for n in range(OUT_UNITS):
                    if n == 2:
                        pe.wait_ge(csq, l + 1)
                        for c in range(4):
                            ins = pe.matmul(pg[:, 0, 0:T], ones_m, osq[:, c, :], start=c == 0, stop=c == 3)
                        ins.then_inc(csum, 1)
                        pe.wait_ge(c_ready, l + 1)
                    output(U_MIX_OUT[l] + n, 8 + 2 * ((n + 2) % 4), n == 0, n == OUT_UNITS - 1)
                turn(f"ffn2_{l}", xn, 10 + 6 * l + 6)
                turned_in(f"ffn2_{l}")
                clear_sums()
                swiglu(U_FFN[2 * l + 1], HG_FFN[2 * l + 1])

_INS = ['x', 'attn_w_in', 'attn_sink', 'attn_rpb', 'attn_w_out', 'ssm_w_in', 'ssm_conv_w', 'ssm_conv_b',
        'ssm_dt_bias', 'ssm_A_log', 'ssm_D', 'ssm_norm_w', 'ssm_w_out', 'mlp_w1', 'mlp_w2', 'ln1_g', 'ln1_b',
        'ln2_g', 'ln2_b', 'rel_bias_2', 'ffn1_norm_2', 'ffn1_w_gate_2', 'ffn1_w_up_2', 'ffn1_w_down_2',
        'mix_norm_2', 'w_in_2', 'conv_w_2', 'conv_b_2', 'conv_norm_2', 'q_norm_2', 'k_norm_2', 'lambda_q1_2',
        'lambda_k1_2', 'lambda_q2_2', 'lambda_k2_2', 'subln_norm_2', 'w_out_2', 'ffn2_norm_2',
        'ffn2_w_gate_2', 'ffn2_w_up_2', 'ffn2_w_down_2']


def kernel(**inputs):
    import concourse.bacc as bacc
    from concourse.bass_utils import run_bass_kernel_spmd

    nc = bacc.Bacc("TRN2", target_bir_lowering=False, num_devices=1)
    arrays, args = {}, {}
    for name in _INS:
        a = np.ascontiguousarray(inputs[name])
        arrays["in_" + name] = a
        args[name] = nc.dram_tensor("in_" + name, a.shape, mybir.dt.from_np(a.dtype), kind="ExternalInput").ap()
    c = shape_constants()
    arrays["in_consts"] = c
    args["consts"] = nc.dram_tensor("in_consts", c.shape, F32, kind="ExternalInput").ap()
    out = nc.dram_tensor("out_x", (1, T, D), F32, kind="ExternalOutput").ap()
    two_blocks(nc, args, out)
    r = run_bass_kernel_spmd(nc, [arrays], core_ids=[0])
    return r.results[0]["out_x"]
```

```python
from contextlib import ExitStack
import math

import numpy as np

import concourse.bass as bass
from concourse import mybir

F32 = mybir.dt.float32
F32R = mybir.dt.float32r
ACT = mybir.ActivationFunctionType
ALU = mybir.AluOpType
AX = mybir.AxisListType

P = 128
T = 256
TT = T // P
D = 1024
KC = D // P
HD = 64
DEPTH = 2
ALPHA = float((2 * DEPTH) ** 0.25)
LN_EPS = 1e-5
NEG = -1e30
SCALE = HD ** -0.5

AQ, AKV, BH = 8, 2, 8
A_COLS = (AQ + 2 * AKV + 3 * BH) * HD
GRID_W, NA_KW, NA_KH = 64, 16, 8
WINDOW = 128
RPB_R, RPB_C = 2 * NA_KH - 1, 2 * NA_KW - 1
DI = 2 * D
SH = DI // HD
SG, SN = 8, 128
GH = SH // SG
CONV = 5
F1 = 4 * D
CCH = 512
CK = 31
DH = 4
F2 = 2816
BUCKETS = 32
EPS2 = 1e-6

U = 256
UN = KC * U
RING = 3

A_UNITS = A_COLS // U
Z_UNITS = DI // U
OUT_UNITS = D // U
SSM_COLS = [2 * DI + i * U for i in range(2)] + [2 * DI + 2 * SG * SN] + [2 * DI + i * U for i in range(2, 8)] \
    + [DI + i * U for i in range(Z_UNITS)] + [i * U for i in range(Z_UNITS)]
DT_AT = 2
G1, G2 = F1 // U, F2 // U
MIX_COLS = [2 * U, 0, 3 * U, U] + [2 * CCH + i * U for i in range(6)]
U_ATT = 0
U_ATT_OUT = U_ATT + A_UNITS
U_MLP = [U_ATT_OUT + OUT_UNITS, 0]
U_SSM = U_MLP[0] + 2 * G1
U_SSM_OUT = U_SSM + len(SSM_COLS)
U_MLP[1] = U_SSM_OUT + DI // U
U_SECOND = U_MLP[1] + 2 * G1
U_FFN, U_MIX, U_MIX_OUT = [], [], []
_u = U_SECOND
for _l in range(DEPTH):
    U_FFN.append(_u)
    U_MIX.append(_u + 3 * G2)
    U_MIX_OUT.append(U_MIX[-1] + len(MIX_COLS))
    U_FFN.append(U_MIX_OUT[-1] + OUT_UNITS)
    _u = U_FFN[-1] + 3 * G2
N_UNITS = _u
HG_MLP = [0, G1]
HG_FFN = [2 * G1 + i * G2 for i in range(2 * DEPTH)]

TURNS = ["x", "ln1_0", "ln2_0", "y", "ln1_1"] + [f"{s}_{l}" for l in range(DEPTH) for s in ("ffn1", "mix", "ffn2")]
TURN_CHUNKS = [DI // P if n == "y" else KC for n in TURNS]
TURN_BANK = {n: sum(TURN_CHUNKS[:i]) // 2 for i, n in enumerate(TURNS)}
NORM_PARTS = [0 if n == "x" else 1 + KC // 2 if n.startswith("ln") else 2 for n in TURNS]
NORM_AT = {n: sum(NORM_PARTS[:i]) for i, n in enumerate(TURNS)}

COL = {"ln1_g": 0, "ln1_b": 16, "ln2_g": 32, "ln2_b": 48, "ffn1": 64, "mix": 80, "ffn2": 96, "ssm_norm": 112,
       "ssm_conv_w": 128, "ssm_conv_b": 288, "conv_b": 320, "conv_norm": 328, "subln": 336, "q_norm": 338,
       "k_norm": 340, "conv_w": 384}
ROW_BLOCKS = [128, 128, 86, 124, 124]
COL["conv_w1"] = 512

CONST = {}
_at = 0
for _n, _w in (("ident", P), ("rot", P), ("dup0", P), ("rdup0", P), ("dup1", P), ("rdup1", P), ("na_flip", P),
               ("cos", T), ("sin", T), ("mask_a", 2 * T), ("mask_na", 2 * T),
               ("mask_ssm", 256), ("select", 64), ("nselect", 64),
               ("flip", P), ("halves", P), ("causal", 384), ("buckets", 384)):
    CONST[_n] = (_at, _w)
    _at += _w
CONST_W = _at


def shape_constants():
    c = np.zeros((P, CONST_W), np.float32)

    def put(name, a):
        at, w = CONST[name]
        assert a.shape[1] == w
        c[:a.shape[0], at:at + w] = a

    eye = np.eye(P, dtype=np.float32)
    put("ident", eye)
    half = HD // 2
    rot = np.zeros((P, P), np.float32)
    for b in range(0, P, HD):
        for i in range(half):
            rot[b + half + i, b + i] = -1.0
            rot[b + i, b + half + i] = 1.0
    put("rot", rot)
    for j in range(2):
        dup = np.zeros((P, P), np.float32)
        for b in range(0, P, HD):
            for i in range(HD):
                dup[j * HD + i, b + i] = 1.0
        put(f"dup{j}", dup)
        put(f"rdup{j}", dup @ rot)
    flip = eye[::-1].copy()
    put("flip", flip)
    na = np.zeros((P, P), np.float32)
    for b in range(0, P, 64):
        for i in range(64):
            na[b + 63 - i, b + i] = 1.0
    put("na_flip", na)
    inv = (10000.0 ** (-np.arange(half, dtype=np.float32) / half)).astype(np.float32)
    ang = (np.arange(T, dtype=np.float32)[:, None] * inv[None, :]).astype(np.float32)
    put("cos", np.tile(np.cos(ang).T, (P // half, 1)).astype(np.float32))
    put("sin", np.tile(np.sin(ang).T, (P // half, 1)).astype(np.float32))
    q = np.arange(T)
    far = np.abs(q[:, None] - q[None, :]) > WINDOW
    put("mask_a", np.where(far, np.float32(NEG), np.float32(0)).reshape(2, P, T).transpose(1, 0, 2).reshape(P, 2 * T))
    col = q % GRID_W
    lo = np.clip(col - NA_KW // 2, 0, GRID_W - NA_KW)
    inside = (col[None, :] >= lo[:, None]) & (col[None, :] < lo[:, None] + NA_KW)
    put("mask_na", np.where(inside, np.float32(0), np.float32(NEG)).reshape(2, P, T).transpose(1, 0, 2)
        .reshape(P, 2 * T))
    s, l = np.arange(P)[:, None], np.arange(P)[None, :]
    put("mask_ssm", np.where(np.concatenate([s > l, s < l], 1), np.float32(NEG), np.float32(0)))
    sel = np.concatenate([np.eye(64), np.eye(64)]).astype(np.float32)
    put("select", sel)
    put("nselect", -sel)
    put("halves", np.kron(np.eye(2), np.ones((64, 64))).astype(np.float32))
    k0, k1 = np.arange(P)[None, :], np.arange(T)[None, :]
    put("causal", np.where(np.concatenate([k0 > s, k1 > s + P], 1), np.float32(NEG), np.float32(0)))
    dist = np.maximum(255 - np.arange(384), 0)
    exact = BUCKETS // 2
    nf = np.maximum(dist, 1).astype(np.float32)
    large = exact + (np.log(nf / np.float32(exact)) / np.float32(math.log(128 / exact))
                     * np.float32(BUCKETS - exact)).astype(np.int32)
    bucket = np.where(dist < exact, dist, np.minimum(large, BUCKETS - 1))
    put("buckets", (bucket[None, :] == np.arange(BUCKETS)[:, None]).astype(np.float32))
    return c


def by_pool(u):
    return U_SSM + 2 <= u < U_SSM + 17 or any(U_MIX[l] + 2 <= u < U_MIX_OUT[l] + OUT_UNITS for l in range(DEPTH))


N_SUMS = 4 + 3 * DEPTH
CONST_BLK = 48
N_PAR = 20


def lambda_init(l):
    return 0.8 - 0.6 * math.exp(-0.3 * l)


def two_blocks(nc, A, out):
    with ExitStack() as ctx:
        def sb(name, shape, dt=F32):
            return ctx.enter_context(nc.sbuf_tensor(name, shape, dt))

        def sem(name):
            return ctx.enter_context(nc.semaphore(name))

        w_raw = sb("w_raw", [P, RING, UN])
        w_hi = sb("w_hi", [P, RING, UN], F32R)
        w_lo = sb("w_lo", [P, RING, UN], F32R)
        op_hi = sb("op_hi", [P, 16, T], F32R)
        op_lo = sb("op_lo", [P, 16, T], F32R)
        X = sb("X", [P, TT, D])
        xn = sb("xn", [P, TT, D])
        turn_buf = sb("turn_buf", [P, 2, 2, T])
        act_buf = sb("act_buf", [P, 2 * T])
        h32 = sb("h32", [P, 2 * T])
        gain_row = sb("gain_row", [P, D])
        bias_row = sb("bias_row", [P, D])
        prow = sb("prow", [P, 5, P])
        pcol = sb("pcol", [P, 5 * P])
        ident = sb("ident", [P, P])
        stats = sb("stats", [P, TT, 2, 6])
        mv = sb("mv", [P, TT, 2])
        std = sb("std", [P, TT])
        rstd = sb("rstd", [P, TT])
        ssum = sb("ssum", [P, 4])
        part = sb("part", [P, TT])
        lnb = sb("lnb", [P, 4])
        zeros = sb("zeros", [P, 512], mybir.dt.bfloat16)
        select = sb("select", [P, 64], F32R)
        nselect = sb("nselect", [P, 64], F32R)
        neg_tri = sb("neg_tri", [P, 2, P], F32R)
        ident_r = sb("ident_r", [P, P], F32R)
        g_pair = sb("g_pair", [P, T], F32R)
        AR = 15872
        arena = sb("arena", [P, AR])

        acc = ctx.enter_context(nc.psum_tensor("acc", [P, 4, 512], F32))
        pg = ctx.enter_context(nc.psum_tensor("pg", [P, 4, 512], F32))

        class Carve:
            def __init__(self, at=0):
                self.at = at

            def __call__(self, *shape):
                n = int(np.prod(shape))
                v = arena[:, self.at:self.at + n]
                self.at += n
                assert self.at <= AR, self.at
                if len(shape) == 2:
                    v = v.rearrange("p (a b) -> p a b", a=shape[0])
                elif len(shape) == 3:
                    v = v.rearrange("p (a b c) -> p a b c", a=shape[0], b=shape[1])
                return v

        cv = Carve()
        n_att = CONST["mask_ssm"][0] - P
        att_c = cv(n_att)

        def att_const(name):
            at, w = CONST[name]
            return att_c[:, at - P:at - P + w]

        q_raw = cv(2, 2 * T)
        r_tmp = cv(2, 2 * T)
        k_raw = cv(T)
        QT = cv(8, T)
        KT = cv(6, T)
        va = cv(TT, AKV * HD)
        vb = cv(TT, BH * HD)
        na_bias = cv(BH, 2, T)
        prob = cv(4, 2, T)
        probT = turn_buf
        sink = cv(16)
        mx = cv(16, 2)
        nmx = cv(16, 2)
        psm = cv(16, 2)
        pes = cv(16, 2)
        pden = cv(16, 2)
        cv = Carve()
        BT = cv(SG, T)
        CT = cv(SG, T)
        xs = cv(TT, DI)
        silz = cv(TT, DI)
        ssd_at = cv.at
        E = cv(2, 768)
        CB = cv(2, 768)
        conv_in = Carve(ssd_at)
        over = Carve(ssd_at)
        conv_in = over(2, 2, T + CONV - 1)
        xsT = over(2, 2, T)
        conv_sum = over(2, 2, T)
        assert over.at <= cv.at + 40
        cv.at = max(cv.at, over.at)
        ssm_c = prow[:, :, :].rearrange("p a n -> p (a n)")[:, 0:384]
        dt_bias = cv(64)
        d_skip = cv(SH)
        a_col = cv(1)
        dt_tok = cv(TT, 64)
        one_col = cv(1)
        aT, gT = act_buf[:, 0:T], act_buf[:, T:2 * T]
        dt_v, dt_a = (h32[:, i * P:i * P + P].rearrange("p (t n) -> p t n", t=TT) for i in range(2))
        xD = [b[:, :].rearrange("p (t n) -> p t n", t=TT) for b in (act_buf, h32)]
        ysq = cv(TT, SG)
        yrs = cv(TT, SG)
        diag = xn[:, 0, 0:TT * P].rearrange("p (t n) -> p t n", t=TT)
        scrap = [turn_buf[:, 0, :, :], turn_buf[:, 1, :, :]] + \
            [xn[:, 1, i * 512:(i + 1) * 512].rearrange("p (a n) -> p a n", a=2) for i in range(2)]
        xdt = xn[:, :, :].rearrange("p a (b c) -> p (a b) c", b=4)
        cv = Carve()
        blk_c = cv(CONST_W - CONST["flip"][0])

        def blk_const(name):
            at, w = CONST[name]
            at -= CONST["flip"][0]
            return blk_c[:, at:at + w]

        ones_m = cv(P)
        rbias = cv(DH, 384)
        rel = cv(DH)
        rvec = cv(384)
        lam_q = cv(4, HD)
        lam_k = cv(4, HD)
        lam_s = cv(4)
        lam_e = cv(4)
        nlam = cv(2)
        sub_g = cv(2)
        gate = cv(2, T)
        uu = cv(4, T + CK - 1)
        cacc = cv(4, T)
        sq = turn_buf[:, :, :, :].rearrange("p a b t -> p a (b t)")
        sdev = cv(2, 2 * T)
        Q2 = cv(DH, T)
        K2 = cv(DH, T)
        V2 = cv(TT, 2 * T)
        prob2 = cv(4, 384)
        pmix = cv(2, 384)
        pmixT = cv(2, 384)
        O2 = cv(DH, T)
        osq = cv(4, T)
        odev = xn[:, 0, :].rearrange("p (a t) -> p a t", a=4)
        c32 = xn[:, 1, :].rearrange("p (a t) -> p a t", a=4)
        m2 = cv(8, 2)
        n2 = cv(8, 2)
        s2 = cv(8, 2)
        r2 = cv(8, 2)

        rel_dram = nc.dram_tensor("rel_scratch", (DH, 384), F32, kind="Internal").ap()

        raw_ready = [sem(f"raw_ready{i}") for i in range(RING)]
        hi_ready = sem("hi_ready")
        lo_ready = sem("lo_ready")
        unit_done = sem("unit_done")
        x_in = [sem(f"x_in{t}") for t in range(TT)]
        par_in = sem("par_in")
        const_in = sem("const_in")
        small_in = sem("small_in")
        bias_in = sem("bias_in")
        par_turned = sem("par_turned")
        par_ready = sem("par_ready")
        fixed_ready = sem("fixed_ready")
        bias_flipped = sem("bias_flipped")
        bias_ready = sem("bias_ready")
        bias_evac = sem("bias_evac")
        ident_in = sem("ident_in")
        sum_done = sem("sum_done")
        norm_ready = sem("norm_ready")
        turned = sem("turned")
        gained = sem("gained")
        xt_ready = sem("xt_ready")
        x_new = sem("x_new")
        var_ready = sem("var_ready")
        std_ready = sem("std_ready")
        rows_in = sem("rows_in")
        x_settled = sem("x_settled")
        x_final = sem("x_final")
        dve_link = sem("dve_link")
        act_link = sem("act_link")
        pool_link = sem("pool_link")
        attn_evac = sem("attn_evac")
        rot_done = sem("rot_done")
        rope_done = sem("rope_done")
        score_done = sem("score_done")
        score_taken = sem("score_taken")
        max_ready = sem("max_ready")
        exp_done = sem("exp_done")
        p_ready = sem("p_ready")
        pT_done = sem("pT_done")
        pt_ready = sem("pt_ready")
        pv_done = sem("pv_done")
        ot_hi = sem("ot_hi")
        ot_ready = sem("ot_ready")
        act_done = sem("act_done")
        h32_ready = sem("h32_ready")
        h_hi = sem("h_hi")
        h_ready = sem("h_ready")
        stored = sem("stored")
        dt_sum = sem("dt_sum")
        dt_soft = sem("dt_soft")
        dt_ready = sem("dt_ready")
        dtT_done = sem("dtT_done")
        g_ready = sem("g_ready")
        sel_ready = sem("sel_ready")
        conv_evac = sem("conv_evac")
        conv_done = sem("conv_done")
        conv_silu = sem("conv_silu")
        xsT_done = sem("xsT_done")
        xs_ready = sem("xs_ready")
        z_ready = sem("z_ready")
        cb_done = sem("cb_done")
        cb_ready = sem("cb_ready")
        xdt_ready = sem("xdt_ready")
        diff_done = sem("diff_done")
        e_ready = sem("e_ready")
        m_ready = sem("m_ready")
        head_done = sem("head_done")
        y_gated = sem("y_gated")
        y_sq = sem("y_sq")
        y_std = sem("y_std")
        lam_in = sem("lam_in")
        lam_sum = sem("lam_sum")
        lam_exp = sem("lam_exp")
        rel_sum = sem("rel_sum")
        rel_row = sem("rel_row")
        rel_out = sem("rel_out")
        gate_ready = sem("gate_ready")
        u_ready = sem("u_ready")
        qk_sq = sem("qk_sq")
        qk_sum = sem("qk_sum")
        qk_std = sem("qk_std")
        qk_ready = sem("qk_ready")
        v_ready = sem("v_ready")
        sc2_done = sem("sc2_done")
        sc2_taken = sem("sc2_taken")
        mx2_ready = sem("mx2_ready")
        ex2_done = sem("ex2_done")
        mix_ready = sem("mix_ready")
        mixT_done = sem("mixT_done")
        mixT_ready = sem("mixT_ready")
        o2_done = sem("o2_done")
        o2_evac = sem("o2_evac")
        osq_sum = sem("osq_sum")
        osq_std = sem("osq_std")
        o2_norm = sem("o2_norm")
        o2_hi = sem("o2_hi")
        o2_ready = sem("o2_ready")
        cconv = sem("cconv")
        csq = sem("csq")
        csum = sem("csum")
        cstd = sem("cstd")
        cnorm = sem("cnorm")
        c_hi = sem("c_hi")
        c_ready = sem("c_ready")

        def at(base, it, per):
            return base if it is None else base + it * per

        class Link:
            def __init__(self, eng, s):
                self.eng, self.s, self.n = eng, s, 0

            def __call__(self, ins):
                self.n += 1
                ins.then_inc(self.s, 1)
                self.eng.wait_ge(self.s, self.n)

        def cols_view(w):
            return w.rearrange("(k p) n -> p k n", p=P)

        v_att = cols_view(A["attn_w_in"][0])
        v_ssm = cols_view(A["ssm_w_in"][0])
        v_att_out = cols_view(A["attn_w_out"][0])
        v_ssm_out = cols_view(A["ssm_w_out"][0])
        v_w1 = [cols_view(A["mlp_w1"][l]) for l in range(DEPTH)]
        v_w2 = [cols_view(A["mlp_w2"][l]) for l in range(DEPTH)]
        ffn = [(cols_view(A[f"ffn{s}_w_gate_2"][l]), cols_view(A[f"ffn{s}_w_up_2"][l]),
                cols_view(A[f"ffn{s}_w_down_2"][l])) for l in range(DEPTH) for s in (1, 2)]
        v_mix = [cols_view(A["w_in_2"][l]) for l in range(DEPTH)]
        v_mix_out = [cols_view(A["w_out_2"][l]) for l in range(DEPTH)]

        n_par = [0]
        n_rows = [0]
        block = ctx.enter_context(nc.Block())

        @block.sync
        def _(sp):
            def load(u, src, it=None, per=0, width=UN):
                if u >= RING:
                    sp.wait_ge(lo_ready, at(u - RING + 1, it, per))
                dst = w_raw[:, u % RING, 0:width].rearrange("p (k n) -> p k n", k=src.shape[1])
                sp.dma_start(dst, src).then_inc(raw_ready[u % RING], 16)

            def columns(v, c):
                return v[:, :, c:c + U]

            def rows(v, g):
                return v[:, 2 * g:2 * g + 2, :]

            def mlp(u0, w1, w2):
                load(u0, columns(w1, 0))
                with sp.Fori(0, (G1 - 1) // 3) as it:
                    for j in range(3):
                        load(u0 + 1 + 2 * j, w1[:, :, bass.ds(it * (3 * U) + (1 + j) * U, U)], it, 6)
                        load(u0 + 2 + 2 * j, w2[:, bass.ds(it * 6 + 2 * j, 2), :], it, 6)
                load(u0 + 2 * G1 - 1, rows(w2, G1 - 1))

            def swiglu(u0, w):
                load(u0, columns(w[0], 0))
                load(u0 + 1, columns(w[1], 0))
                with sp.Fori(0, G2 - 1) as it:
                    load(u0 + 2, w[0][:, :, bass.ds(it * U + U, U)], it, 3)
                    load(u0 + 3, w[1][:, :, bass.ds(it * U + U, U)], it, 3)
                    load(u0 + 4, w[2][:, bass.ds(it * 2, 2), :], it, 3)
                load(u0 + 3 * G2 - 1, rows(w[2], G2 - 1))

            for t in range(TT):
                sp.dma_start(X[:, t, :], A["x"][0, t * P:(t + 1) * P, :]).then_inc(x_in[t], 16)
            for n in range(A_UNITS):
                load(U_ATT + n, columns(v_att, n * U))
            for n in range(OUT_UNITS):
                load(U_ATT_OUT + n, rows(v_att_out, n))
            mlp(U_MLP[0], v_w1[0], v_w2[0])
            for n, c in enumerate(SSM_COLS):
                if n == DT_AT:
                    load(U_SSM + n, v_ssm[:, :, c:c + 64], width=KC * 64)
                else:
                    load(U_SSM + n, columns(v_ssm, c))
            for n in range(DI // U):
                load(U_SSM_OUT + n, rows(v_ssm_out, n))
            mlp(U_MLP[1], v_w1[1], v_w2[1])
            for l in range(DEPTH):
                swiglu(U_FFN[2 * l], ffn[2 * l])
                for n, c in enumerate(MIX_COLS):
                    load(U_MIX[l] + n, columns(v_mix[l], c))
                for n in range(OUT_UNITS):
                    load(U_MIX_OUT[l] + n, rows(v_mix_out[l], (n + 2) % 4))
                swiglu(U_FFN[2 * l + 1], ffn[2 * l + 1])
            for t in range(TT):
                sp.wait_ge(x_new, 4 * (N_SUMS - 1) + 2 * (t + 1))
                sp.dma_start(out[0, t * P:(t + 1) * P, :], X[:, t, :]).then_inc(stored, 16)
            sp.wait_ge(stored, 16 * TT)

        @block.gpsimd
        def _(pool):
            link = Link(pool, pool_link)

            def par(dst, src):
                pool.dma_start(dst, src).then_inc(par_in, 16)
                n_par[0] += 1

            def rows_of(v):
                return v.rearrange("l (c p) -> (l c) p", p=P)

            for i, n in enumerate(("ln1_g", "ln1_b", "ln2_g", "ln2_b", "ffn1_norm_2", "mix_norm_2", "ffn2_norm_2",
                                   "ssm_norm_w")):
                par(prow[16 * i:16 * i + 16, 0, :], rows_of(A[n]))
            cw = A["ssm_conv_w"][0].rearrange("k (c p) -> (k c) p", p=P)
            par(prow[:, 1, :], cw[0:128, :])
            par(prow[0:32, 2, :], cw[128:160, :])
            par(prow[32:64, 2, :], rows_of(A["ssm_conv_b"]))
            par(prow[64:72, 2, :], rows_of(A["conv_b_2"]))
            par(prow[72:80, 2, :], rows_of(A["conv_norm_2"]))
            par(prow[80:82, 2, :], A["subln_norm_2"])
            for h in range(2):
                par(prow[82:84, 2, h * HD:h * HD + HD], A["q_norm_2"])
                par(prow[84:86, 2, h * HD:h * HD + HD], A["k_norm_2"])
            for l in range(DEPTH):
                par(prow[0:CK * 4, 3 + l, :], A["conv_w_2"][l].rearrange("k (c p) -> (k c) p", p=P))

            rpb = A["attn_rpb"]
            for h in range(BH):
                for qt in range(TT):
                    for r in range(2):
                        src = bass.AP(rpb.tensor, rpb.offset + h * RPB_R * RPB_C + (NA_KH - 1 - 2 * qt - r) * RPB_C
                                      + NA_KW - 1 - (GRID_W - 1), [[1, 64], [RPB_C, 4], [1, GRID_W]])
                        pool.dma_start(na_bias[r * 64:r * 64 + 64, h, qt, :].rearrange("p (a k) -> p a k", a=4),
                                       src).then_inc(bias_in, 16)
            pool.dma_start(sink[:, 0:AQ], A["attn_sink"].broadcast_to([P, AQ])).then_inc(small_in, 16)

            def split(u):
                assert by_pool(u)
                pool.wait_ge(hi_ready, u + 1)
                if not by_pool(u - 1):
                    pool.wait_ge(lo_ready, u)
                r = u % RING
                pool.tensor_tensor(w_lo[:, r, :], w_raw[:, r, :], w_hi[:, r, :].bitcast(F32), ALU.subtract) \
                    .then_inc(lo_ready, 1)

            lns = [("ln1", 0), ("ln2", 0), ("ln1", 1), ("ln2", 1)]

            def rows_load(i):
                n, l = lns[i]
                pool.dma_start(gain_row[:, :], A[n + "_g"][l:l + 1, :].broadcast_to([P, D])).then_inc(rows_in, 16)
                pool.dma_start(bias_row[:, :], A[n + "_b"][l:l + 1, :].broadcast_to([P, D])).then_inc(rows_in, 16)

            def settle(i, name):
                pool.wait_ge(rows_in, 32 * (i + 1))
                pool.wait_ge(norm_ready, NORM_AT[name] + 1 + KC // 2)
                for t in range(TT):
                    link(pool.tensor_tensor(X[:, t, :], xn[:, t, :], gain_row[:, :], ALU.mult))
                for t in range(TT):
                    ins = pool.tensor_tensor(X[:, t, :], X[:, t, :], bias_row[:, :], ALU.add)
                    ins.then_inc(x_settled, 1)
                pool.wait_ge(x_settled, 2 * (i + 1))

            rows_load(0)
            settle(0, "ln1_0")
            rows_load(1)
            pool.wait_ge(h_ready, HG_MLP[0] + G1)
            pool.dma_start(dt_bias, A["ssm_dt_bias"].broadcast_to([P, 64])).then_inc(small_in, 16)
            pool.dma_start(d_skip, A["ssm_D"].broadcast_to([P, SH])).then_inc(small_in, 16)
            pool.dma_start(a_col[0:64, :], A["ssm_A_log"].rearrange("a d (h o) -> (a d h) o", o=1)) \
                .then_inc(small_in, 16)
            settle(1, "ln2_0")
            rows_load(2)
            for n in range(2, 17):
                split(U_SSM + n)

            pool.wait_ge(dt_ready, 1)
            pool.wait_ge(small_in, 64)
            for g in range(SG):
                b = g % 2
                pool.wait_ge(xs_ready, g + 1)
                if g >= 2:
                    pool.wait_ge(head_done, GH * (g - 1))
                for t in range(TT):
                    xg = xs[:, t, g * U:g * U + U].rearrange("p (h e) -> p h e", h=GH)
                    for d in range(2):
                        dts = dt_tok[:, t, d * SH + g * GH:d * SH + (g + 1) * GH]
                        pool.tensor_tensor(xdt[:, b * 4 + d * 2 + t, :].rearrange("p (h e) -> p h e", h=GH), xg,
                                           dts.unsqueeze(2).broadcast_to([P, GH, HD]), ALU.mult)
                if g >= 2:
                    pool.wait_ge(y_gated, g - 1)
                for t in range(TT):
                    xg = xs[:, t, g * U:g * U + U].rearrange("p (h e) -> p h e", h=GH)
                    ds = d_skip[:, g * GH:(g + 1) * GH]
                    ins = pool.tensor_tensor(xD[b][:, t, :].rearrange("p (h e) -> p h e", h=GH), xg,
                                             ds.unsqueeze(2).broadcast_to([P, GH, HD]), ALU.mult)
                ins.then_inc(xdt_ready, 1)
            pool.wait_ge(norm_ready, NORM_AT["ln1_1"] + 1)
            pool.dma_start(rel[0:BUCKETS, :], A["rel_bias_2"]).then_inc(lam_in, 16)
            for i, n in enumerate(("lambda_q1_2", "lambda_q2_2")):
                pool.dma_start(lam_q[:, 2 * i:2 * i + 2, :], A[n].unsqueeze(0).broadcast_to([P, DEPTH, HD])) \
                    .then_inc(lam_in, 16)
            for i, n in enumerate(("lambda_k1_2", "lambda_k2_2")):
                pool.dma_start(lam_k[:, 2 * i:2 * i + 2, :], A[n].unsqueeze(0).broadcast_to([P, DEPTH, HD])) \
                    .then_inc(lam_in, 16)
            settle(2, "ln1_1")
            rows_load(3)
            pool.wait_ge(rel_row, 1)
            pool.dma_start(rel_dram, rvec[0:DH, :]).then_inc(rel_out, 16)
            pool.wait_ge(rel_out, 16)
            for h in range(DH):
                for off, k0, n in ((128, 0, 128), (0, 128, 256)):
                    src = bass.AP(rel_dram.tensor, rel_dram.offset + h * 384 + off, [[1, P], [1, n]])
                    pool.dma_start(rbias[:, h, k0:k0 + n], src).then_inc(bias_in, 16)
            for h in range(DH):
                pool.wait_ge(bias_evac, h + 1)
                if h == 0:
                    pool.wait_ge(const_in, CONST_BLK)
                pool.tensor_tensor(rbias[:, h, :], rbias[:, h, :], blk_const("causal"), ALU.add) \
                    .then_inc(bias_ready, 1)
            for l in range(DEPTH):
                for u in range(U_MIX[l] + 2, U_MIX_OUT[l] + OUT_UNITS):
                    split(u)

        @block.scalar
        def _(act):
            link = Link(act, act_link)

            def split(u, it=None, per=0):
                if u >= N_UNITS:
                    return
                act.wait_ge(raw_ready[u % RING], at(16 * (u // RING + 1), it, 16 * per // RING))
                if u >= RING:
                    act.wait_ge(unit_done, at(u - RING + 1, it, per))
                act.copy(w_hi[:, u % RING, :], w_raw[:, u % RING, :]).then_inc(hi_ready, 1)

            def turn(name, gain, bias):
                for b in range(TURN_CHUNKS[TURNS.index(name)] // 2):
                    k = TURN_BANK[name] + b
                    act.wait_ge(turned, k + 1)
                    if bias is not None and b >= 2:
                        act.wait_ge(xt_ready, k - 1)
                    for c in range(2):
                        j = 2 * b + c
                        ins = act.activation(op_hi[:, j, :] if bias is None else turn_buf[:, b % 2, c, :],
                                             pg[:, b % 4, c * T:(c + 1) * T], ACT.Identity,
                                             scale=1.0 if gain is None else pcol[:, gain + j:gain + j + 1],
                                             bias=0.0 if bias is None else pcol[:, bias + j:bias + j + 1])
                    ins.then_inc(gained, 1)

            def ln_std(k):
                act.activation(part[:, 0:1], lnb[:, 0:1], ACT.Sqrt)
                for t in range(TT):
                    act.wait_ge(var_ready, 2 * (k - 1) + t + 1)
                    act.activation(std[:, t:t + 1], mv[:, t, 1:2], ACT.Sqrt, bias=lnb[:, 0:1]) \
                        .then_inc(std_ready, 1)

            def rms_std(k, src_ready, base):
                link(act.activation(part[:, 0:1], lnb[:, 0:1], ACT.Sqrt))
                for t in range(TT):
                    for a in range(2):
                        q = 2 * t + a
                        act.wait_ge(src_ready, base + q + 1)
                        link(act.activation(scrap[q], X[:, t, a * 512:(a + 1) * 512]
                                            .rearrange("p (a n) -> p a n", a=2), ACT.Square,
                                            accum_out=ssum[:, q:q + 1]))
                        if a == 0:
                            link(act.activation(part[:, t:t + 1], ssum[:, q:q + 1], ACT.Identity, scale=1.0 / D,
                                                bias=lnb[:, 1:2]))
                    act.activation(std[:, t:t + 1], ssum[:, q:q + 1], ACT.Sqrt, bias=part[:, t:t + 1],
                                   scale=1.0 / D).then_inc(std_ready, 1)

            def hidden(h, u_in, func, src, it=None, per_h=0, per_u=0):
                act.wait_ge(unit_done, at(u_in + 1, it, per_u))
                act.activation(act_buf[:, :], src, func).then_inc(act_done, 1)

            def hidden_hi(h, u_free, it=None, per_h=0, per_u=0):
                act.wait_ge(h32_ready, at(h + 1, it, per_h))
                if u_free is not None:
                    act.wait_ge(unit_done, at(u_free + 1, it, per_u))
                act.copy(op_hi[:, 8:10, :], h32[:, :].rearrange("p (c t) -> p c t", c=2)).then_inc(h_hi, 1)

            def mlp(u0, h0):
                split(u0 + 2)
                hidden(h0, u0, ACT.Relu, pg[:, 0, :])
                hidden_hi(h0, None)
                with act.Fori(0, (G1 - 1) // 3) as it:
                    for j in range(3):
                        u = u0 + 1 + 2 * j
                        split(u + 2, it, 6)
                        hidden(h0 + 1 + j, u, ACT.Relu, pg[:, (1 + j) % 3, :], it, 3, 6)
                        split(u + 3, it, 6)
                        hidden_hi(h0 + 1 + j, u + 1, it, 3, 6)
                split(u0 + 2 * G1 + 1)

            def swiglu(u0, h0):
                split(u0 + 2)
                hidden(h0, u0, ACT.Silu, pg[:, 0, :])
                split(u0 + 3)
                hidden_hi(h0, None)

                def group(u, h, it=None):
                    split(u + 2, it, 3)
                    hidden(h, u, ACT.Silu, pg[:, 0, :], it, 1, 3)
                    split(u + 3, it, 3)
                    split(u + 4, it, 3)
                    hidden_hi(h, u + 2, it, 1, 3)

                last = u0 + 3 * G2 == N_UNITS
                with act.Fori(0, G2 - 1 - last) as it:
                    group(u0 + 2, h0 + 1, it)
                if last:
                    group(u0 + 3 * G2 - 4, h0 + G2 - 1)
                split(u0 + 3 * G2 + 1)

            def o2_out(act, l, h):
                i = DH * l + h
                act.wait_ge(o2_done, i + 1)
                act.copy(O2[:, h, :], acc[:, h % 2, 0:T])
                act.activation(osq[:, h, :], acc[:, h % 2, 0:T], ACT.Square).then_inc(o2_evac, 1)

            act.dma_start(ident[:, :], A["consts"][:, 0:P]).then_inc(ident_in, 16)
            act.dma_start(att_c, A["consts"][:, P:P + n_att]).then_inc(const_in, 16)
            turn("x", None, None)
            split(0)
            split(1)

            for n in range(A_UNITS):
                u = U_ATT + n
                split(u + 2)
                act.wait_ge(unit_done, u + 1)
                bank = pg[:, n % 4, :]
                pair = bank.rearrange("p (c t) -> p c t", c=2)
                if n < 2:
                    ins = act.copy(q_raw[:, n, :], bank)
                elif n == 2:
                    act.copy(k_raw, bank[:, 0:T])
                    ins = act.copy(va, bank[:, T:2 * T].rearrange("p (t n) -> p t n", t=TT))
                elif n < 5:
                    ins = act.copy(QT[:, 4 + 2 * (n - 3):6 + 2 * (n - 3), :], pair)
                elif n < 7:
                    ins = act.copy(KT[:, 2 + 2 * (n - 5):4 + 2 * (n - 5), :], pair)
                else:
                    ins = act.copy(vb[:, :, (n - 7) * U:(n - 6) * U], pair)
                ins.then_inc(attn_evac, 1)
            for s in range(AQ + BH + 4):
                if s < AQ + BH:
                    act.wait_ge(max_ready, s + 1)
                    for qt in range(TT):
                        act.activation(prob[:, s % 4, qt, :], prob[:, s % 4, qt, :], ACT.Exp,
                                       bias=nmx[:, s, qt:qt + 1], accum_out=psm[:, s, qt:qt + 1])
                    act.activation(pes[:, s, :], nmx[:, s, :], ACT.Exp, bias=sink[:, s:s + 1]).then_inc(exp_done, 1)
                h = s - 2
                if 0 <= h < AQ + BH:
                    act.wait_ge(pT_done, h + 1)
                    if h >= 2:
                        act.wait_ge(pv_done, h - 1)
                    act.copy(probT[:, h % 2, :, :], pg[:, 2 + h % 2, :].rearrange("p (c t) -> p c t", c=2)) \
                        .then_inc(pt_ready, 1)
                if s >= 5 and s % 2 == 1:
                    c = (s - 5) // 2
                    act.wait_ge(pv_done, 2 * c + 2)
                    act.copy(op_hi[:, 8 + c, :], acc[:, c % 4, 0:T]).then_inc(ot_hi, 1)
            for n in range(OUT_UNITS):
                split(U_ATT_OUT + n + 2)
            ln_std(1)
            turn("ln1_0", COL["ln1_g"], COL["ln1_b"])
            mlp(U_MLP[0], HG_MLP[0])
            act.wait_ge(h_ready, HG_MLP[0] + G1)
            c0 = CONST["mask_ssm"][0]
            act.dma_start(ssm_c, A["consts"][:, c0:c0 + 384]).then_inc(const_in, 16)
            ln_std(2)
            act.wait_ge(const_in, 32)
            act.copy(select[:, :], ssm_c[:, 256:320])
            act.copy(neg_tri[:, :, :], ssm_c[:, 0:256].rearrange("p (d n) -> p d n", d=2))
            act.copy(ident_r[:, :], ident[:, :])
            act.copy(nselect[:, :], ssm_c[:, 320:384]).then_inc(sel_ready, 1)
            turn("ln2_0", COL["ln2_g"], COL["ln2_b"])

            def conv_act(i):
                act.wait_ge(conv_done, i + 1)
                bias = COL["ssm_conv_b"]
                for c in range(2):
                    ch = (16 + 2 * i + c) % 32
                    if i < 8:
                        dst = (BT if i < 4 else CT)[:, 2 * (i % 4) + c, :]
                    else:
                        if i >= 10 and c == 0:
                            act.wait_ge(xsT_done, i - 9)
                        dst = xsT[:, i % 2, c, :]
                    ins = act.activation(dst, conv_sum[:, i % 2, c, :], ACT.Silu,
                                         bias=pcol[:, bias + ch:bias + ch + 1])
                ins.then_inc(conv_silu, 1)

            i = 0
            for n in range(len(SSM_COLS)):
                u = U_SSM + n
                split(u + 2)
                if n == DT_AT:
                    act.wait_ge(dt_sum, 1)
                    link(act.activation(dt_a, dt_v, ACT.Abs))
                    link(act.activation(dt_a, dt_a, ACT.Exp, scale=-1.0))
                    act.activation(dt_a, dt_a, ACT.Ln, bias=1.0).then_inc(dt_soft, 1)
                    act.activation(a_col[0:64, :], a_col[0:64, :], ACT.Exp).then_inc(dt_soft, 1)
                    continue
                act.wait_ge(unit_done, u + 1)
                pair = pg[:, n % 4, :].rearrange("p (c t) -> p c t", c=2)
                if n < len(SSM_COLS) - Z_UNITS:
                    if i >= 2:
                        act.wait_ge(conv_done, i - 1)
                    act.copy(conv_in[:, i % 2, :, 2:2 + T], pair).then_inc(conv_evac, 1)
                    if i >= 1:
                        conv_act(i - 1)
                    i += 1
                else:
                    if i == 16:
                        conv_act(15)
                        i += 1
                    z = n - (len(SSM_COLS) - Z_UNITS)
                    act.activation(silz[:, :, z * U:z * U + U], pair, ACT.Silu).then_inc(z_ready, 1)
            for h in range(SH):
                b = h % 2
                act.wait_ge(diff_done, h + 1)
                if h >= 2:
                    act.wait_ge(head_done, h - 1)
                act.activation(E[:, b, :], pg[:, 2 * b:2 * b + 2, :].rearrange("p a n -> p (a n)")[:, 0:768],
                               ACT.Exp).then_inc(e_ready, 1)
                if h % GH == 1 and h > GH:
                    g = h // GH - 1
                    act.wait_ge(y_gated, g + 1)
                    for t in range(TT):
                        ins = act.activation(turn_buf[:, 0, t, :], xs[:, t, g * U:g * U + U], ACT.Square,
                                             accum_out=ysq[:, t, g:g + 1])
                    ins.then_inc(y_sq, 1)
            act.wait_ge(y_gated, SG)
            for t in range(TT):
                ins = act.activation(turn_buf[:, 0, t, :], xs[:, t, (SG - 1) * U:SG * U], ACT.Square,
                                     accum_out=ysq[:, t, SG - 1:SG])
            link(ins)
            act.activation(yrs, ysq, ACT.Sqrt, bias=lnb[:, 0:1], scale=1.0 / U).then_inc(y_std, 1)
            turn("y", COL["ssm_norm"], None)
            for n in range(DI // U):
                split(U_SSM_OUT + n + 2)
            ln_std(3)
            act.wait_ge(norm_ready, NORM_AT["ln1_1"] + 1)
            act.dma_start(blk_c, A["consts"][:, CONST["flip"][0]:CONST_W]).then_inc(const_in, 16)
            turn("ln1_1", COL["ln1_g"] + 8, COL["ln1_b"] + 8)
            act.wait_ge(lam_sum, 1)
            act.activation(lam_e, lam_s, ACT.Exp).then_inc(lam_exp, 1)
            mlp(U_MLP[1], HG_MLP[1])
            for h in range(DH):
                act.wait_ge(bias_flipped, BH + h + 1)
                act.copy(rbias[:, h, :], pg[:, h, 0:384]).then_inc(bias_evac, 1)
            ln_std(4)

            for l in range(DEPTH):
                if l == 0:
                    rms_std(5, x_final, 0)
                else:
                    rms_std(4 + 3 * l + 1, x_new, 4 * (3 + 3 * l))
                turn(f"ffn1_{l}", COL["ffn1"] + 8 * l, None)
                swiglu(U_FFN[2 * l], HG_FFN[2 * l])
                rms_std(4 + 3 * l + 2, x_new, 4 * (4 + 3 * l))
                turn(f"mix_{l}", COL["mix"] + 8 * l, None)
                for n in range(len(MIX_COLS)):
                    u = U_MIX[l] + n
                    split(u + 2)
                    bank = pg[:, n % 4, :]
                    pair = bank.rearrange("p (c t) -> p c t", c=2)
                    if n in (0, 2):
                        act.wait_ge(unit_done, u + 1)
                        if n == 2:
                            act.wait_ge(u_ready, 4 * l + 2)
                        act.activation(gate, pair, ACT.Sigmoid).then_inc(gate_ready, 1)
                    elif 4 <= n < 8:
                        i = 4 * l + n - 4
                        act.wait_ge(unit_done, u + 1)
                        if i >= 2:
                            act.wait_ge(qk_sum, i - 1)
                        act.activation(sq[:, i % 2, :], bank, ACT.Square).then_inc(qk_sq, 1)
                        act.wait_ge(qk_sum, i + 1)
                        if i >= 2:
                            act.wait_ge(qk_ready, i - 1)
                        act.activation(sdev[:, i % 2, :], acc[:, i % 2, :], ACT.Sqrt, bias=lnb[:, 1:2],
                                       scale=1.0 / HD).then_inc(qk_std, 1)
                    elif n >= 8:
                        act.wait_ge(unit_done, u + 1)
                        act.copy(V2[:, :, (n - 8) * U:(n - 7) * U], pair).then_inc(v_ready, 1)
                for s in range(2 * DH + 3):
                    i = 8 * l + s
                    if s < 2 * DH:
                        act.wait_ge(mx2_ready, i + 1)
                        b = s % 4
                        act.activation(prob2[:, b, 0:P], prob2[:, b, 0:P], ACT.Exp, bias=n2[:, s, 0:1],
                                       accum_out=s2[:, s, 0:1])
                        act.activation(prob2[:, b, P:384], prob2[:, b, P:384], ACT.Exp, bias=n2[:, s, 1:2],
                                       accum_out=s2[:, s, 1:2]).then_inc(ex2_done, 1)
                    if s >= 4 and s % 2 == 0:
                        h = DH * l + (s - 4) // 2
                        act.wait_ge(mixT_done, h + 1)
                        if h >= 2:
                            act.wait_ge(o2_done, h - 1)
                        act.copy(pmixT[:, h % 2, :], pg[:, 2 + h % 2, 0:384]).then_inc(mixT_ready, 1)
                    if s >= 6 and s % 2 == 0:
                        o2_out(act, l, (s - 6) // 2)
                o2_out(act, l, DH - 1)
                act.wait_ge(osq_sum, l + 1)
                act.activation(odev, acc[:, 2:4, :].rearrange("p a (b n) -> p (a b) n", b=2), ACT.Sqrt,
                               bias=lnb[:, 1:2], scale=1.0 / P).then_inc(osq_std, 1)
                act.wait_ge(o2_norm, l + 1)
                act.copy(op_hi[:, 12:16, :], O2).then_inc(o2_hi, 1)
                act.wait_ge(cconv, l + 1)
                act.activation(osq, cacc, ACT.Square).then_inc(csq, 1)
                act.wait_ge(csum, l + 1)
                act.activation(odev[:, 0, :], pg[:, 0, 0:T], ACT.Sqrt, bias=lnb[:, 1:2],
                               scale=1.0 / CCH).then_inc(cstd, 1)
                act.wait_ge(cnorm, l + 1)
                for c in range(4):
                    k = COL["conv_norm"] + 4 * l + c
                    ins = act.activation(c32[:, c, :], osq[:, c, :], ACT.Silu, scale=pcol[:, k:k + 1])
                link(ins)
                act.copy(op_hi[:, 8:12, :], c32).then_inc(c_hi, 1)
                for n in range(OUT_UNITS):
                    split(U_MIX_OUT[l] + n + 2)
                rms_std(4 + 3 * l + 3, x_new, 4 * (5 + 3 * l))
                turn(f"ffn2_{l}", COL["ffn2"] + 8 * l, None)
                swiglu(U_FFN[2 * l + 1], HG_FFN[2 * l + 1])

        @block.vector
        def _(dve):
            link = Link(dve, dve_link)

            def split(u, it=None, per=0):
                if u >= N_UNITS or it is None and by_pool(u):
                    return
                dve.wait_ge(hi_ready, at(u + 1, it, per))
                if it is None and by_pool(u - 1):
                    dve.wait_ge(lo_ready, u)
                s = u % RING
                dve.tensor_tensor(w_lo[:, s, :], w_raw[:, s, :], w_hi[:, s, :].bitcast(F32), ALU.subtract) \
                    .then_inc(lo_ready, 1)

            def turn(name, gain=None):
                for b in range(TURN_CHUNKS[TURNS.index(name)] // 2):
                    k = TURN_BANK[name] + b
                    dve.wait_ge(gained, k + 1)
                    dst = slice(2 * b, 2 * b + 2)
                    hi = op_hi[:, dst, :]
                    if name.startswith("ln"):
                        link(dve.tensor_copy(hi, turn_buf[:, b % 2, :, :]))
                        ins = dve.tensor_tensor(op_lo[:, dst, :], turn_buf[:, b % 2, :, :], hi.bitcast(F32),
                                                ALU.subtract)
                    elif gain is None:
                        ins = dve.tensor_tensor(op_lo[:, dst, :], pg[:, b % 4, :].rearrange("p (c t) -> p c t", c=2),
                                                hi.bitcast(F32), ALU.subtract)
                    else:
                        for c in range(2):
                            j = 2 * b + c
                            ins = dve.scalar_tensor_tensor(out=op_lo[:, j, :], in0=pg[:, b % 4, c * T:(c + 1) * T],
                                                           scalar=pcol[:, gain + j:gain + j + 1],
                                                           in1=op_hi[:, j, :].bitcast(F32),
                                                           op0=ALU.mult, op1=ALU.subtract)
                    ins.then_inc(xt_ready, 1)

            def bank_done(u_last, k, q):
                if q < 3:
                    dve.wait_ge(sum_done, 3 * (k - 1) + q + 1)
                else:
                    dve.wait_ge(unit_done, u_last + 1)

            def rstd_make(k, t):
                dve.wait_ge(std_ready, 2 * (k - 1) + t + 1)
                link(dve.reciprocal(rstd[:, t:t + 1], std[:, t:t + 1]))

            def ln(u_last, k, apply):
                if k > 1:
                    dve.wait_ge(x_settled, 2 * (k - 1))
                for q in range(4):
                    t, a = q // 2, q % 2
                    bank_done(u_last, k, q)
                    x = X[:, t, a * 512:(a + 1) * 512]
                    dve.scalar_tensor_tensor(out=x, in0=x, scalar=ALPHA, in1=acc[:, q, :], op0=ALU.mult,
                                             op1=ALU.add).then_inc(x_new, 1)
                    dve.wait_ge(x_new, 4 * (k - 1) + q + 1)
                    ins = dve.bn_stats(stats[:, t, a, :], x)
                    if a == 1:
                        link(ins)
                        dve.bn_aggr(mv[:, t, :], stats[:, t, :, :].rearrange("p a n -> p (a n)")) \
                            .then_inc(var_ready, 1)
                    if q == 2:
                        apply(k, 0)
                apply(k, 1)

            def normalise(k, t):
                rstd_make(k, t)
                parts = KC // 2 if t else 1
                w = D // parts
                for i in range(parts):
                    dve.tensor_scalar(xn[:, t, i * w:(i + 1) * w], X[:, t, i * w:(i + 1) * w], mv[:, t, 0:1],
                                      rstd[:, t:t + 1], ALU.subtract, ALU.mult).then_inc(norm_ready, 1)

            def settle(k, t):
                if t == 0:
                    dve.wait_ge(rows_in, 128)
                dve.wait_ge(var_ready, 2 * (k - 1) + t + 1)
                for a in range(2):
                    x = X[:, t, a * 512:(a + 1) * 512]
                    ins = dve.scalar_tensor_tensor(out=x, in0=x, scalar=mv[:, t, 0:1],
                                                   in1=gain_row[:, a * 512:(a + 1) * 512],
                                                   op0=ALU.subtract, op1=ALU.mult)
                link(ins)
                rstd_make(k, t)
                for a in range(2):
                    x = X[:, t, a * 512:(a + 1) * 512]
                    dve.scalar_tensor_tensor(out=x, in0=x, scalar=rstd[:, t:t + 1],
                                             in1=bias_row[:, a * 512:(a + 1) * 512],
                                             op0=ALU.mult, op1=ALU.add).then_inc(x_final, 1)

            def rms(k, t):
                rstd_make(k, t)
                dve.tensor_scalar(diag[:, t, :], ident[:, :], rstd[:, t:t + 1], None, ALU.mult) \
                    .then_inc(norm_ready, 1)

            def residual(u_last, k, factor, norm=True):
                for q in range(4):
                    bank_done(u_last, k, q)
                    x = X[:, q // 2, (q % 2) * 512:(q % 2 + 1) * 512]
                    dve.scalar_tensor_tensor(out=x, in0=acc[:, q, :], scalar=factor, in1=x, op0=ALU.mult,
                                             op1=ALU.add).then_inc(x_new, 1)
                    if norm and q == 2:
                        rms(k + 1, 0)
                if norm:
                    rms(k + 1, 1)

            def hidden(h, u_in, make, it=None, per_h=0, per_u=0):
                dve.wait_ge(act_done, at(h + 1, it, per_h))
                if h:
                    dve.wait_ge(h_ready, at(h, it, per_h))
                if u_in is not None:
                    dve.wait_ge(unit_done, at(u_in + 1, it, per_u))
                make().then_inc(h32_ready, 1)

            def hidden_lo(h, it=None, per_h=0):
                dve.wait_ge(h_hi, at(h + 1, it, per_h))
                dve.tensor_tensor(op_lo[:, 8:10, :], h32[:, :].rearrange("p (c t) -> p c t", c=2),
                                  op_hi[:, 8:10, :].bitcast(F32), ALU.subtract).then_inc(h_ready, 1)

            def square():
                return dve.tensor_tensor(h32[:, :], act_buf[:, :], act_buf[:, :], ALU.mult)

            def gated():
                return dve.tensor_tensor(h32[:, :], act_buf[:, :], pg[:, 1, :], ALU.mult)

            def mlp(u0, h0):
                split(u0 + 2)
                hidden(h0, None, square)
                hidden_lo(h0)
                with dve.Fori(0, (G1 - 1) // 3) as it:
                    for j in range(3):
                        u = u0 + 1 + 2 * j
                        split(u + 2, it, 6)
                        hidden(h0 + 1 + j, None, square, it, 3, 6)
                        split(u + 3, it, 6)
                        hidden_lo(h0 + 1 + j, it, 3)
                split(u0 + 2 * G1 + 1)

            def swiglu(u0, h0):
                split(u0 + 2)
                split(u0 + 3)
                hidden(h0, u0 + 1, gated)
                hidden_lo(h0)

                def group(u, h, it=None):
                    split(u + 2, it, 3)
                    split(u + 3, it, 3)
                    hidden(h, u + 1, gated, it, 1, 3)
                    split(u + 4, it, 3)
                    hidden_lo(h, it, 1)

                last = u0 + 3 * G2 == N_UNITS
                with dve.Fori(0, G2 - 1 - last) as it:
                    group(u0 + 2, h0 + 1, it)
                if last:
                    group(u0 + 3 * G2 - 4, h0 + G2 - 1)
                split(u0 + 3 * G2 + 1)

            def xs_evac(dve, j):
                dve.wait_ge(xsT_done, j + 1)
                dve.tensor_copy(xs[:, :, j * U:j * U + U], acc[:, 2 + j % 2, :].rearrange("p (t n) -> p t n", t=TT)) \
                    .then_inc(xs_ready, 1)

            dve.memset(lnb[:, 0:1], LN_EPS)
            dve.memset(lnb[:, 1:2], EPS2)
            dve.memset(zeros[:, :], 0.0)
            dve.memset(sink[:, AQ:16], NEG).then_inc(fixed_ready, 1)
            turn("x")
            split(0)
            split(1)
            def na_bias_make(h):
                dve.wait_ge(bias_flipped, h + 1)
                dve.tensor_tensor(na_bias[:, h, :, :].rearrange("p a n -> p (a n)"), acc[:, h % 2, :],
                                  att_const("mask_na"), ALU.add).then_inc(bias_ready, 1)

            def rope_sum(dst, plain, turned_ps, width):
                c = width // T
                cos = att_const("cos").unsqueeze(1).broadcast_to([P, c, T])
                sin = att_const("sin").unsqueeze(1).broadcast_to([P, c, T])
                a, b = r_tmp[:, 0, 0:width], r_tmp[:, 1, 0:width]
                v = lambda z: z.rearrange("p (c t) -> p c t", c=c)
                dve.tensor_tensor(v(a), v(turned_ps), sin, ALU.mult)
                link(dve.tensor_tensor(v(b), v(plain), cos, ALU.mult))
                return dve.tensor_tensor(dst, v(a), v(b), ALU.add)

            dve.wait_ge(const_in, 16)
            for n in range(A_UNITS):
                split(U_ATT + n + 2)
                if 5 <= n < 9:
                    na_bias_make(2 * n - 10)
                    na_bias_make(2 * n - 9)
                if n in (1, 2):
                    i = n - 1
                    dve.wait_ge(rot_done, i + 1)
                    link(rope_sum(QT[:, 2 * i:2 * i + 2, :], q_raw[:, i, :], acc[:, i, :], 2 * T))
                if n == 3:
                    dve.wait_ge(rot_done, 3)
                    for j in range(AKV):
                        ins = rope_sum(KT[:, j:j + 1, :], acc[:, 2 + j, 0:T], acc[:, 2 + j, T:2 * T], T)
                        if j == 0:
                            link(ins)
                    ins.then_inc(rope_done, 1)
            for b in range(5):
                dve.wait_ge(par_turned, b + 1)
                dve.tensor_copy(pcol[:, b * P:b * P + ROW_BLOCKS[b]], acc[:, b % 4, 0:ROW_BLOCKS[b]]) \
                    .then_inc(par_ready, 1)
            dve.wait_ge(small_in, 16)
            dve.wait_ge(bias_ready, BH)
            dve.wait_ge(fixed_ready, 1)
            for s in range(AQ + BH + 4):
                h = s
                if h < AQ + BH:
                    dve.wait_ge(score_done, h + 1)
                    if h >= 4:
                        dve.wait_ge(pT_done, h - 3)
                    p = prob[:, h % 4, :, :]
                    mask = att_const("mask_a") if h < AQ else na_bias[:, h - AQ, :, :].rearrange("p a n -> p (a n)")
                    dve.scalar_tensor_tensor(out=p.rearrange("p a n -> p (a n)"), in0=pg[:, h % 2, :], scalar=SCALE,
                                             in1=mask, op0=ALU.mult, op1=ALU.add).then_inc(score_taken, 1)
                    dve.wait_ge(score_taken, h + 1)
                    link(dve.tensor_reduce(mx[:, h, :], p, AX.X, ALU.max))
                    dve.tensor_scalar(nmx[:, h, :], mx[:, h, :], sink[:, h:h + 1], -1.0, ALU.max, ALU.mult) \
                        .then_inc(max_ready, 1)
                h = s - 2
                if 0 <= h < AQ + BH:
                    dve.wait_ge(exp_done, h + 1)
                    link(dve.tensor_tensor(pden[:, h, :], psm[:, h, :], pes[:, h, :], ALU.add))
                    link(dve.reciprocal(pden[:, h, :], pden[:, h, :]))
                    for qt in range(TT):
                        ins = dve.tensor_scalar(prob[:, h % 4, qt, :], prob[:, h % 4, qt, :], pden[:, h, qt:qt + 1],
                                                None, ALU.mult)
                    ins.then_inc(p_ready, 1)
                if s >= 5 and s % 2 == 1:
                    c = (s - 5) // 2
                    dve.wait_ge(ot_hi, c + 1)
                    dve.tensor_tensor(op_lo[:, 8 + c, :], acc[:, c % 4, 0:T], op_hi[:, 8 + c, :].bitcast(F32),
                                      ALU.subtract).then_inc(ot_ready, 1)
            for n in range(OUT_UNITS):
                split(U_ATT_OUT + n + 2)
            ln(U_MLP[0] - 1, 1, normalise)
            turn("ln1_0")
            mlp(U_MLP[0], HG_MLP[0])
            ln(U_SSM - 1, 2, normalise)
            turn("ln2_0")

            dve.memset(one_col, 1.0)
            dve.memset(conv_in[:, :, :, 0:2], 0.0)
            link(dve.memset(conv_in[:, :, :, 2 + T:], 0.0))
            i = 0
            for n in range(len(SSM_COLS)):
                split(U_SSM + n + 2)
                if n == DT_AT:
                    dve.wait_ge(unit_done, U_SSM + n + 1)
                    dve.wait_ge(small_in, 64)
                    dve.tensor_tensor(dt_v, pg[:, n % 4, 0:128].rearrange("p (t n) -> p t n", t=TT),
                                      dt_bias.unsqueeze(1).broadcast_to([P, TT, 64]), ALU.add).then_inc(dt_sum, 1)
                    dve.wait_ge(dt_soft, 2)
                    dve.scalar_tensor_tensor(out=dt_tok, in0=dt_v, scalar=0.0, in1=dt_a, op0=ALU.max,
                                             op1=ALU.add).then_inc(dt_ready, 1)
                    continue
                if n == DT_AT + 2:
                    dve.wait_ge(dtT_done, 1)
                    link(dve.tensor_scalar(aT[0:64, :], acc[0:64, 0, 0:T], a_col[0:64, :], -1.0, ALU.mult, ALU.mult))
                    link(dve.tensor_tensor_scan(gT[0:64, :], one_col[0:64, :].broadcast_to([64, T]), aT[0:64, :], 0.0, ALU.mult, ALU.add))
                    link(dve.tensor_tensor(gT[32:64, :], aT[32:64, :], gT[32:64, :], ALU.subtract))
                    link(dve.tensor_copy(g_pair[0:64, :], gT[0:64, :]))
                    link(dve.tensor_tensor(gT[0:64, :], gT[0:64, :], g_pair[0:64, :].bitcast(F32), ALU.subtract))
                    dve.tensor_copy(g_pair[64:128, :], gT[0:64, :]).then_inc(g_ready, 1)
                if n < len(SSM_COLS) - Z_UNITS:
                    dve.wait_ge(conv_evac, i + 1)
                    if i >= 2:
                        dve.wait_ge(conv_silu, i - 1)
                    for k in range(CONV):
                        for c in range(2):
                            wc = COL["ssm_conv_w"] + 32 * k + (16 + 2 * i + c) % 32
                            src = conv_in[:, i % 2, c, k:k + T]
                            dst = conv_sum[:, i % 2, c, :]
                            if k == 0:
                                ins = dve.tensor_scalar(dst, src, pcol[:, wc:wc + 1], None, ALU.mult)
                            else:
                                ins = dve.scalar_tensor_tensor(out=dst, in0=src, scalar=pcol[:, wc:wc + 1], in1=dst,
                                                               op0=ALU.mult, op1=ALU.add)
                        if k < CONV - 1:
                            link(ins)
                    ins.then_inc(conv_done, 1)
                    i += 1
                    if i >= 11:
                        xs_evac(dve, i - 11)
                elif i == 16:
                    xs_evac(dve, 6)
                    xs_evac(dve, 7)
                    i += 1
            dve.wait_ge(const_in, 32)

            def cb_make(g):
                dve.wait_ge(cb_done, g + 1)
                src = acc[:, 2 + g % 2, :]
                for a, z, o in ((0, 256, 0), (384, 512, 256), (0, 128, 384), (256, 512, 512)):
                    ins = dve.tensor_copy(CB[:, g % 2, o:o + z - a], src[:, a:z])
                ins.then_inc(cb_ready, 1)
                dve.wait_ge(cb_ready, g + 1)

            def y_make(g):
                dve.wait_ge(head_done, GH * (g + 1))
                dve.wait_ge(xdt_ready, g + 1)
                yg = xs[:, :, g * U:g * U + U]
                link(dve.tensor_tensor(yg, acc[:, g % 2, :].rearrange("p (t n) -> p t n", t=TT), xD[g % 2],
                                       ALU.add))
                dve.wait_ge(z_ready, Z_UNITS)
                dve.tensor_tensor(yg, yg, silz[:, :, g * U:g * U + U], ALU.mult).then_inc(y_gated, 1)

            for h in range(SH):
                g, b = h // GH, h % 2
                if h % GH == 0:
                    cb_make(g)
                dve.wait_ge(e_ready, h + 1)
                dve.tensor_tensor(E[:, b, :], E[:, b, :], CB[:, g % 2, :], ALU.mult).then_inc(m_ready, 1)
                if h % GH == 0 and g:
                    y_make(g - 1)
            y_make(SG - 1)
            dve.wait_ge(y_std, 1)
            link(dve.reciprocal(yrs, yrs))
            for t in range(TT):
                for g in range(SG):
                    ins = dve.tensor_scalar(xs[:, t, g * U:g * U + U], xs[:, t, g * U:g * U + U],
                                            yrs[:, t, g:g + 1], None, ALU.mult)
                ins.then_inc(norm_ready, 1)
            turn("y", COL["ssm_norm"])
            for n in range(DI // U):
                split(U_SSM_OUT + n + 2)
            ln(U_MLP[1] - 1, 3, normalise)
            turn("ln1_1")
            dve.wait_ge(lam_in, 80)
            link(dve.tensor_tensor(lam_q, lam_q, lam_k, ALU.mult))
            dve.tensor_reduce(lam_s, lam_q, AX.X, ALU.add).then_inc(lam_sum, 1)
            dve.wait_ge(rel_sum, 1)
            dve.tensor_copy(rvec[0:DH, :], pg[0:DH, 3, 0:384]).then_inc(rel_row, 1)
            dve.memset(ones_m, 1.0)
            dve.memset(uu[:, :, 0:CK - 1], 0.0)
            dve.wait_ge(lam_exp, 1)
            for l in range(DEPTH):
                link(dve.tensor_tensor(nlam[:, l:l + 1], lam_e[:, 2 + l:3 + l], lam_e[:, l:l + 1], ALU.subtract))
                link(dve.tensor_scalar(nlam[:, l:l + 1], nlam[:, l:l + 1], -lambda_init(l), None, ALU.add))
                link(dve.tensor_scalar(sub_g[:, l:l + 1], pcol[:, COL["subln"] + l:COL["subln"] + l + 1],
                                       1.0 - lambda_init(l), None, ALU.mult))
            mlp(U_MLP[1], HG_MLP[1])
            ln(U_SECOND - 1, 4, settle)
            for t in range(TT):
                rms(5, t)

            for l in range(DEPTH):
                turn(f"ffn1_{l}", COL["ffn1"] + 8 * l)
                swiglu(U_FFN[2 * l], HG_FFN[2 * l])
                residual(U_MIX[l] - 1, 5 + 3 * l, 0.5)
                turn(f"mix_{l}", COL["mix"] + 8 * l)

                def gated_columns(n):
                    dve.wait_ge(unit_done, U_MIX[l] + n + 1)
                    dve.wait_ge(gate_ready, 2 * l + (n + 1) // 2)
                    dve.tensor_tensor(uu[:, n - 1:n + 1, CK - 1:],
                                      pg[:, n % 4, :].rearrange("p (c t) -> p c t", c=2), gate, ALU.mult) \
                        .then_inc(u_ready, 2)
                    dve.wait_ge(u_ready, 4 * l + n + 1)

                def convolve(c0, k0, k1):
                    for k in range(k0, k1):
                        for c in (c0, c0 + 1):
                            wc = COL["conv_w"] + l * P + 4 * k + c
                            w = pcol[:, wc:wc + 1]
                            if k == 0:
                                bc = COL["conv_b"] + 4 * l + c
                                ins = dve.tensor_scalar(cacc[:, c, :], uu[:, c, 0:T], w, pcol[:, bc:bc + 1],
                                                        ALU.mult, ALU.add)
                            else:
                                ins = dve.scalar_tensor_tensor(out=cacc[:, c, :], in0=uu[:, c, k:k + T], scalar=w,
                                                               in1=cacc[:, c, :], op0=ALU.mult, op1=ALU.add)
                        link(ins)

                def head_norm(n):
                    i = 4 * l + n - 4
                    dve.wait_ge(qk_std, i + 1)
                    link(dve.reciprocal(sdev[:, i % 2, :], sdev[:, i % 2, :]))
                    gc = (COL["q_norm"] if n < 6 else COL["k_norm"]) + l
                    c = 2 * (n % 2)
                    dst = (Q2 if n < 6 else K2)[:, c:c + 2, :]
                    dve.scalar_tensor_tensor(out=dst, in0=pg[:, n % 4, :].rearrange("p (c t) -> p c t", c=2),
                                             scalar=pcol[:, gc:gc + 1],
                                             in1=sdev[:, i % 2, :].rearrange("p (c t) -> p c t", c=2),
                                             op0=ALU.mult, op1=ALU.mult).then_inc(qk_ready, 1)

                gated_columns(1)
                convolve(0, 0, CK)
                gated_columns(3)
                head_norm(4)
                head_norm(5)
                convolve(2, 0, 10)
                head_norm(6)
                convolve(2, 10, 18)
                head_norm(7)
                convolve(2, 18, CK)
                dve.engine_nop().then_inc(cconv, 1)
                for s in range(2 * DH + 2):
                    i = 8 * l + s
                    if s < 2 * DH:
                        h = s // 2
                        dve.wait_ge(sc2_done, i + 1)
                        b = s % 4
                        dve.scalar_tensor_tensor(out=prob2[:, b, :], in0=pg[:, s % 2, 0:384], scalar=SCALE,
                                                 in1=rbias[:, h, :], op0=ALU.mult, op1=ALU.add) \
                            .then_inc(sc2_taken, 1)
                        dve.wait_ge(sc2_taken, i + 1)
                        dve.tensor_reduce(m2[:, s, 0:1], prob2[:, b, 0:P], AX.X, ALU.max)
                        link(dve.tensor_reduce(m2[:, s, 1:2], prob2[:, b, P:384], AX.X, ALU.max))
                        dve.tensor_scalar(n2[:, s, :], m2[:, s, :], -1.0, None, ALU.mult).then_inc(mx2_ready, 1)
                    if s >= 3 and s % 2 == 1:
                        h = (s - 3) // 2
                        k = DH * l + h
                        dve.wait_ge(ex2_done, 8 * l + 2 * h + 2)
                        link(dve.reciprocal(r2[:, 2 * h:2 * h + 2, :], s2[:, 2 * h:2 * h + 2, :]))
                        link(dve.tensor_scalar(r2[:, 2 * h + 1, :], r2[:, 2 * h + 1, :], nlam[:, l:l + 1], None,
                                               ALU.mult))
                        if k >= 2:
                            dve.wait_ge(mixT_done, k - 1)
                        b0, b1 = (2 * h) % 4, (2 * h + 1) % 4
                        for a, z, qt in ((0, P, 0), (P, 384, 1)):
                            ins = dve.tensor_scalar(pmix[:, k % 2, a:z], prob2[:, b0, a:z],
                                                    r2[:, 2 * h, qt:qt + 1], None, ALU.mult)
                        link(ins)
                        for a, z, qt in ((0, P, 0), (P, 384, 1)):
                            ins = dve.scalar_tensor_tensor(out=pmix[:, k % 2, a:z], in0=prob2[:, b1, a:z],
                                                           scalar=r2[:, 2 * h + 1, qt:qt + 1],
                                                           in1=pmix[:, k % 2, a:z], op0=ALU.mult, op1=ALU.add)
                        ins.then_inc(mix_ready, 1)
                dve.wait_ge(osq_std, l + 1)
                link(dve.reciprocal(odev, odev))
                flat = lambda z: z.rearrange("p a n -> p (a n)")
                dve.scalar_tensor_tensor(out=flat(O2), in0=flat(O2), scalar=sub_g[:, l:l + 1], in1=flat(odev),
                                         op0=ALU.mult, op1=ALU.mult).then_inc(o2_norm, 1)
                dve.wait_ge(o2_hi, l + 1)
                dve.tensor_tensor(op_lo[:, 12:16, :], O2, op_hi[:, 12:16, :].bitcast(F32), ALU.subtract) \
                    .then_inc(o2_ready, 1)
                dve.wait_ge(cstd, l + 1)
                link(dve.reciprocal(odev[:, 0, :], odev[:, 0, :]))
                dve.tensor_tensor(osq, cacc, odev[:, 0:1, :].broadcast_to([P, 4, T]), ALU.mult).then_inc(cnorm, 1)
                dve.wait_ge(c_hi, l + 1)
                dve.tensor_tensor(op_lo[:, 8:12, :], c32, op_hi[:, 8:12, :].bitcast(F32), ALU.subtract) \
                    .then_inc(c_ready, 1)
                for n in range(OUT_UNITS):
                    split(U_MIX_OUT[l] + n + 2)
                residual(U_FFN[2 * l + 1] - 1, 6 + 3 * l, 1.0)
                turn(f"ffn2_{l}", COL["ffn2"] + 8 * l)
                swiglu(U_FFN[2 * l + 1], HG_FFN[2 * l + 1])
                residual((U_FFN + [N_UNITS])[2 * l + 2] - 1, 7 + 3 * l, 0.5, norm=l < DEPTH - 1)

        @block.tensor
        def _(pe):
            def take(u, it=None, per=0):
                pe.wait_ge(lo_ready, at(u + 1, it, per))

            def three(psum, w, x, first, last, swap=False):
                terms = ((0, 0), (1, 0), (0, 1))
                for i, (a, b) in enumerate(terms):
                    l, r = (x[b], w[a]) if swap else (w[a], x[b])
                    ins = pe.matmul(psum, l, r, start=first and i == 0, stop=last and i == 2)
                return ins

            def wslice(u, a, z):
                s = u % RING
                return w_hi[:, s, a:z], w_lo[:, s, a:z]

            def feature_chunk(u, bank, c, step=U, fresh=None):
                for k in range(KC):
                    if fresh and c == 0 and k and k % 2 == 0:
                        pe.wait_ge(xt_ready, TURN_BANK[fresh] + k // 2 + 1)
                    o = k * step + c * P
                    ins = three(bank, wslice(u, o, o + P), (op_hi[:, k, :], op_lo[:, k, :]), k == 0, k == KC - 1)
                return ins

            def token_tile(u, bank, t, c0, width, step=U):
                for k in range(KC):
                    o = k * step + c0
                    ts = slice(t * P, t * P + P)
                    ins = three(bank, wslice(u, o, o + width), (op_hi[:, k, ts], op_lo[:, k, ts]), k == 0,
                                k == KC - 1, swap=True)
                return ins

            def project(u, bank, tokens=False, it=None, per=0, fresh=None):
                take(u, it, per)
                if fresh:
                    pe.wait_ge(xt_ready, TURN_BANK[fresh] + 1)
                for c in range(2):
                    o = bank[:, c * T:(c + 1) * T]
                    ins = token_tile(u, o, c, 0, U) if tokens else feature_chunk(u, o, c, fresh=fresh)
                ins.then_inc(unit_done, 1)

            def output(u, chunk, first, last, it=None, per=0):
                take(u, it, per)

                def add(k, t, h):
                    ts = slice(t * P, t * P + P)
                    o = k * D + h * 512
                    return three(acc[:, 2 * t + h, :], wslice(u, o, o + 512),
                                 (op_hi[:, chunk + k, ts], op_lo[:, chunk + k, ts]),
                                 first and k == 0, last and k == 1, swap=True)

                if not last:
                    for k in range(2):
                        for t in range(TT):
                            for h in range(2):
                                ins = add(k, t, h)
                else:
                    for q in range(4):
                        for k in range(2):
                            ins = add(k, q // 2, q % 2)
                        if q < 3:
                            ins.then_inc(sum_done, 1)
                ins.then_inc(unit_done, 1)

            def turn_chunk(src, j, t):
                o = pg[:, j // 2 % 4, (j % 2) * T + t * P:(j % 2) * T + t * P + P]
                if src is None:
                    return pe.matmul(o, X[:, t, j * P:(j + 1) * P], diag[:, t, :], start=True, stop=True)
                return pe.transpose(o, src[:, t, j * P:(j + 1) * P], ident[:, :])

            def turn(name, src):
                n = TURNS.index(name)
                ready = NORM_AT[name]
                if name == "x":
                    pe.wait_ge(ident_in, 16)
                for t in range(TT):
                    if name == "x":
                        pe.wait_ge(x_in[t], 16)
                    elif t == 0 or NORM_PARTS[n] == 2:
                        pe.wait_ge(norm_ready, ready + t + 1)
                    for j in range(KC):
                        if NORM_PARTS[n] > 2 and t == 1 and j % 2 == 0:
                            pe.wait_ge(norm_ready, ready + 2 + j // 2)
                        ins = turn_chunk(src, j, t)
                        if t == 1 and j % 2 == 1:
                            ins.then_inc(turned, 1)

            def turn_y():
                pe.wait_ge(norm_ready, NORM_AT["y"] + 2)
                for b in range(DI // P // 2):
                    if b >= 4:
                        pe.wait_ge(xt_ready, TURN_BANK["y"] + b - 3)
                    for c in range(2):
                        for t in range(TT):
                            ins = turn_chunk(xs, 2 * b + c, t)
                    ins.then_inc(turned, 1)

            def mlp(u0, h0, fresh):
                project(u0, pg[:, 0, :], fresh=fresh)
                with pe.Fori(0, (G1 - 1) // 3) as it:
                    for j in range(3):
                        project(u0 + 1 + 2 * j, pg[:, (1 + j) % 3, :], False, it, 6)
                        pe.wait_ge(h_ready, at(h0 + j + 1, it, 3))
                        output(u0 + 2 + 2 * j, 8, False, False, it, 6)
                pe.wait_ge(h_ready, h0 + G1)
                output(u0 + 2 * G1 - 1, 8, False, True)

            def swiglu(u0, h0, fresh):
                project(u0, pg[:, 0, :], fresh=fresh)
                project(u0 + 1, pg[:, 1, :])
                with pe.Fori(0, G2 - 1) as it:
                    pe.wait_ge(act_done, at(h0 + 1, it, 1))
                    project(u0 + 2, pg[:, 0, :], False, it, 3)
                    pe.wait_ge(h32_ready, at(h0 + 1, it, 1))
                    project(u0 + 3, pg[:, 1, :], False, it, 3)
                    pe.wait_ge(h_ready, at(h0 + 1, it, 1))
                    output(u0 + 4, 8, False, False, it, 3)
                pe.wait_ge(h_ready, h0 + G2)
                output(u0 + 3 * G2 - 1, 8, False, True)

            def clear_sums():
                for b in range(4):
                    pe.matmul(acc[:, b, :], zeros[:, 0:P], zeros[:, :], start=True, stop=False)

            def qk_sums(pe, i):
                pe.wait_ge(qk_sq, i + 1)
                if i >= 2:
                    pe.wait_ge(qk_std, i - 1)
                pe.matmul(acc[:, i % 2, :], blk_const("halves"), sq[:, i % 2, :], start=True, stop=True) \
                    .then_inc(qk_sum, 1)

            def o2(pe, l, h):
                k = DH * l + h
                pe.wait_ge(mixT_ready, k + 1)
                if k >= 2:
                    pe.wait_ge(o2_evac, k - 1)
                pe.matmul(acc[:, h % 2, 0:T], V2[:, 0, h * P:h * P + P], pmixT[:, k % 2, 0:T], start=True, stop=False)
                pe.matmul(acc[:, h % 2, P:T], V2[:, 1, h * P:h * P + P], pmixT[:, k % 2, T:384], start=False,
                          stop=True).then_inc(o2_done, 1)

            turn("x", X)
            pe.wait_ge(const_in, 16)
            for n in range(A_UNITS):
                u = U_ATT + n
                if n >= 4:
                    pe.wait_ge(attn_evac, n - 3)
                bank = pg[:, n % 4, :]
                if n == 2:
                    take(u)
                    feature_chunk(u, bank[:, 0:T], 0)
                    for t in range(TT):
                        ins = token_tile(u, bank[:, T + t * P:T + t * P + P], t, P, P)
                    ins.then_inc(unit_done, 1)
                else:
                    project(u, bank, tokens=n >= 7, fresh="x" if n == 0 else None)
                if n in (1, 2):
                    i = n - 1
                    pe.wait_ge(attn_evac, i + 1)
                    pe.matmul(acc[:, i, :], att_const("rot"), q_raw[:, i, :], start=True, stop=True) \
                        .then_inc(rot_done, 1)
                if 4 <= n < 8:
                    if n == 4:
                        pe.wait_ge(bias_in, 16 * BH * 4)
                        pe.wait_ge(rope_done, 1)
                    for h in (2 * n - 8, 2 * n - 7):
                        if h >= 2:
                            pe.wait_ge(bias_ready, h - 1)
                        pe.matmul(acc[:, h % 2, :], att_const("na_flip"),
                                  na_bias[:, h, :, :].rearrange("p a n -> p (a n)"), start=True, stop=True) \
                            .then_inc(bias_flipped, 1)
                if n == 8:
                    pe.wait_ge(par_in, 16 * N_PAR)
                    pe.wait_ge(bias_ready, BH)
                    for b in range(5):
                        r = ROW_BLOCKS[b]
                        if b >= 4:
                            pe.wait_ge(par_ready, b - 3)
                        pe.transpose(acc[:, b % 4, 0:r], prow[0:r, b, :], ident[0:r, 0:r]).then_inc(par_turned, 1)
                if n == 3:
                    pe.wait_ge(attn_evac, 3)
                    for j in range(AKV):
                        pe.matmul(acc[:, 2 + j, 0:T], att_const(f"dup{j}"), k_raw, start=True, stop=True)
                        ins = pe.matmul(acc[:, 2 + j, T:2 * T], att_const(f"rdup{j}"), k_raw, start=True, stop=True)
                    ins.then_inc(rot_done, 1)
            pe.wait_ge(par_ready, 5)
            pe.wait_ge(attn_evac, A_UNITS)
            for s in range(AQ + BH + 3):
                h = s
                if h < AQ + BH:
                    if h >= 2:
                        pe.wait_ge(score_taken, h - 1)
                    p0 = (h % 2) * HD
                    ki = h // 4 if h < AQ else 2 + (h - AQ) // 2
                    for qt in range(TT):
                        ins = pe.matmul(pg[:, h % 2, qt * T:(qt + 1) * T],
                                        QT[p0:p0 + HD, h // 2, qt * P:qt * P + P], KT[p0:p0 + HD, ki, :],
                                        start=True, stop=True)
                    ins.then_inc(score_done, 1)
                h = s - 2
                if 0 <= h < AQ + BH:
                    pe.wait_ge(p_ready, h + 1)
                    if h >= 2:
                        pe.wait_ge(pt_ready, h - 1)
                    for kt in range(TT):
                        for qt in range(TT):
                            ins = pe.transpose(pg[:, 2 + h % 2, kt * T + qt * P:kt * T + qt * P + P],
                                               prob[:, h % 4, qt, kt * P:kt * P + P], ident[:, :])
                    ins.then_inc(pT_done, 1)
                h = s - 3
                if 0 <= h < AQ + BH:
                    pe.wait_ge(pt_ready, h + 1)
                    c = h // 2
                    if c >= 4 and h % 2 == 0:
                        pe.wait_ge(ot_ready, c - 3)
                    p0 = (h % 2) * HD
                    for kt in range(TT):
                        v = va[:, kt, (h // 4) * HD:(h // 4 + 1) * HD] if h < AQ \
                            else vb[:, kt, (h - AQ) * HD:(h - AQ + 1) * HD]
                        ins = pe.matmul(acc[p0:p0 + HD, c % 4, 0:T], v, probT[:, h % 2, kt, :], start=kt == 0,
                                        stop=kt == TT - 1)
                    ins.then_inc(pv_done, 1)
            pe.wait_ge(ot_ready, 8)
            for n in range(OUT_UNITS):
                output(U_ATT_OUT + n, 8 + 2 * n, n == 0, n == OUT_UNITS - 1)
            turn("ln1_0", xn)
            clear_sums()
            mlp(U_MLP[0], HG_MLP[0], "ln1_0")
            turn("ln2_0", xn)

            i = 0
            for n in range(len(SSM_COLS)):
                u = U_SSM + n
                bank = pg[:, n % 4, :]
                if n >= 4:
                    m = n - 4
                    if m < DT_AT:
                        pe.wait_ge(conv_evac, m + 1)
                    elif m == DT_AT:
                        pe.wait_ge(dt_sum, 1)
                    elif m < 17:
                        pe.wait_ge(conv_evac, m)
                    else:
                        pe.wait_ge(z_ready, m - 16)
                if n == DT_AT:
                    take(u)
                    for t in range(TT):
                        ins = token_tile(u, bank[:, t * 64:t * 64 + 64], t, 0, 64, step=64)
                    ins.then_inc(unit_done, 1)
                    continue
                project(u, bank, tokens=n >= 17, fresh="ln2_0" if n == 0 else None)
                if n == DT_AT + 1:
                    pe.wait_ge(dt_ready, 1)
                    for t in range(TT):
                        ins = pe.transpose(acc[0:64, 0, t * P:t * P + P], dt_tok[:, t, :], ident[:, :])
                    ins.then_inc(dtT_done, 1)
                if n >= 11 and n < 19:
                    j = n - 11
                    pe.wait_ge(conv_silu, j + 9)
                    if j >= 2:
                        pe.wait_ge(xs_ready, j - 1)
                    for t in range(TT):
                        for c in range(2):
                            ins = pe.transpose(acc[:, 2 + j % 2, t * U + c * P:t * U + c * P + P],
                                               xsT[:, j % 2, c, t * P:t * P + P], ident[:, :])
                    ins.then_inc(xsT_done, 1)

            def cb(g):
                if g >= 2:
                    pe.wait_ge(cb_ready, g - 1)
                for st in range(TT):
                    ins = pe.matmul(acc[:, 2 + g % 2, st * T:(st + 1) * T], BT[:, g, st * P:st * P + P], CT[:, g, :],
                                    start=True, stop=True)
                ins.then_inc(cb_done, 1)

            def diff(h):
                b = h % 2
                if h >= 2:
                    pe.wait_ge(e_ready, h - 1)
                o = pg[:, 2 * b:2 * b + 2, :].rearrange("p a n -> p (a n)")
                for at_, w, r, st, l0, d0 in ((0, 256, h, 0, 0, 0), (256, 128, h, 1, 128, 256),
                                              (384, 128, SH + h, 0, 0, 384), (512, 256, SH + h, 1, 0, 640)):
                    pe.matmul(o[:, at_:at_ + w], select[:, r:r + 1].broadcast_to([P, P]), g_pair[:, l0:l0 + w],
                              start=True, stop=False)
                    pe.matmul(o[:, at_:at_ + w], g_pair[:, st * P:st * P + P],
                                    nselect[:, r:r + 1].broadcast_to([P, w]), start=False, stop=False)
                    ins = pe.matmul(o[:, d0:d0 + P], ident_r[:, :], neg_tri[:, r // SH, :], start=False, stop=True)
                ins.then_inc(diff_done, 1)

            def y(h):
                g, b = h // GH, h % 2
                e0 = (h % GH) * HD
                pe.wait_ge(m_ready, h + 1)
                if h % GH == 0:
                    pe.wait_ge(xdt_ready, g + 1)
                    if g >= 2:
                        pe.wait_ge(y_gated, g - 1)
                x4 = lambda d, t: xdt[:, (g % 2) * 4 + d * 2 + t, e0:e0 + HD]
                terms = [[(0, 0, 0), (384, 1, 0), (512, 1, 1)], [(128, 0, 0), (256, 0, 1), (640, 1, 1)]]
                for lt in range(TT):
                    for i_, (o, d, st) in enumerate(terms[lt]):
                        ins = pe.matmul(acc[:, g % 2, lt * U + e0:lt * U + e0 + HD], E[:, b, o:o + P], x4(d, st),
                                        start=i_ == 0, stop=i_ == 2)
                ins.then_inc(head_done, 1)

            pe.wait_ge(z_ready, Z_UNITS)
            pe.wait_ge(xs_ready, 8)
            pe.wait_ge(g_ready, 1)
            pe.wait_ge(sel_ready, 1)
            cb(0)
            diff(0)
            for h in range(SH):
                if h + 1 < SH:
                    if (h + 1) % GH == 0:
                        cb((h + 1) // GH)
                    diff(h + 1)
                y(h)
            turn_y()
            for n in range(DI // U):
                pe.wait_ge(xt_ready, TURN_BANK["y"] + n + 1)
                output(U_SSM_OUT + n, 2 * n, n == 0, n == DI // U - 1)
            turn("ln1_1", xn)
            pe.wait_ge(lam_in, 80)
            pe.wait_ge(const_in, CONST_BLK)
            pe.wait_ge(xt_ready, TURN_BANK["ln1_1"] + KC // 2)
            pe.matmul(pg[0:DH, 3, 0:384], rel[0:BUCKETS, :], blk_const("buckets")[0:BUCKETS, :], start=True,
                      stop=True).then_inc(rel_sum, 1)
            clear_sums()
            mlp(U_MLP[1], HG_MLP[1], "ln1_1")

            pe.wait_ge(bias_in, 16 * (BH * 4 + DH * 2))
            for h in range(DH):
                pe.matmul(pg[:, h, 0:384], blk_const("flip"), rbias[:, h, :], start=True, stop=True) \
                    .then_inc(bias_flipped, 1)
            pe.wait_ge(bias_evac, DH)
            for l in range(DEPTH):
                turn(f"ffn1_{l}", None)
                clear_sums()
                swiglu(U_FFN[2 * l], HG_FFN[2 * l], f"ffn1_{l}")
                turn(f"mix_{l}", None)
                for n in range(len(MIX_COLS)):
                    u = U_MIX[l] + n
                    m = n - 4
                    if m in (0, 1):
                        pe.wait_ge(u_ready, 4 * l + 2)
                    elif m in (2, 3):
                        pe.wait_ge(u_ready, 4 * l + 4)
                    elif m >= 4:
                        pe.wait_ge(qk_ready, 4 * l + m - 3)
                    project(u, pg[:, n % 4, :], tokens=n >= 8, fresh=f"mix_{l}" if n == 0 else None)
                    if 5 <= n < 9:
                        qk_sums(pe, 4 * l + n - 5)
                pe.wait_ge(qk_ready, 4 * l + 4)
                pe.wait_ge(v_ready, 2 * l + 2)
                for s in range(2 * DH + 4):
                    i = 8 * l + s
                    if s < 2 * DH:
                        h, m = s // 2, s % 2
                        if s >= 2:
                            pe.wait_ge(sc2_taken, i - 1)
                        p0 = m * HD
                        pe.matmul(pg[:, s % 2, 0:P], Q2[p0:p0 + HD, h, 0:P], K2[p0:p0 + HD, h, 0:P], start=True,
                                  stop=True)
                        pe.matmul(pg[:, s % 2, P:384], Q2[p0:p0 + HD, h, P:T], K2[p0:p0 + HD, h, :], start=True,
                                  stop=True).then_inc(sc2_done, 1)
                    if s >= 4 and s % 2 == 0 and s < 2 * DH + 4:
                        k = DH * l + (s - 4) // 2
                        pe.wait_ge(mix_ready, k + 1)
                        if k >= 2:
                            pe.wait_ge(mixT_ready, k - 1)
                        for o, a in ((0, 0), (P, P), (2 * P, 2 * P)):
                            ins = pe.transpose(pg[:, 2 + k % 2, o:o + P], pmix[:, k % 2, a:a + P], ident[:, :])
                        ins.then_inc(mixT_done, 1)
                    if s >= 5 and s % 2 == 1:
                        o2(pe, l, (s - 5) // 2)
                pe.wait_ge(o2_evac, DH * l + DH)
                for a in range(2):
                    ins = pe.matmul(acc[:, 2 + a, :], ones_m, osq[:, 2 * a:2 * a + 2, :].rearrange("p a n -> p (a n)"),
                                    start=True, stop=True)
                ins.then_inc(osq_sum, 1)
                pe.wait_ge(o2_ready, l + 1)
                for n in range(OUT_UNITS):
                    if n == 2:
                        pe.wait_ge(csq, l + 1)
                        for c in range(4):
                            ins = pe.matmul(pg[:, 0, 0:T], ones_m, osq[:, c, :], start=c == 0, stop=c == 3)
                        ins.then_inc(csum, 1)
                        pe.wait_ge(c_ready, l + 1)
                    output(U_MIX_OUT[l] + n, 8 + 2 * ((n + 2) % 4), n == 0, n == OUT_UNITS - 1)
                turn(f"ffn2_{l}", None)
                clear_sums()
                swiglu(U_FFN[2 * l + 1], HG_FFN[2 * l + 1], f"ffn2_{l}")

_INS = ['x', 'attn_w_in', 'attn_sink', 'attn_rpb', 'attn_w_out', 'ssm_w_in', 'ssm_conv_w', 'ssm_conv_b',
        'ssm_dt_bias', 'ssm_A_log', 'ssm_D', 'ssm_norm_w', 'ssm_w_out', 'mlp_w1', 'mlp_w2', 'ln1_g', 'ln1_b',
        'ln2_g', 'ln2_b', 'rel_bias_2', 'ffn1_norm_2', 'ffn1_w_gate_2', 'ffn1_w_up_2', 'ffn1_w_down_2',
        'mix_norm_2', 'w_in_2', 'conv_w_2', 'conv_b_2', 'conv_norm_2', 'q_norm_2', 'k_norm_2', 'lambda_q1_2',
        'lambda_k1_2', 'lambda_q2_2', 'lambda_k2_2', 'subln_norm_2', 'w_out_2', 'ffn2_norm_2',
        'ffn2_w_gate_2', 'ffn2_w_up_2', 'ffn2_w_down_2']


def kernel(**inputs):
    import concourse.bacc as bacc
    from concourse.bass_utils import run_bass_kernel_spmd

    nc = bacc.Bacc("TRN2", target_bir_lowering=False, num_devices=1)
    arrays, args = {}, {}
    for name in _INS:
        a = np.ascontiguousarray(inputs[name])
        arrays["in_" + name] = a
        args[name] = nc.dram_tensor("in_" + name, a.shape, mybir.dt.from_np(a.dtype), kind="ExternalInput").ap()
    c = shape_constants()
    arrays["in_consts"] = c
    args["consts"] = nc.dram_tensor("in_consts", c.shape, F32, kind="ExternalInput").ap()
    out = nc.dram_tensor("out_x", (1, T, D), F32, kind="ExternalOutput").ap()
    two_blocks(nc, args, out)
    r = run_bass_kernel_spmd(nc, [arrays], core_ids=[0])
    return r.results[0]["out_x"]
```

```python
from contextlib import ExitStack
import math

import numpy as np

import concourse.bass as bass
from concourse import mybir

F32 = mybir.dt.float32
F32R = mybir.dt.float32r
ACT = mybir.ActivationFunctionType
ALU = mybir.AluOpType
AX = mybir.AxisListType

P = 128
T = 256
TT = T // P
D = 1024
KC = D // P
HD = 64
DEPTH = 2
ALPHA = float((2 * DEPTH) ** 0.25)
LN_EPS = 1e-5
NEG = -1e30
SCALE = HD ** -0.5

AQ, AKV, BH = 8, 2, 8
A_COLS = (AQ + 2 * AKV + 3 * BH) * HD
GRID_W, NA_KW, NA_KH = 64, 16, 8
WINDOW = 128
RPB_R, RPB_C = 2 * NA_KH - 1, 2 * NA_KW - 1
DI = 2 * D
SH = DI // HD
SG, SN = 8, 128
GH = SH // SG
CONV = 5
F1 = 4 * D
CCH = 512
CK = 31
DH = 4
F2 = 2816
BUCKETS = 32
EPS2 = 1e-6

U = 256
UN = KC * U
RING = 3

A_UNITS = A_COLS // U
Z_UNITS = DI // U
OUT_UNITS = D // U
SSM_COLS = [2 * DI + i * U for i in range(2)] + [2 * DI + 2 * SG * SN] + [2 * DI + i * U for i in range(2, 8)] \
    + [DI + i * U for i in range(Z_UNITS)] + [i * U for i in range(Z_UNITS)]
DT_AT = 2
G1, G2 = F1 // U, F2 // U
MIX_COLS = [2 * U, 0, 3 * U, U] + [2 * CCH + i * U for i in (0, 2, 1, 3, 4, 5)]
TAPS = [14,11,7,7,7,7,2,2,0,0]
POOL_TAPS = 10
assert 2 * sum(TAPS) + POOL_TAPS == 4 * CK
U_ATT = 0
U_ATT_OUT = U_ATT + A_UNITS
U_MLP = [U_ATT_OUT + OUT_UNITS, 0]
U_SSM = U_MLP[0] + 2 * G1
U_SSM_OUT = U_SSM + len(SSM_COLS)
U_MLP[1] = U_SSM_OUT + DI // U
U_SECOND = U_MLP[1] + 2 * G1
U_FFN, U_MIX, U_MIX_OUT = [], [], []
_u = U_SECOND
for _l in range(DEPTH):
    U_FFN.append(_u)
    U_MIX.append(_u + 3 * G2)
    U_MIX_OUT.append(U_MIX[-1] + len(MIX_COLS))
    U_FFN.append(U_MIX_OUT[-1] + OUT_UNITS)
    _u = U_FFN[-1] + 3 * G2
N_UNITS = _u
HG_MLP = [0, G1]
HG_FFN = [2 * G1 + i * G2 for i in range(2 * DEPTH)]

TURNS = ["x", "ln1_0", "ln2_0", "y", "ln1_1"] + [f"{s}_{l}" for l in range(DEPTH) for s in ("ffn1", "mix", "ffn2")]
TURN_CHUNKS = [DI // P if n == "y" else KC for n in TURNS]
TURN_BANK = {n: sum(TURN_CHUNKS[:i]) // 2 for i, n in enumerate(TURNS)}
NORM_PARTS = [0 if n == "x" else SG if n == "y" else 1 + KC // 2 if n.startswith("ln") else 2 for n in TURNS]
NORM_AT = {n: sum(NORM_PARTS[:i]) for i, n in enumerate(TURNS)}

COL = {"ln1_g": 0, "ln1_b": 16, "ln2_g": 32, "ln2_b": 48, "ffn1": 64, "mix": 80, "ffn2": 96, "ssm_norm": 112,
       "ssm_conv_w": 128, "ssm_conv_b": 288, "conv_b": 320, "conv_norm": 328, "subln": 336, "q_norm": 338,
       "k_norm": 340, "conv_w": 384}
ROW_BLOCKS = [128, 128, 86, 124, 124]
COL["conv_w1"] = 512

CONST = {}
_at = 0
for _n, _w in (("ident", P), ("rot", P), ("dup0", P), ("rdup0", P), ("dup1", P), ("rdup1", P), ("na_flip", P),
               ("cos", T), ("sin", T), ("mask_a", 2 * T), ("mask_na", 2 * T),
               ("mask_ssm", 256), ("select", 64), ("nselect", 64),
               ("flip", P), ("halves", P), ("causal", 384), ("buckets", 384)):
    CONST[_n] = (_at, _w)
    _at += _w
CONST_W = _at


def shape_constants():
    c = np.zeros((P, CONST_W), np.float32)

    def put(name, a):
        at, w = CONST[name]
        assert a.shape[1] == w
        c[:a.shape[0], at:at + w] = a

    eye = np.eye(P, dtype=np.float32)
    put("ident", eye)
    half = HD // 2
    rot = np.zeros((P, P), np.float32)
    for b in range(0, P, HD):
        for i in range(half):
            rot[b + half + i, b + i] = -1.0
            rot[b + i, b + half + i] = 1.0
    put("rot", rot)
    for j in range(2):
        dup = np.zeros((P, P), np.float32)
        for b in range(0, P, HD):
            for i in range(HD):
                dup[j * HD + i, b + i] = 1.0
        put(f"dup{j}", dup)
        put(f"rdup{j}", dup @ rot)
    flip = eye[::-1].copy()
    put("flip", flip)
    na = np.zeros((P, P), np.float32)
    for b in range(0, P, 64):
        for i in range(64):
            na[b + 63 - i, b + i] = 1.0
    put("na_flip", na)
    inv = (10000.0 ** (-np.arange(half, dtype=np.float32) / half)).astype(np.float32)
    ang = (np.arange(T, dtype=np.float32)[:, None] * inv[None, :]).astype(np.float32)
    put("cos", np.tile(np.cos(ang).T, (P // half, 1)).astype(np.float32))
    put("sin", np.tile(np.sin(ang).T, (P // half, 1)).astype(np.float32))
    q = np.arange(T)
    far = np.abs(q[:, None] - q[None, :]) > WINDOW
    put("mask_a", np.where(far, np.float32(NEG), np.float32(0)).reshape(2, P, T).transpose(1, 0, 2).reshape(P, 2 * T))
    col = q % GRID_W
    lo = np.clip(col - NA_KW // 2, 0, GRID_W - NA_KW)
    inside = (col[None, :] >= lo[:, None]) & (col[None, :] < lo[:, None] + NA_KW)
    put("mask_na", np.where(inside, np.float32(0), np.float32(NEG)).reshape(2, P, T).transpose(1, 0, 2)
        .reshape(P, 2 * T))
    s, l = np.arange(P)[:, None], np.arange(P)[None, :]
    put("mask_ssm", np.where(np.concatenate([s > l, s < l], 1), np.float32(NEG), np.float32(0)))
    sel = np.concatenate([np.eye(64), np.eye(64)]).astype(np.float32)
    put("select", sel)
    put("nselect", -sel)
    put("halves", np.kron(np.eye(2), np.ones((64, 64))).astype(np.float32))
    k0, k1 = np.arange(P)[None, :], np.arange(T)[None, :]
    put("causal", np.where(np.concatenate([k0 > s, k1 > s + P], 1), np.float32(NEG), np.float32(0)))
    dist = np.maximum(255 - np.arange(384), 0)
    exact = BUCKETS // 2
    nf = np.maximum(dist, 1).astype(np.float32)
    large = exact + (np.log(nf / np.float32(exact)) / np.float32(math.log(128 / exact))
                     * np.float32(BUCKETS - exact)).astype(np.int32)
    bucket = np.where(dist < exact, dist, np.minimum(large, BUCKETS - 1))
    put("buckets", (bucket[None, :] == np.arange(BUCKETS)[:, None]).astype(np.float32))
    return c


def by_pool(u):
    return U_SSM + 2 <= u < U_SSM + 17 or any(U_MIX[l] + 2 <= u < U_MIX_OUT[l] + OUT_UNITS for l in range(DEPTH))


N_SUMS = 4 + 3 * DEPTH
CONST_BLK = 48
N_PAR = 20


def lambda_init(l):
    return 0.8 - 0.6 * math.exp(-0.3 * l)


def two_blocks(nc, A, out):
    with ExitStack() as ctx:
        def sb(name, shape, dt=F32):
            return ctx.enter_context(nc.sbuf_tensor(name, shape, dt))

        def sem(name):
            return ctx.enter_context(nc.semaphore(name))

        w_raw = sb("w_raw", [P, RING, UN])
        w_hi = sb("w_hi", [P, RING, UN], F32R)
        w_lo = sb("w_lo", [P, RING, UN], F32R)
        op_hi = sb("op_hi", [P, 16, T], F32R)
        op_lo = sb("op_lo", [P, 16, T], F32R)
        X = sb("X", [P, TT, D])
        xn = sb("xn", [P, TT, D])
        turn_buf = sb("turn_buf", [P, 2, 2, T])
        act_buf = sb("act_buf", [P, 2 * T])
        h32 = sb("h32", [P, 2 * T])
        gain_row = sb("gain_row", [P, D])
        bias_row = sb("bias_row", [P, D])
        prow = sb("prow", [P, 5, P])
        pcol = sb("pcol", [P, 5 * P])
        ident = sb("ident", [P, P])
        stats = sb("stats", [P, TT, 2, 6])
        mv = sb("mv", [P, TT, 2])
        std = sb("std", [P, TT])
        rstd = sb("rstd", [P, TT])
        ssum = sb("ssum", [P, 4])
        part = sb("part", [P, TT])
        lnb = sb("lnb", [P, 4])
        zeros = sb("zeros", [P, 2], mybir.dt.bfloat16)
        select = sb("select", [P, 64], F32R)
        nselect = sb("nselect", [P, 64], F32R)
        neg_tri = sb("neg_tri", [P, 2, P], F32R)
        ident_r = sb("ident_r", [P, P], F32R)
        g_pair = sb("g_pair", [P, TT, 2, P], F32R)
        AR = 15872
        arena = sb("arena", [P, AR])

        acc = ctx.enter_context(nc.psum_tensor("acc", [P, 4, 512], F32))
        pg = ctx.enter_context(nc.psum_tensor("pg", [P, 4, 512], F32))

        class Carve:
            def __init__(self, at=0):
                self.at = at

            def __call__(self, *shape):
                n = int(np.prod(shape))
                v = arena[:, self.at:self.at + n]
                self.at += n
                assert self.at <= AR, self.at
                if len(shape) == 2:
                    v = v.rearrange("p (a b) -> p a b", a=shape[0])
                elif len(shape) == 3:
                    v = v.rearrange("p (a b c) -> p a b c", a=shape[0], b=shape[1])
                return v

        cv = Carve()
        n_att = CONST["mask_ssm"][0] - P
        att_c = cv(n_att)

        def att_const(name):
            at, w = CONST[name]
            return att_c[:, at - P:at - P + w]

        q_raw = cv(2, 2 * T)
        r_tmp = cv(2, 2 * T)
        k_raw = cv(T)
        QT = cv(8, T)
        KT = cv(6, T)
        va = cv(TT, AKV * HD)
        vb = cv(TT, BH * HD)
        na_bias = cv(BH, 2, T)
        prob = cv(4, 2, T)
        probT = turn_buf
        sink = cv(16)
        mx = cv(16, 2)
        nmx = cv(16, 2)
        psm = cv(16, 2)
        pes = cv(16, 2)
        pden = cv(16, 2)
        cv = Carve()
        BT = cv(SG, T)
        CT = cv(SG, T)
        xs = cv(TT, DI)
        silz = cv(TT, DI)
        ssd_at = cv.at
        E = cv(4, 6, P)
        over = Carve(ssd_at)
        conv_in = over(2, 2, T + CONV - 1)
        xsT = over(2, 2, T)
        conv_sum = over(2, 2, T)
        cv.at = max(cv.at, over.at)
        ssm_c = prow[:, :, :].rearrange("p a n -> p (a n)")[:, 0:384]
        dt_bias = cv(64)
        d_skip = cv(SH)
        a_col = cv(1)
        dt_tok = cv(TT, 64)
        one_col = cv(1)
        aT, gT = act_buf[:, 0:T], act_buf[:, T:2 * T]
        dt_v, dt_a = (h32[:, i * P:i * P + P].rearrange("p (t n) -> p t n", t=TT) for i in range(2))
        xD = [b[:, :].rearrange("p (t n) -> p t n", t=TT) for b in (act_buf, h32)]
        ysq = cv(TT, SG)
        yrs = cv(TT, SG)
        diag = xn[:, 0, 0:TT * P].rearrange("p (t n) -> p t n", t=TT)
        scrap = [turn_buf[:, 0, :, :], turn_buf[:, 1, :, :]] + \
            [xn[:, 1, i * 512:(i + 1) * 512].rearrange("p (a n) -> p a n", a=2) for i in range(2)]
        cv = Carve()
        blk_c = cv(CONST_W - CONST["flip"][0])

        def blk_const(name):
            at, w = CONST[name]
            at -= CONST["flip"][0]
            return blk_c[:, at:at + w]

        ones_m = cv(1)
        rbias = cv(DH, 384)
        rel = cv(DH)
        rvec = cv(384)
        lam_q = cv(4, HD)
        lam_k = cv(4, HD)
        lam_s = cv(4)
        lam_e = cv(4)
        nlam = cv(2)
        sub_g = cv(2)
        gate = cv(2, T)
        uu = cv(4, T + CK - 1)
        cacc = cv(4, T)
        pool_acc, pool_tap = (v.rearrange("p a n -> p (a n)") for v in (lam_q, lam_k))
        sq = turn_buf[:, :, :, :].rearrange("p a b t -> p a (b t)")
        hdev = cv(2, 8)
        hexp = cv(2, 2 * T)
        odev = cv(2, 4)
        cdev = cv(TT)
        Q2 = cv(DH, T)
        K2 = cv(DH, T)
        V2 = cv(TT, 2 * T)
        prob2 = cv(4, 384)
        pmix = cv(2, 384)
        pmixT = cv(2, 384)
        O2 = cv(DH, T)
        osq = cv(4, T)
        o_scrap = xn[:, 0, :].rearrange("p (a t) -> p a t", a=4)
        c32 = xn[:, 1, :].rearrange("p (a t) -> p a t", a=4)
        m2 = cv(8, 2)
        n2 = cv(8, 2)
        s2 = cv(8, 2)
        r2 = cv(8, 2)

        rel_dram = nc.dram_tensor("rel_scratch", (DH, 384), F32, kind="Internal").ap()

        raw_ready = [sem(f"raw_ready{i}") for i in range(RING)]
        hi_ready = sem("hi_ready")
        lo_ready = sem("lo_ready")
        unit_done = sem("unit_done")
        x_in = [sem(f"x_in{t}") for t in range(TT)]
        par_in = sem("par_in")
        const_in = sem("const_in")
        small_in = sem("small_in")
        bias_in = sem("bias_in")
        par_turned = sem("par_turned")
        par_ready = sem("par_ready")
        fixed_ready = sem("fixed_ready")
        bias_flipped = sem("bias_flipped")
        bias_ready = sem("bias_ready")
        bias_evac = sem("bias_evac")
        ident_in = sem("ident_in")
        sum_done = sem("sum_done")
        norm_ready = sem("norm_ready")
        turned = sem("turned")
        gained = sem("gained")
        xt_ready = sem("xt_ready")
        x_new = sem("x_new")
        var_ready = sem("var_ready")
        std_ready = sem("std_ready")
        rows_in = sem("rows_in")
        x_settled = sem("x_settled")
        x_final = sem("x_final")
        dve_link = sem("dve_link")
        act_link = sem("act_link")
        pool_link = sem("pool_link")
        attn_evac = sem("attn_evac")
        rot_done = sem("rot_done")
        rope_done = sem("rope_done")
        score_done = sem("score_done")
        score_taken = sem("score_taken")
        max_ready = sem("max_ready")
        exp_done = sem("exp_done")
        p_ready = sem("p_ready")
        pT_done = sem("pT_done")
        pt_ready = sem("pt_ready")
        pv_done = sem("pv_done")
        ot_hi = sem("ot_hi")
        ot_ready = sem("ot_ready")
        act_done = sem("act_done")
        h32_ready = sem("h32_ready")
        h_hi = sem("h_hi")
        h_ready = sem("h_ready")
        stored = sem("stored")
        dt_sum = sem("dt_sum")
        dt_soft = sem("dt_soft")
        dt_ready = sem("dt_ready")
        dtT_done = sem("dtT_done")
        g_ready = sem("g_ready")
        sel_ready = sem("sel_ready")
        conv_evac = sem("conv_evac")
        conv_done = sem("conv_done")
        conv_silu = sem("conv_silu")
        xsT_done = sem("xsT_done")
        xs_ready = sem("xs_ready")
        z_ready = sem("z_ready")
        cb_done = sem("cb_done")
        skip_ready = sem("skip_ready")
        diff_done = sem("diff_done")
        e_ready = sem("e_ready")
        e_sum = sem("e_sum")
        m_ready = sem("m_ready")
        head_done = sem("head_done")
        y_gated = sem("y_gated")
        y_sq = sem("y_sq")
        y_std = sem("y_std")
        lam_in = sem("lam_in")
        lam_sum = sem("lam_sum")
        lam_exp = sem("lam_exp")
        rel_sum = sem("rel_sum")
        rel_row = sem("rel_row")
        rel_out = sem("rel_out")
        gate_ready = sem("gate_ready")
        u_ready = sem("u_ready")
        qk_sq = sem("qk_sq")
        qk_sum = sem("qk_sum")
        qk_std = sem("qk_std")
        qk_rstd = sem("qk_rstd")
        qk_exp = sem("qk_exp")
        qk_spread = sem("qk_spread")
        qk_ready = sem("qk_ready")
        v_ready = sem("v_ready")
        sc2_done = sem("sc2_done")
        sc2_taken = sem("sc2_taken")
        mx2_ready = sem("mx2_ready")
        ex2_done = sem("ex2_done")
        mix_ready = sem("mix_ready")
        mixT_done = sem("mixT_done")
        mixT_ready = sem("mixT_ready")
        o2_done = sem("o2_done")
        o2_evac = sem("o2_evac")
        osq_std = sem("osq_std")
        o2_norm = sem("o2_norm")
        oT_done = sem("oT_done")
        o2_hi = sem("o2_hi")
        o2_ready = sem("o2_ready")
        cconv = sem("cconv")
        pool_conv = sem("pool_conv")
        csq = sem("csq")
        cpair = sem("cpair")
        csum = sem("csum")
        cstd = sem("cstd")
        crstd = sem("crstd")
        cspread = sem("cspread")
        cnorm = sem("cnorm")
        c_hi = sem("c_hi")
        c_ready = sem("c_ready")

        def at(base, it, per):
            return base if it is None else base + it * per

        def head_pair(n):
            c = 2 * ((n - 4) // 2)
            return (K2 if n % 2 else Q2)[:, c:c + 2, :].rearrange("p c t -> p (c t)")

        class Link:
            def __init__(self, eng, s):
                self.eng, self.s, self.n = eng, s, 0

            def __call__(self, ins):
                self.n += 1
                ins.then_inc(self.s, 1)
                self.eng.wait_ge(self.s, self.n)

            def mark(self, ins):
                self.n += 1
                ins.then_inc(self.s, 1)

            def all_but(self, k):
                self.eng.wait_ge(self.s, self.n - k)

        def cols_view(w):
            return w.rearrange("(k p) n -> p k n", p=P)

        v_att = cols_view(A["attn_w_in"][0])
        v_ssm = cols_view(A["ssm_w_in"][0])
        v_att_out = cols_view(A["attn_w_out"][0])
        v_ssm_out = cols_view(A["ssm_w_out"][0])
        v_w1 = [cols_view(A["mlp_w1"][l]) for l in range(DEPTH)]
        v_w2 = [cols_view(A["mlp_w2"][l]) for l in range(DEPTH)]
        ffn = [(cols_view(A[f"ffn{s}_w_gate_2"][l]), cols_view(A[f"ffn{s}_w_up_2"][l]),
                cols_view(A[f"ffn{s}_w_down_2"][l])) for l in range(DEPTH) for s in (1, 2)]
        v_mix = [cols_view(A["w_in_2"][l]) for l in range(DEPTH)]
        v_mix_out = [cols_view(A["w_out_2"][l]) for l in range(DEPTH)]

        n_par = [0]
        n_rows = [0]
        block = ctx.enter_context(nc.Block())

        @block.sync
        def _(sp):
            def load(u, src, it=None, per=0, width=UN):
                if u >= RING:
                    sp.wait_ge(lo_ready, at(u - RING + 1, it, per))
                dst = w_raw[:, u % RING, 0:width].rearrange("p (k n) -> p k n", k=src.shape[1])
                sp.dma_start(dst, src).then_inc(raw_ready[u % RING], 16)

            def columns(v, c):
                return v[:, :, c:c + U]

            def rows(v, g):
                return v[:, 2 * g:2 * g + 2, :]

            def mlp(u0, w1, w2):
                load(u0, columns(w1, 0))
                with sp.Fori(0, (G1 - 1) // 3) as it:
                    for j in range(3):
                        load(u0 + 1 + 2 * j, w1[:, :, bass.ds(it * (3 * U) + (1 + j) * U, U)], it, 6)
                        load(u0 + 2 + 2 * j, w2[:, bass.ds(it * 6 + 2 * j, 2), :], it, 6)
                load(u0 + 2 * G1 - 1, rows(w2, G1 - 1))

            def swiglu(u0, w):
                load(u0, columns(w[0], 0))
                load(u0 + 1, columns(w[1], 0))
                with sp.Fori(0, G2 - 1) as it:
                    load(u0 + 2, w[0][:, :, bass.ds(it * U + U, U)], it, 3)
                    load(u0 + 3, w[1][:, :, bass.ds(it * U + U, U)], it, 3)
                    load(u0 + 4, w[2][:, bass.ds(it * 2, 2), :], it, 3)
                load(u0 + 3 * G2 - 1, rows(w[2], G2 - 1))

            for n in range(A_UNITS):
                load(U_ATT + n, columns(v_att, n * U))
                if n == 0:
                    for t in range(TT):
                        sp.dma_start(X[:, t, :], A["x"][0, t * P:(t + 1) * P, :]).then_inc(x_in[t], 16)
                if n == 1:
                    sp.dma_start(att_c, A["consts"][:, P:P + n_att]).then_inc(const_in, 16)
            for n in range(OUT_UNITS):
                load(U_ATT_OUT + n, rows(v_att_out, n))
            mlp(U_MLP[0], v_w1[0], v_w2[0])
            for n, c in enumerate(SSM_COLS):
                if n == DT_AT:
                    load(U_SSM + n, v_ssm[:, :, c:c + 64], width=KC * 64)
                else:
                    load(U_SSM + n, columns(v_ssm, c))
            for n in range(DI // U):
                load(U_SSM_OUT + n, rows(v_ssm_out, n))
            mlp(U_MLP[1], v_w1[1], v_w2[1])
            for l in range(DEPTH):
                swiglu(U_FFN[2 * l], ffn[2 * l])
                for n, c in enumerate(MIX_COLS):
                    load(U_MIX[l] + n, columns(v_mix[l], c))
                for n in range(OUT_UNITS):
                    load(U_MIX_OUT[l] + n, rows(v_mix_out[l], n))
                swiglu(U_FFN[2 * l + 1], ffn[2 * l + 1])
            for t in range(TT):
                sp.wait_ge(x_new, 4 * (N_SUMS - 1) + 2 * (t + 1))
                sp.dma_start(out[0, t * P:(t + 1) * P, :], X[:, t, :]).then_inc(stored, 16)
            sp.wait_ge(stored, 16 * TT)

        @block.gpsimd
        def _(pool):
            link = Link(pool, pool_link)

            def par(dst, src):
                pool.dma_start(dst, src).then_inc(par_in, 16)
                n_par[0] += 1

            def rows_of(v):
                return v.rearrange("l (c p) -> (l c) p", p=P)

            rpb = A["attn_rpb"]
            for h in range(BH):
                for qt in range(TT):
                    for r in range(2):
                        src = bass.AP(rpb.tensor, rpb.offset + h * RPB_R * RPB_C + (NA_KH - 1 - 2 * qt - r) * RPB_C
                                      + NA_KW - 1 - (GRID_W - 1), [[1, 64], [RPB_C, 4], [1, GRID_W]])
                        pool.dma_start(na_bias[r * 64:r * 64 + 64, h, qt, :].rearrange("p (a k) -> p a k", a=4),
                                       src).then_inc(bias_in, 16)
            for i, n in enumerate(("ln1_g", "ln1_b", "ln2_g", "ln2_b", "ffn1_norm_2", "mix_norm_2", "ffn2_norm_2",
                                   "ssm_norm_w")):
                par(prow[16 * i:16 * i + 16, 0, :], rows_of(A[n]))
            cw = A["ssm_conv_w"][0].rearrange("k (c p) -> (k c) p", p=P)
            par(prow[:, 1, :], cw[0:128, :])
            par(prow[0:32, 2, :], cw[128:160, :])
            par(prow[32:64, 2, :], rows_of(A["ssm_conv_b"]))
            par(prow[64:72, 2, :], rows_of(A["conv_b_2"]))
            par(prow[72:80, 2, :], rows_of(A["conv_norm_2"]))
            par(prow[80:82, 2, :], A["subln_norm_2"])
            for h in range(2):
                par(prow[82:84, 2, h * HD:h * HD + HD], A["q_norm_2"])
                par(prow[84:86, 2, h * HD:h * HD + HD], A["k_norm_2"])
            for l in range(DEPTH):
                par(prow[0:CK * 4, 3 + l, :], A["conv_w_2"][l].rearrange("k (c p) -> (k c) p", p=P))

            pool.dma_start(sink[:, 0:AQ], A["attn_sink"].broadcast_to([P, AQ])).then_inc(small_in, 16)

            def split(u):
                assert by_pool(u)
                pool.wait_ge(hi_ready, u + 1)
                if not by_pool(u - 1):
                    pool.wait_ge(lo_ready, u)
                r = u % RING
                pool.tensor_tensor(w_lo[:, r, :], w_raw[:, r, :], w_hi[:, r, :].bitcast(F32), ALU.subtract) \
                    .then_inc(lo_ready, 1)

            lns = [("ln1", 0), ("ln2", 0), ("ln1", 1), ("ln2", 1)]

            def rows_load(i):
                n, l = lns[i]
                pool.dma_start(gain_row[:, :], A[n + "_g"][l:l + 1, :].broadcast_to([P, D])).then_inc(rows_in, 16)
                pool.dma_start(bias_row[:, :], A[n + "_b"][l:l + 1, :].broadcast_to([P, D])).then_inc(rows_in, 16)

            def settle(i, name):
                pool.wait_ge(rows_in, 32 * (i + 1))
                pool.wait_ge(norm_ready, NORM_AT[name] + 1 + KC // 2)
                for t in range(TT):
                    link(pool.tensor_tensor(X[:, t, :], xn[:, t, :], gain_row[:, :], ALU.mult))
                for t in range(TT):
                    ins = pool.tensor_tensor(X[:, t, :], X[:, t, :], bias_row[:, :], ALU.add)
                    ins.then_inc(x_settled, 1)
                pool.wait_ge(x_settled, 2 * (i + 1))

            rows_load(0)
            settle(0, "ln1_0")
            rows_load(1)
            pool.wait_ge(h_ready, HG_MLP[0] + G1)
            pool.dma_start(dt_bias, A["ssm_dt_bias"].broadcast_to([P, 64])).then_inc(small_in, 16)
            pool.dma_start(d_skip, A["ssm_D"].broadcast_to([P, SH])).then_inc(small_in, 16)
            pool.dma_start(a_col[0:64, :], A["ssm_A_log"].rearrange("a d (h o) -> (a d h) o", o=1)) \
                .then_inc(small_in, 16)
            settle(1, "ln2_0")
            rows_load(2)
            for n in range(2, 17):
                split(U_SSM + n)

            pool.wait_ge(dt_ready, 1)
            pool.wait_ge(small_in, 64)
            for g in range(SG):
                b = g % 2
                pool.wait_ge(xs_ready, g + 1)
                if g >= 2:
                    pool.wait_ge(y_gated, g - 1)
                for t in range(TT):
                    xg = xs[:, t, g * U:g * U + U].rearrange("p (h e) -> p h e", h=GH)
                    ds = d_skip[:, g * GH:(g + 1) * GH]
                    ins = pool.tensor_tensor(xD[b][:, t, :].rearrange("p (h e) -> p h e", h=GH), xg,
                                             ds.unsqueeze(2).broadcast_to([P, GH, HD]), ALU.mult)
                ins.then_inc(skip_ready, 1)
                for h in range(g * GH, (g + 1) * GH):
                    pool.wait_ge(m_ready, h + 1)
                    e = E[:, h % 4, 0:3:2, :]
                    pool.tensor_tensor(e, e, E[:, h % 4, 3:6:2, :], ALU.add).then_inc(e_sum, 1)
            pool.wait_ge(norm_ready, NORM_AT["ln1_1"] + 1)
            pool.dma_start(rel[0:BUCKETS, :], A["rel_bias_2"]).then_inc(lam_in, 16)
            for i, n in enumerate(("lambda_q1_2", "lambda_q2_2")):
                pool.dma_start(lam_q[:, 2 * i:2 * i + 2, :], A[n].unsqueeze(0).broadcast_to([P, DEPTH, HD])) \
                    .then_inc(lam_in, 16)
            for i, n in enumerate(("lambda_k1_2", "lambda_k2_2")):
                pool.dma_start(lam_k[:, 2 * i:2 * i + 2, :], A[n].unsqueeze(0).broadcast_to([P, DEPTH, HD])) \
                    .then_inc(lam_in, 16)
            settle(2, "ln1_1")
            rows_load(3)
            pool.wait_ge(rel_row, 1)
            pool.dma_start(rel_dram, rvec[0:DH, :]).then_inc(rel_out, 16)
            pool.wait_ge(rel_out, 16)
            for h in range(DH):
                for off, k0, n in ((128, 0, 128), (0, 128, 256)):
                    src = bass.AP(rel_dram.tensor, rel_dram.offset + h * 384 + off, [[1, P], [1, n]])
                    pool.dma_start(rbias[:, h, k0:k0 + n], src).then_inc(bias_in, 16)
            for h in range(DH):
                pool.wait_ge(bias_evac, h + 1)
                if h == 0:
                    pool.wait_ge(const_in, CONST_BLK)
                pool.tensor_tensor(rbias[:, h, :], rbias[:, h, :], blk_const("causal"), ALU.add) \
                    .then_inc(bias_ready, 1)
            for l in range(DEPTH):
                for u in range(U_MIX[l] + 2, U_MIX_OUT[l] + 2):
                    split(u)
                for k in range(CK - POOL_TAPS, CK):
                    wc = COL["conv_w"] + l * P + 4 * k + 3
                    dst = pool_tap if k > CK - POOL_TAPS else pool_acc
                    link(pool.tensor_scalar(dst, uu[:, 3, k:k + T], pcol[:, wc:wc + 1], None, ALU.mult))
                    if k > CK - POOL_TAPS:
                        ins = pool.tensor_tensor(pool_acc, pool_acc, pool_tap, ALU.add)
                        if k < CK - 1:
                            link(ins)
                ins.then_inc(pool_conv, 1)
                for u in range(U_MIX_OUT[l] + 2, U_MIX_OUT[l] + OUT_UNITS):
                    split(u)

        @block.scalar
        def _(act):
            link = Link(act, act_link)

            def split(u, it=None, per=0):
                if u >= N_UNITS:
                    return
                act.wait_ge(raw_ready[u % RING], at(16 * (u // RING + 1), it, 16 * per // RING))
                if u >= RING:
                    act.wait_ge(unit_done, at(u - RING + 1, it, per))
                act.copy(w_hi[:, u % RING, :], w_raw[:, u % RING, :]).then_inc(hi_ready, 1)

            def turn(name, gain, bias):
                turn_banks(name, gain, bias, 0, TURN_CHUNKS[TURNS.index(name)] // 2)

            def turn_banks(name, gain, bias, b0, b1):
                for b in range(b0, b1):
                    k = TURN_BANK[name] + b
                    act.wait_ge(turned, k + 1)
                    if bias is not None and b >= 2:
                        act.wait_ge(xt_ready, k - 1)
                    for c in range(2):
                        j = 2 * b + c
                        ins = act.activation(op_hi[:, j, :] if bias is None else turn_buf[:, b % 2, c, :],
                                             pg[:, b % 4, c * T:(c + 1) * T], ACT.Identity,
                                             scale=1.0 if gain is None else pcol[:, gain + j:gain + j + 1],
                                             bias=0.0 if bias is None else pcol[:, bias + j:bias + j + 1])
                    ins.then_inc(gained, 1)

            def ln_std(k):
                link(act.activation(part[:, 0:1], lnb[:, 0:1], ACT.Sqrt))
                for t in range(TT):
                    act.wait_ge(var_ready, 2 * (k - 1) + t + 1)
                    act.activation(std[:, t:t + 1], mv[:, t, 1:2], ACT.Sqrt, bias=lnb[:, 0:1]) \
                        .then_inc(std_ready, 1)
                    if k == 4:
                        rms_tile(t, x_final, 0)

            def rms_std(k, src_ready, base):
                link(act.activation(part[:, 0:1], lnb[:, 0:1], ACT.Sqrt))
                for t in range(TT):
                    rms_tile(t, src_ready, base)

            def rms_tile(t, src_ready, base):
                for a in range(2):
                    q = 2 * t + a
                    act.wait_ge(src_ready, base + q + 1)
                    link(act.activation(scrap[q], X[:, t, a * 512:(a + 1) * 512].rearrange("p (a n) -> p a n", a=2),
                                        ACT.Square, accum_out=ssum[:, q:q + 1]))
                    if a == 0:
                        link(act.activation(part[:, t:t + 1], ssum[:, q:q + 1], ACT.Identity, scale=1.0 / D,
                                            bias=lnb[:, 1:2]))
                act.activation(std[:, t:t + 1], ssum[:, q:q + 1], ACT.Sqrt, bias=part[:, t:t + 1],
                               scale=1.0 / D).then_inc(std_ready, 1)

            def hidden(h, u_in, func, src, it=None, per_h=0, per_u=0):
                act.wait_ge(unit_done, at(u_in + 1, it, per_u))
                act.activation(act_buf[:, :], src, func).then_inc(act_done, 1)

            def hidden_hi(h, u_free, it=None, per_h=0, per_u=0, at_chunk=8):
                act.wait_ge(h32_ready, at(h + 1, it, per_h))
                if u_free is not None:
                    act.wait_ge(unit_done, at(u_free + 1, it, per_u))
                act.copy(op_hi[:, at_chunk:at_chunk + 2, :], h32[:, :].rearrange("p (c t) -> p c t", c=2)) \
                    .then_inc(h_hi, 1)

            def mlp(u0, h0, between=None):
                split(u0 + 2)
                hidden(h0, u0, ACT.Relu, pg[:, 0, :])
                hidden_hi(h0, None)
                if between:
                    between()

                def groups(u1, h1, it=None, last=False):
                    for j in range(3):
                        u = u1 + 2 * j
                        split(u + 2, it, 6)
                        hidden(h1 + j, u, ACT.Relu, pg[:, (1 + j) % 3, :], it, 3, 6)
                        if last and j == 2:
                            hidden_hi(h1 + j, None, at_chunk=10)
                        split(u + 3, it, 6)
                        if not (last and j == 2):
                            hidden_hi(h1 + j, u + 1, it, 3, 6)

                with act.Fori(0, (G1 - 1) // 3 - 1) as it:
                    groups(u0 + 1, h0 + 1, it)
                groups(u0 + 2 * G1 - 7, h0 + G1 - 3, last=True)
                split(u0 + 2 * G1 + 1)

            def swiglu(u0, h0, between=None):
                split(u0 + 2)
                hidden(h0, u0, ACT.Silu, pg[:, 0, :])
                split(u0 + 3)
                hidden_hi(h0, None)
                if between:
                    between(0)

                def group(u, h, it=None, last=False):
                    split(u + 2, it, 3)
                    hidden(h, u, ACT.Silu, pg[:, 0, :], it, 1, 3)
                    split(u + 3, it, 3)
                    if last:
                        hidden_hi(h, None, at_chunk=10)
                    split(u + 4, it, 3)
                    if not last:
                        hidden_hi(h, u + 2, it, 1, 3)

                with act.Fori(0, G2 - 2) as it:
                    group(u0 + 2, h0 + 1, it)
                group(u0 + 3 * G2 - 4, h0 + G2 - 1, last=True)
                split(u0 + 3 * G2 + 1)
                if between:
                    between(2)

            def head_expand(l, n):
                i = 4 * l + n - 4
                act.wait_ge(qk_rstd, i + 1)
                act.copy(hexp[:, i % 2, :].rearrange("p (k n) -> p k n", n=HD),
                         hdev[:, i % 2, :].unsqueeze(2).broadcast_to([P, 8, HD])).then_inc(qk_exp, 1)

            def o2_out(l, h):
                i = DH * l + h
                act.wait_ge(o2_done, i + 1)
                act.copy(O2[:, h, :], acc[:, h % 2, 0:T])
                for t in range(TT):
                    ins = act.activation(o_scrap[:, h, t * P:(t + 1) * P], acc[:, h % 2, t * P:(t + 1) * P],
                                         ACT.Square, accum_out=odev[:, h // 2, (h % 2) * TT + t:(h % 2) * TT + t + 1])
                ins.then_inc(o2_evac, 1)

            act.dma_start(ident[:, :], A["consts"][:, 0:P]).then_inc(ident_in, 16)
            split(0)
            turn("x", None, None)
            split(1)

            for n in range(A_UNITS):
                u = U_ATT + n
                split(u + 2)
                act.wait_ge(unit_done, u + 1)
                bank = pg[:, n % 4, :]
                pair = bank.rearrange("p (c t) -> p c t", c=2)
                if n < 2:
                    ins = act.copy(q_raw[:, n, :], bank)
                elif n == 2:
                    act.copy(k_raw, bank[:, 0:T])
                    ins = act.copy(va, bank[:, T:2 * T].rearrange("p (t n) -> p t n", t=TT))
                elif n < 5:
                    ins = act.copy(QT[:, 4 + 2 * (n - 3):6 + 2 * (n - 3), :], pair)
                elif n < 7:
                    ins = act.copy(KT[:, 2 + 2 * (n - 5):4 + 2 * (n - 5), :], pair)
                else:
                    ins = act.copy(vb[:, :, (n - 7) * U:(n - 6) * U], pair)
                ins.then_inc(attn_evac, 1)
            for s in range(AQ + BH + 5):
                if s < AQ + BH:
                    act.wait_ge(max_ready, s + 1)
                    for qt in range(TT):
                        act.activation(prob[:, s % 4, qt, :], prob[:, s % 4, qt, :], ACT.Exp,
                                       bias=nmx[:, s, qt:qt + 1], accum_out=psm[:, s, qt:qt + 1])
                    act.activation(pes[:, s, :], nmx[:, s, :], ACT.Exp, bias=sink[:, s:s + 1]).then_inc(exp_done, 1)
                h = s - 3
                if 0 <= h < AQ + BH:
                    act.wait_ge(pT_done, h + 1)
                    if h >= 2:
                        act.wait_ge(pv_done, h - 1)
                    act.copy(probT[:, h % 2, :, :], pg[:, 2 + h % 2, :].rearrange("p (c t) -> p c t", c=2)) \
                        .then_inc(pt_ready, 1)
                if s >= 6 and s % 2 == 0:
                    c = (s - 6) // 2
                    act.wait_ge(pv_done, 2 * c + 2)
                    act.copy(op_hi[:, 8 + c, :], acc[:, c % 4, 0:T]).then_inc(ot_hi, 1)
            for n in range(OUT_UNITS):
                split(U_ATT_OUT + n + 2)
            ln_std(1)
            turn("ln1_0", COL["ln1_g"], COL["ln1_b"])
            mlp(U_MLP[0], HG_MLP[0])
            act.wait_ge(h_ready, HG_MLP[0] + G1)
            c0 = CONST["mask_ssm"][0]
            act.dma_start(ssm_c, A["consts"][:, c0:c0 + 384]).then_inc(const_in, 16)
            ln_std(2)
            act.wait_ge(const_in, 32)
            act.copy(select[:, :], ssm_c[:, 256:320])
            act.copy(neg_tri[:, :, :], ssm_c[:, 0:256].rearrange("p (d n) -> p d n", d=2))
            act.copy(ident_r[:, :], ident[:, :])
            act.copy(nselect[:, :], ssm_c[:, 320:384]).then_inc(sel_ready, 1)
            turn("ln2_0", COL["ln2_g"], COL["ln2_b"])

            def conv_act(i):
                act.wait_ge(conv_done, i + 1)
                bias = COL["ssm_conv_b"]
                for c in range(2):
                    ch = (16 + 2 * i + c) % 32
                    if i < 8:
                        dst = (BT if i < 4 else CT)[:, 2 * (i % 4) + c, :]
                    else:
                        if i >= 10 and c == 0:
                            act.wait_ge(xsT_done, i - 9)
                        dst = xsT[:, i % 2, c, :]
                    ins = act.activation(dst, conv_sum[:, i % 2, c, :], ACT.Silu,
                                         bias=pcol[:, bias + ch:bias + ch + 1])
                ins.then_inc(conv_silu, 1)

            i = 0
            for n in range(len(SSM_COLS)):
                u = U_SSM + n
                split(u + 2)
                if n == DT_AT:
                    act.wait_ge(dt_sum, 1)
                    link(act.activation(dt_a, dt_v, ACT.Abs))
                    link(act.activation(dt_a, dt_a, ACT.Exp, scale=-1.0))
                    act.activation(dt_a, dt_a, ACT.Ln, bias=1.0).then_inc(dt_soft, 1)
                    act.activation(a_col[0:64, :], a_col[0:64, :], ACT.Exp).then_inc(dt_soft, 1)
                    continue
                act.wait_ge(unit_done, u + 1)
                pair = pg[:, n % 4, :].rearrange("p (c t) -> p c t", c=2)
                if n < len(SSM_COLS) - Z_UNITS:
                    if i >= 2:
                        act.wait_ge(conv_done, i - 1)
                    act.copy(conv_in[:, i % 2, :, 2:2 + T], pair).then_inc(conv_evac, 1)
                    if i >= 1:
                        conv_act(i - 1)
                    i += 1
                else:
                    if i == 16:
                        conv_act(15)
                        i += 1
                    z = n - (len(SSM_COLS) - Z_UNITS)
                    act.activation(silz[:, :, z * U:z * U + U], pair, ACT.Silu).then_inc(z_ready, 1)
            for h in range(SH):
                b = h % 2
                for d in range(2):
                    act.wait_ge(diff_done, 2 * h + d + 1)
                    if h >= 4 and d == 0:
                        act.wait_ge(head_done, h - 3)
                    act.activation(E[:, h % 4, 3 * d:3 * d + 3, :].rearrange("p a n -> p (a n)"),
                                   pg[:, 2 * b + d, 0:384], ACT.Exp).then_inc(e_ready, 1)
                if h % GH == 3 and h > GH:
                    g = h // GH - 1
                    act.wait_ge(y_gated, g + 1)
                    for t in range(TT):
                        ins = act.activation(turn_buf[:, 0, t, :], xs[:, t, g * U:g * U + U], ACT.Square,
                                             accum_out=ysq[:, t, g:g + 1])
                    ins.then_inc(y_sq, 1)
                if h == SH - 1:
                    act.wait_ge(y_sq, SG - 1)
                    act.activation(yrs[:, :, 0:SG - 1], ysq[:, :, 0:SG - 1], ACT.Sqrt, bias=lnb[:, 0:1],
                                   scale=1.0 / U).then_inc(y_std, 1)
            turn_banks("y", COL["ssm_norm"], None, 0, 4)
            act.wait_ge(y_gated, SG)
            for t in range(TT):
                ins = act.activation(scrap[3].rearrange("p a n -> p (a n)")[:, t * U:(t + 1) * U],
                                     xs[:, t, (SG - 1) * U:SG * U], ACT.Square, accum_out=ysq[:, t, SG - 1:SG])
            link(ins)
            act.activation(yrs[:, :, SG - 1], ysq[:, :, SG - 1], ACT.Sqrt, bias=lnb[:, 0:1], scale=1.0 / U) \
                .then_inc(y_std, 1)
            for n in range(DI // U):
                split(U_SSM_OUT + n + 2)
                if n < 4:
                    turn_banks("y", COL["ssm_norm"], None, n + 4, n + 5)
            ln_std(3)
            act.wait_ge(norm_ready, NORM_AT["ln1_1"] + 1)
            act.dma_start(blk_c, A["consts"][:, CONST["flip"][0]:CONST_W]).then_inc(const_in, 16)
            turn("ln1_1", COL["ln1_g"] + 8, COL["ln1_b"] + 8)

            def lambda_exp():
                act.wait_ge(lam_sum, 1)
                act.activation(lam_e, lam_s, ACT.Exp).then_inc(lam_exp, 1)

            def bias_back(h0):
                for h in (h0, h0 + 1):
                    act.wait_ge(bias_flipped, BH + h + 1)
                    act.copy(rbias[:, h, :], pg[:, 2 + h % 2, 0:384]).then_inc(bias_evac, 1)

            mlp(U_MLP[1], HG_MLP[1], lambda_exp)
            ln_std(4)

            for l in range(DEPTH):
                if l:
                    rms_std(4 + 3 * l + 1, x_new, 4 * (3 + 3 * l))
                turn(f"ffn1_{l}", COL["ffn1"] + 8 * l, None)
                swiglu(U_FFN[2 * l], HG_FFN[2 * l], None if l else bias_back)
                rms_std(4 + 3 * l + 2, x_new, 4 * (4 + 3 * l))
                turn(f"mix_{l}", COL["mix"] + 8 * l, None)
                for n in range(len(MIX_COLS)):
                    u = U_MIX[l] + n
                    if not 5 <= n <= 8:
                        split(u + 2)
                    bank = pg[:, n % 4, :]
                    pair = bank.rearrange("p (c t) -> p c t", c=2)
                    if n in (0, 2):
                        act.wait_ge(unit_done, u + 1)
                        if n == 2:
                            act.wait_ge(u_ready, 4 * l + 2)
                        act.activation(gate, pair, ACT.Sigmoid).then_inc(gate_ready, 1)
                    elif 4 <= n < 8:
                        i = 4 * l + n - 4
                        act.wait_ge(unit_done, u + 1)
                        if i >= 2:
                            act.wait_ge(qk_sum, i - 1)
                        gc = (COL["k_norm"] if n % 2 else COL["q_norm"]) + l
                        act.activation(head_pair(n), bank, ACT.Identity, scale=pcol[:, gc:gc + 1])
                        act.activation(sq[:, i % 2, :], bank, ACT.Square).then_inc(qk_sq, 1)
                        if n > 4:
                            head_expand(l, n - 1)
                        split(u + 3)
                        act.wait_ge(qk_sum, i + 1)
                        if i >= 2:
                            act.wait_ge(qk_spread, i - 1)
                        act.activation(hdev[:, i % 2, :], acc[:, i % 2, 0:8], ACT.Sqrt, bias=lnb[:, 1:2],
                                       scale=1.0 / HD).then_inc(qk_std, 1)
                    elif n >= 8:
                        act.wait_ge(unit_done, u + 1)
                        act.copy(V2[:, :, (n - 8) * U:(n - 7) * U], pair).then_inc(v_ready, 1)
                        if n == 8:
                            head_expand(l, 7)
                split(U_MIX_OUT[l] + 2)
                for s in range(2 * DH + 3):
                    i = 8 * l + s
                    if s < 2 * DH:
                        act.wait_ge(mx2_ready, i + 1)
                        b = s % 4
                        act.activation(prob2[:, b, 0:P], prob2[:, b, 0:P], ACT.Exp, bias=n2[:, s, 0:1],
                                       accum_out=s2[:, s, 0:1])
                        act.activation(prob2[:, b, P:384], prob2[:, b, P:384], ACT.Exp, bias=n2[:, s, 1:2],
                                       accum_out=s2[:, s, 1:2]).then_inc(ex2_done, 1)
                    if s >= 4 and s % 2 == 0:
                        h = DH * l + (s - 4) // 2
                        act.wait_ge(mixT_done, h + 1)
                        if h >= 2:
                            act.wait_ge(o2_done, h - 1)
                        act.copy(pmixT[:, h % 2, :], pg[:, 2 + h % 2, 0:384]).then_inc(mixT_ready, 1)
                    if s >= 6 and s % 2 == 0:
                        o2_out(l, (s - 6) // 2)
                    if s == 7:
                        act.wait_ge(cconv, l + 1)
                        act.activation(osq, cacc, ACT.Square).then_inc(csq, 1)
                    if s == 10:
                        act.wait_ge(csum, l + 1)
                        act.activation(cdev, acc[:, 2, 0:TT], ACT.Sqrt, bias=lnb[:, 1:2],
                                       scale=1.0 / CCH).then_inc(cstd, 1)
                o2_out(l, DH - 1)
                act.wait_ge(o2_evac, DH * (l + 1))
                act.activation(odev, odev, ACT.Sqrt, bias=lnb[:, 1:2], scale=1.0 / P).then_inc(osq_std, 1)
                for c in range(4):
                    if c % 2 == 0:
                        act.wait_ge(cnorm, 2 * l + c // 2 + 1)
                    k = COL["conv_norm"] + 4 * l + c
                    ins = act.activation(c32[:, c, :], osq[:, c, :], ACT.Silu, scale=pcol[:, k:k + 1])
                    if c % 2 == 1:
                        link(ins)
                        act.copy(op_hi[:, 7 + c:9 + c, :], c32[:, c - 1:c + 1, :]).then_inc(c_hi, 1)
                for a in range(2):
                    act.wait_ge(oT_done, 2 * l + a + 1)
                    act.activation(op_hi[:, 12 + 2 * a:14 + 2 * a, :],
                                   pg[:, 2 + a, :].rearrange("p (c t) -> p c t", c=2),
                                   ACT.Identity, scale=sub_g[:, l:l + 1]).then_inc(o2_hi, 1)
                for n in range(1, OUT_UNITS):
                    split(U_MIX_OUT[l] + n + 2)
                rms_std(4 + 3 * l + 3, x_new, 4 * (5 + 3 * l))
                turn(f"ffn2_{l}", COL["ffn2"] + 8 * l, None)
                swiglu(U_FFN[2 * l + 1], HG_FFN[2 * l + 1])

        @block.vector
        def _(dve):
            link = Link(dve, dve_link)

            def split(u, it=None, per=0):
                if u >= N_UNITS or it is None and by_pool(u):
                    return
                dve.wait_ge(hi_ready, at(u + 1, it, per))
                if it is None and by_pool(u - 1):
                    dve.wait_ge(lo_ready, u)
                s = u % RING
                dve.tensor_tensor(w_lo[:, s, :], w_raw[:, s, :], w_hi[:, s, :].bitcast(F32), ALU.subtract) \
                    .then_inc(lo_ready, 1)

            def turn(name, gain=None, u_next=None):
                turn_banks(name, gain, 0, TURN_CHUNKS[TURNS.index(name)] // 2)
                if u_next is not None:
                    split(u_next)

            def turn_banks(name, gain, b0, b1):
                for b in range(b0, b1):
                    k = TURN_BANK[name] + b
                    dve.wait_ge(gained, k + 1)
                    dst = slice(2 * b, 2 * b + 2)
                    hi = op_hi[:, dst, :]
                    if name.startswith("ln"):
                        link(dve.tensor_copy(hi, turn_buf[:, b % 2, :, :]))
                        ins = dve.tensor_tensor(op_lo[:, dst, :], turn_buf[:, b % 2, :, :], hi.bitcast(F32),
                                                ALU.subtract)
                    elif gain is None:
                        ins = dve.tensor_tensor(op_lo[:, dst, :], pg[:, b % 4, :].rearrange("p (c t) -> p c t", c=2),
                                                hi.bitcast(F32), ALU.subtract)
                    else:
                        for c in range(2):
                            j = 2 * b + c
                            ins = dve.scalar_tensor_tensor(out=op_lo[:, j, :], in0=pg[:, b % 4, c * T:(c + 1) * T],
                                                           scalar=pcol[:, gain + j:gain + j + 1],
                                                           in1=op_hi[:, j, :].bitcast(F32),
                                                           op0=ALU.mult, op1=ALU.subtract)
                    ins.then_inc(xt_ready, 1)

            def bank_done(u_last, k, q):
                if q < 3:
                    dve.wait_ge(sum_done, 3 * (k - 1) + q + 1)
                else:
                    dve.wait_ge(unit_done, u_last + 1)

            def rstd_make(k, t):
                dve.wait_ge(std_ready, 2 * (k - 1) + t + 1 if not 4 <= k <= 5 else 2 * t + k + 3)
                link(dve.reciprocal(rstd[:, t:t + 1], std[:, t:t + 1]))

            def ln(u_last, k, apply):
                if k > 1:
                    dve.wait_ge(x_settled, 2 * (k - 1))
                for q in range(4):
                    t, a = q // 2, q % 2
                    bank_done(u_last, k, q)
                    x = X[:, t, a * 512:(a + 1) * 512]
                    dve.scalar_tensor_tensor(out=x, in0=x, scalar=ALPHA, in1=acc[:, q, :], op0=ALU.mult,
                                             op1=ALU.add).then_inc(x_new, 1)
                    dve.wait_ge(x_new, 4 * (k - 1) + q + 1)
                    ins = dve.bn_stats(stats[:, t, a, :], x)
                    if a == 1:
                        link(ins)
                        dve.bn_aggr(mv[:, t, :], stats[:, t, :, :].rearrange("p a n -> p (a n)")) \
                            .then_inc(var_ready, 1)
                    if q == 2:
                        apply(k, 0)
                if k == 4:
                    rms(5, 0)
                apply(k, 1)
                if k == 4:
                    rms(5, 1)

            def normalise(k, t):
                rstd_make(k, t)
                parts = KC // 2 if t else 1
                w = D // parts
                for i in range(parts):
                    dve.tensor_scalar(xn[:, t, i * w:(i + 1) * w], X[:, t, i * w:(i + 1) * w], mv[:, t, 0:1],
                                      rstd[:, t:t + 1], ALU.subtract, ALU.mult).then_inc(norm_ready, 1)

            def settle(k, t):
                if t == 0:
                    dve.wait_ge(rows_in, 128)
                dve.wait_ge(var_ready, 2 * (k - 1) + t + 1)
                for a in range(2):
                    x = X[:, t, a * 512:(a + 1) * 512]
                    ins = dve.scalar_tensor_tensor(out=x, in0=x, scalar=mv[:, t, 0:1],
                                                   in1=gain_row[:, a * 512:(a + 1) * 512],
                                                   op0=ALU.subtract, op1=ALU.mult)
                link(ins)
                rstd_make(k, t)
                for a in range(2):
                    x = X[:, t, a * 512:(a + 1) * 512]
                    dve.scalar_tensor_tensor(out=x, in0=x, scalar=rstd[:, t:t + 1],
                                             in1=bias_row[:, a * 512:(a + 1) * 512],
                                             op0=ALU.mult, op1=ALU.add).then_inc(x_final, 1)

            def rms(k, t):
                rstd_make(k, t)
                dve.tensor_scalar(diag[:, t, :], ident[:, :], rstd[:, t:t + 1], None, ALU.mult) \
                    .then_inc(norm_ready, 1)

            def residual(u_last, k, factor, norm=True):
                for q in range(4):
                    bank_done(u_last, k, q)
                    x = X[:, q // 2, (q % 2) * 512:(q % 2 + 1) * 512]
                    dve.scalar_tensor_tensor(out=x, in0=acc[:, q, :], scalar=factor, in1=x, op0=ALU.mult,
                                             op1=ALU.add).then_inc(x_new, 1)
                    if norm and q == 2:
                        rms(k + 1, 0)
                if norm:
                    rms(k + 1, 1)

            def hidden(h, u_in, make, it=None, per_h=0, per_u=0):
                dve.wait_ge(act_done, at(h + 1, it, per_h))
                if h:
                    dve.wait_ge(h_ready, at(h, it, per_h))
                if u_in is not None:
                    dve.wait_ge(unit_done, at(u_in + 1, it, per_u))
                make().then_inc(h32_ready, 1)

            def hidden_lo(h, it=None, per_h=0, at_chunk=8):
                dve.wait_ge(h_hi, at(h + 1, it, per_h))
                dst = slice(at_chunk, at_chunk + 2)
                dve.tensor_tensor(op_lo[:, dst, :], h32[:, :].rearrange("p (c t) -> p c t", c=2),
                                  op_hi[:, dst, :].bitcast(F32), ALU.subtract).then_inc(h_ready, 1)

            def square():
                return dve.tensor_tensor(h32[:, :], act_buf[:, :], act_buf[:, :], ALU.mult)

            def gated():
                return dve.tensor_tensor(h32[:, :], act_buf[:, :], pg[:, 1, :], ALU.mult)

            def mlp(u0, h0, between=None):
                split(u0 + 2)
                hidden(h0, None, square)
                hidden_lo(h0)
                if between:
                    between()

                def groups(u1, h1, it=None, last=False):
                    for j in range(3):
                        u = u1 + 2 * j
                        split(u + 2, it, 6)
                        hidden(h1 + j, None, square, it, 3, 6)
                        if last and j == 2:
                            hidden_lo(h1 + j, at_chunk=10)
                        split(u + 3, it, 6)
                        if not (last and j == 2):
                            hidden_lo(h1 + j, it, 3)

                with dve.Fori(0, (G1 - 1) // 3 - 1) as it:
                    groups(u0 + 1, h0 + 1, it)
                groups(u0 + 2 * G1 - 7, h0 + G1 - 3, last=True)

            def swiglu(u0, h0):
                split(u0 + 2)
                split(u0 + 3)
                hidden(h0, u0 + 1, gated)
                hidden_lo(h0)

                def group(u, h, it=None, last=False):
                    split(u + 2, it, 3)
                    split(u + 3, it, 3)
                    hidden(h, u + 1, gated, it, 1, 3)
                    if last:
                        hidden_lo(h, at_chunk=10)
                    split(u + 4, it, 3)
                    if not last:
                        hidden_lo(h, it, 1)

                with dve.Fori(0, G2 - 2) as it:
                    group(u0 + 2, h0 + 1, it)
                group(u0 + 3 * G2 - 4, h0 + G2 - 1, last=True)

            def xs_evac(dve, j):
                dve.wait_ge(xsT_done, j + 1)
                dve.tensor_copy(xs[:, :, j * U:j * U + U], acc[:, 2 + j % 2, :].rearrange("p (t n) -> p t n", t=TT)) \
                    .then_inc(xs_ready, 1)

            dve.memset(lnb[:, 0:1], LN_EPS)
            dve.memset(lnb[:, 1:2], EPS2)
            dve.memset(zeros[:, :], 0.0)
            dve.memset(sink[:, AQ:16], NEG).then_inc(fixed_ready, 1)
            split(0)
            turn("x")
            split(1)
            def na_bias_make(h):
                dve.wait_ge(bias_flipped, h + 1)
                dve.tensor_tensor(na_bias[:, h, :, :].rearrange("p a n -> p (a n)"), acc[:, h % 2, :],
                                  att_const("mask_na"), ALU.add).then_inc(bias_ready, 1)

            def rope_sum(dst, plain, turned_ps, width):
                c = width // T
                cos = att_const("cos").unsqueeze(1).broadcast_to([P, c, T])
                sin = att_const("sin").unsqueeze(1).broadcast_to([P, c, T])
                a, b = r_tmp[:, 0, 0:width], r_tmp[:, 1, 0:width]
                v = lambda z: z.rearrange("p (c t) -> p c t", c=c)
                dve.tensor_tensor(v(a), v(turned_ps), sin, ALU.mult)
                link(dve.tensor_tensor(v(b), v(plain), cos, ALU.mult))
                return dve.tensor_tensor(dst, v(a), v(b), ALU.add)

            dve.wait_ge(const_in, 16)
            for n in range(A_UNITS):
                split(U_ATT + n + 2)
                if 5 <= n < 9:
                    na_bias_make(2 * n - 10)
                    na_bias_make(2 * n - 9)
                if n in (1, 2):
                    i = n - 1
                    dve.wait_ge(rot_done, i + 1)
                    link(rope_sum(QT[:, 2 * i:2 * i + 2, :], q_raw[:, i, :], acc[:, i, :], 2 * T))
                if n == 3:
                    dve.wait_ge(rot_done, 3)
                    for j in range(AKV):
                        ins = rope_sum(KT[:, j:j + 1, :], acc[:, 2 + j, 0:T], acc[:, 2 + j, T:2 * T], T)
                        if j == 0:
                            link(ins)
                    ins.then_inc(rope_done, 1)
            for b in range(5):
                dve.wait_ge(par_turned, b + 1)
                dve.tensor_copy(pcol[:, b * P:b * P + ROW_BLOCKS[b]], acc[:, b % 4, 0:ROW_BLOCKS[b]]) \
                    .then_inc(par_ready, 1)
            dve.wait_ge(small_in, 16)
            dve.wait_ge(bias_ready, BH)
            dve.wait_ge(fixed_ready, 1)
            for s in range(AQ + BH + 5):
                h = s
                if h < AQ + BH:
                    dve.wait_ge(score_done, h + 1)
                    if h >= 4:
                        dve.wait_ge(pT_done, h - 3)
                    p = prob[:, h % 4, :, :]
                    mask = att_const("mask_a") if h < AQ else na_bias[:, h - AQ, :, :].rearrange("p a n -> p (a n)")
                    dve.scalar_tensor_tensor(out=p.rearrange("p a n -> p (a n)"), in0=pg[:, h % 2, :], scalar=SCALE,
                                             in1=mask, op0=ALU.mult, op1=ALU.add).then_inc(score_taken, 1)
                g = s - 2
                before = 0 <= g < AQ + BH
                if before:
                    dve.wait_ge(exp_done, g + 1)
                    link.mark(dve.tensor_tensor(pden[:, g, :], psm[:, g, :], pes[:, g, :], ALU.add))
                if h < AQ + BH:
                    dve.wait_ge(score_taken, h + 1)
                    link.mark(dve.tensor_reduce(mx[:, h, :], p, AX.X, ALU.max))
                if before:
                    link.all_but(1 if h < AQ + BH else 0)
                    link.mark(dve.reciprocal(pden[:, g, :], pden[:, g, :]))
                if h < AQ + BH:
                    link.all_but(1 if before else 0)
                    dve.tensor_scalar(nmx[:, h, :], mx[:, h, :], sink[:, h:h + 1], -1.0, ALU.max, ALU.mult) \
                        .then_inc(max_ready, 1)
                if before:
                    link.all_but(0)
                    for qt in range(TT):
                        ins = dve.tensor_scalar(prob[:, g % 4, qt, :], prob[:, g % 4, qt, :], pden[:, g, qt:qt + 1],
                                                None, ALU.mult)
                    ins.then_inc(p_ready, 1)
                if s >= 6 and s % 2 == 0:
                    c = (s - 6) // 2
                    dve.wait_ge(ot_hi, c + 1)
                    dve.tensor_tensor(op_lo[:, 8 + c, :], acc[:, c % 4, 0:T], op_hi[:, 8 + c, :].bitcast(F32),
                                      ALU.subtract).then_inc(ot_ready, 1)
            for n in range(OUT_UNITS - 1):
                split(U_ATT_OUT + n + 2)
            ln(U_MLP[0] - 1, 1, normalise)
            turn("ln1_0", u_next=U_MLP[0] + 1)
            mlp(U_MLP[0], HG_MLP[0])
            ln(U_SSM - 1, 2, normalise)
            turn("ln2_0", u_next=U_SSM + 1)

            dve.memset(one_col, 1.0)
            dve.memset(conv_in[:, :, :, 0:2], 0.0)
            link(dve.memset(conv_in[:, :, :, 2 + T:], 0.0))
            i = 0
            for n in range(len(SSM_COLS)):
                split(U_SSM + n + 2)
                if n == DT_AT:
                    dve.wait_ge(unit_done, U_SSM + n + 1)
                    dve.wait_ge(small_in, 64)
                    dve.tensor_tensor(dt_v, pg[:, n % 4, 0:128].rearrange("p (t n) -> p t n", t=TT),
                                      dt_bias.unsqueeze(1).broadcast_to([P, TT, 64]), ALU.add).then_inc(dt_sum, 1)
                    dve.wait_ge(dt_soft, 2)
                    dve.scalar_tensor_tensor(out=dt_tok, in0=dt_v, scalar=0.0, in1=dt_a, op0=ALU.max,
                                             op1=ALU.add).then_inc(dt_ready, 1)
                    continue
                if n == DT_AT + 2:
                    dve.wait_ge(dtT_done, 1)
                    link(dve.tensor_scalar(aT[0:64, :], acc[0:64, 0, 0:T], a_col[0:64, :], -1.0, ALU.mult, ALU.mult))
                    link(dve.tensor_tensor_scan(gT[0:64, :], one_col[0:64, :].broadcast_to([64, T]), aT[0:64, :],
                                                0.0, ALU.mult, ALU.add))
                    link(dve.tensor_tensor(gT[32:64, :], aT[32:64, :], gT[32:64, :], ALU.subtract))
                    twice = gT[0:64, :].rearrange("p (t n) -> p t n", t=TT).unsqueeze(2).broadcast_to([64, TT, 2, P])
                    link(dve.tensor_copy(g_pair[0:64, :, :, :], twice))
                    link(dve.tensor_tensor(gT[0:64, :].rearrange("p (t n) -> p t n", t=TT),
                                           gT[0:64, :].rearrange("p (t n) -> p t n", t=TT),
                                           g_pair[0:64, :, 0, :].bitcast(F32), ALU.subtract))
                    dve.tensor_copy(g_pair[64:128, :, :, :], twice).then_inc(g_ready, 1)
                if n < len(SSM_COLS) - Z_UNITS:
                    dve.wait_ge(conv_evac, i + 1)
                    if i >= 2:
                        dve.wait_ge(conv_silu, i - 1)
                    for k in range(CONV):
                        for c in range(2):
                            wc = COL["ssm_conv_w"] + 32 * k + (16 + 2 * i + c) % 32
                            src = conv_in[:, i % 2, c, k:k + T]
                            dst = conv_sum[:, i % 2, c, :]
                            if k == 0:
                                ins = dve.tensor_scalar(dst, src, pcol[:, wc:wc + 1], None, ALU.mult)
                            else:
                                link.all_but(1 if (k, c) < (CONV - 1, 1) else 0)
                                ins = dve.scalar_tensor_tensor(out=dst, in0=src, scalar=pcol[:, wc:wc + 1], in1=dst,
                                                               op0=ALU.mult, op1=ALU.add)
                            if (k, c) < (CONV - 1, 1):
                                link.mark(ins)
                    ins.then_inc(conv_done, 1)
                    i += 1
                    if i >= 11:
                        xs_evac(dve, i - 11)
                elif i == 16:
                    xs_evac(dve, 6)
                    xs_evac(dve, 7)
                    i += 1
            dve.wait_ge(const_in, 32)

            def y_make(g):
                dve.wait_ge(head_done, GH * (g + 1))
                dve.wait_ge(skip_ready, g + 1)
                yg = xs[:, :, g * U:g * U + U]
                link(dve.tensor_tensor(yg, acc[:, g % 2, :].rearrange("p (t n) -> p t n", t=TT), xD[g % 2],
                                       ALU.add))
                dve.wait_ge(z_ready, Z_UNITS)
                dve.tensor_tensor(yg, yg, silz[:, :, g * U:g * U + U], ALU.mult).then_inc(y_gated, 1)

            for h in range(SH):
                g = h // GH
                if h % GH == 0:
                    dve.wait_ge(cb_done, g + 1)
                cb = acc[:, 2 + g % 2, :]
                for d, st, a, z, l0 in ((0, 0, 0, 2, 0), (0, 1, 2, 3, P), (1, 0, 3, 4, 0), (1, 1, 4, 6, 0)):
                    if st == 0:
                        dve.wait_ge(e_ready, 2 * h + d + 1)
                    e = E[:, h % 4, a:z, :].rearrange("p a n -> p (a n)")
                    o = st * T + l0
                    ins = dve.scalar_tensor_tensor(out=e, in0=e, scalar=dt_tok[:, st, d * SH + h:d * SH + h + 1],
                                                   in1=cb[:, o:o + (z - a) * P], op0=ALU.mult, op1=ALU.mult)
                ins.then_inc(m_ready, 1)
                if h % GH == 2 and g:
                    y_make(g - 1)
            y_make(SG - 1)

            def group_norm(g0, g1):
                link(dve.reciprocal(yrs[:, :, g0:g1], yrs[:, :, g0:g1]))
                for g in range(g0, g1):
                    for t in range(TT):
                        ins = dve.tensor_scalar(xs[:, t, g * U:g * U + U], xs[:, t, g * U:g * U + U],
                                                yrs[:, t, g:g + 1], None, ALU.mult)
                    ins.then_inc(norm_ready, 1)

            dve.wait_ge(y_std, 1)
            group_norm(0, SG - 1)
            turn_banks("y", COL["ssm_norm"], 0, 4)
            dve.wait_ge(y_std, 2)
            group_norm(SG - 1, SG)
            for n in range(DI // U):
                if n < DI // U - 1:
                    split(U_SSM_OUT + n + 2)
                if n < 4:
                    turn_banks("y", COL["ssm_norm"], n + 4, n + 5)
            ln(U_MLP[1] - 1, 3, normalise)
            turn("ln1_1", u_next=U_MLP[1] + 1)
            def second_block_prep():
                dve.wait_ge(lam_in, 80)
                link(dve.tensor_tensor(lam_q, lam_q, lam_k, ALU.mult))
                dve.tensor_reduce(lam_s, lam_q, AX.X, ALU.add).then_inc(lam_sum, 1)
                dve.wait_ge(rel_sum, 1)
                dve.tensor_copy(rvec[0:DH, :], pg[0:DH, 3, 0:384]).then_inc(rel_row, 1)
                dve.memset(ones_m[:, 0:1], 1.0)
                dve.memset(uu[:, :, 0:CK - 1], 0.0)
                dve.wait_ge(lam_exp, 1)
                for l in range(DEPTH):
                    link(dve.tensor_tensor(nlam[:, l:l + 1], lam_e[:, 2 + l:3 + l], lam_e[:, l:l + 1], ALU.subtract))
                    link(dve.tensor_scalar(nlam[:, l:l + 1], nlam[:, l:l + 1], -lambda_init(l), None, ALU.add))
                    link(dve.tensor_scalar(sub_g[:, l:l + 1], pcol[:, COL["subln"] + l:COL["subln"] + l + 1],
                                           1.0 - lambda_init(l), None, ALU.mult))

            mlp(U_MLP[1], HG_MLP[1], second_block_prep)
            ln(U_SECOND - 1, 4, settle)
            for l in range(DEPTH):
                turn(f"ffn1_{l}", COL["ffn1"] + 8 * l, U_FFN[2 * l] + 1)
                swiglu(U_FFN[2 * l], HG_FFN[2 * l])
                residual(U_MIX[l] - 1, 5 + 3 * l, 0.5)
                turn(f"mix_{l}", COL["mix"] + 8 * l, U_MIX[l] + 1)

                def gated_columns(n):
                    dve.wait_ge(unit_done, U_MIX[l] + n + 1)
                    dve.wait_ge(gate_ready, 2 * l + (n + 1) // 2)
                    dve.tensor_tensor(uu[:, n - 1:n + 1, CK - 1:],
                                      pg[:, n % 4, :].rearrange("p (c t) -> p c t", c=2), gate, ALU.mult) \
                        .then_inc(u_ready, 2)
                    dve.wait_ge(u_ready, 4 * l + n + 1)

                count = [CK, CK, CK, CK - POOL_TAPS]
                taps = [(k, c) for k in range(TAPS[0]) for c in (0, 1)]
                left = [[(k, c) for k in range(TAPS[0] if c < 2 else 0, count[c])] for c in range(4)]
                taps += [tap for _, tap in sorted(((j + 0.5) / len(some), tap) for some in left
                                                  for j, tap in enumerate(some))]
                done = [0]
                last = {}

                def convolve_on(i):
                    for k, c in taps[done[0]:done[0] + 2 * TAPS[i]]:
                        wc = COL["conv_w"] + l * P + 4 * k + c
                        w = pcol[:, wc:wc + 1]
                        if k == 0:
                            bc = COL["conv_b"] + 4 * l + c
                            ins = dve.tensor_scalar(cacc[:, c, :], uu[:, c, 0:T], w, pcol[:, bc:bc + 1],
                                                    ALU.mult, ALU.add)
                        else:
                            link.all_but(link.n - last[c])
                            ins = dve.scalar_tensor_tensor(out=cacc[:, c, :], in0=uu[:, c, k:k + T], scalar=w,
                                                           in1=cacc[:, c, :], op0=ALU.mult, op1=ALU.add)
                        link.mark(ins)
                        last[c] = link.n
                    done[0] += 2 * TAPS[i]
                    if i == len(TAPS) - 1:
                        dve.wait_ge(pool_conv, l + 1)
                        link.all_but(0)
                        dve.tensor_tensor(cacc[:, 3, :], cacc[:, 3, :], pool_acc, ALU.add).then_inc(cconv, 1)

                def head_rstd(n):
                    i = 4 * l + n - 4
                    dve.wait_ge(qk_std, i + 1)
                    dve.reciprocal(hdev[:, i % 2, :], hdev[:, i % 2, :]).then_inc(qk_rstd, 1)

                def head_norm(n):
                    i = 4 * l + n - 4
                    dve.wait_ge(qk_spread, i + 1)
                    dst = head_pair(n)
                    dve.tensor_tensor(dst, dst, acc[:, 2 + i % 2, :], ALU.mult).then_inc(qk_ready, 1)

                gated_columns(1)
                convolve_on(0)
                gated_columns(3)
                for n in range(4, 8):
                    convolve_on(n - 3)
                    if n > 4:
                        head_norm(n - 1)
                    head_rstd(n)
                convolve_on(5)
                head_norm(7)
                for s in range(2 * DH + 2):
                    i = 8 * l + s
                    if s < 2 * DH:
                        h = s // 2
                        dve.wait_ge(sc2_done, i + 1)
                        b = s % 4
                        dve.scalar_tensor_tensor(out=prob2[:, b, :], in0=pg[:, s % 2, 0:384], scalar=SCALE,
                                                 in1=rbias[:, h, :], op0=ALU.mult, op1=ALU.add) \
                            .then_inc(sc2_taken, 1)
                    mix = s >= 3 and s % 2 == 1
                    if mix:
                        h = (s - 3) // 2
                        k = DH * l + h
                        dve.wait_ge(ex2_done, 8 * l + 2 * h + 2)
                        link.mark(dve.reciprocal(r2[:, 2 * h:2 * h + 2, :], s2[:, 2 * h:2 * h + 2, :]))
                    if s < 2 * DH:
                        dve.wait_ge(sc2_taken, i + 1)
                        dve.tensor_reduce(m2[:, s, 0:1], prob2[:, b, 0:P], AX.X, ALU.max)
                        link.mark(dve.tensor_reduce(m2[:, s, 1:2], prob2[:, b, P:384], AX.X, ALU.max))
                    if mix:
                        link.all_but(1 if s < 2 * DH else 0)
                        link.mark(dve.tensor_scalar(r2[:, 2 * h + 1, :], r2[:, 2 * h + 1, :], nlam[:, l:l + 1], None,
                                                    ALU.mult))
                    if s < 2 * DH:
                        link.all_but(1 if mix else 0)
                        dve.tensor_scalar(n2[:, s, :], m2[:, s, :], -1.0, None, ALU.mult).then_inc(mx2_ready, 1)
                    if s + 7 < len(TAPS):
                        convolve_on(s + 6)
                    if s == 7:
                        convolve_on(len(TAPS) - 1)
                    if mix:
                        if k >= 2:
                            dve.wait_ge(mixT_done, k - 1)
                        link.all_but(0)
                        b0, b1 = (2 * h) % 4, (2 * h + 1) % 4
                        for a, z, qt in ((0, P, 0), (P, 384, 1)):
                            link.mark(dve.tensor_scalar(pmix[:, k % 2, a:z], prob2[:, b0, a:z],
                                                        r2[:, 2 * h, qt:qt + 1], None, ALU.mult))
                        for a, z, qt in ((0, P, 0), (P, 384, 1)):
                            link.all_but(1 - qt)
                            ins = dve.scalar_tensor_tensor(out=pmix[:, k % 2, a:z], in0=prob2[:, b1, a:z],
                                                           scalar=r2[:, 2 * h + 1, qt:qt + 1],
                                                           in1=pmix[:, k % 2, a:z], op0=ALU.mult, op1=ALU.add)
                        ins.then_inc(mix_ready, 1)
                dve.wait_ge(csq, l + 1)
                link(dve.tensor_tensor(osq[:, 0:2, :], osq[:, 0:2, :], osq[:, 2:4, :], ALU.add))
                dve.tensor_tensor(osq[:, 0, :], osq[:, 0, :], osq[:, 1, :], ALU.add).then_inc(cpair, 1)
                dve.wait_ge(cstd, l + 1)
                dve.reciprocal(cdev, cdev).then_inc(crstd, 1)
                dve.wait_ge(cspread, l + 1)
                for a in range(2):
                    dve.tensor_tensor(osq[:, 2 * a:2 * a + 2, :], cacc[:, 2 * a:2 * a + 2, :],
                                      acc[:, 3, 0:T].unsqueeze(1).broadcast_to([P, 2, T]), ALU.mult).then_inc(cnorm, 1)
                dve.wait_ge(osq_std, l + 1)
                link(dve.reciprocal(odev, odev))
                for a in range(2):
                    o = O2[:, 2 * a:2 * a + 2, :].rearrange("p h (t n) -> p (h t) n", t=TT)
                    dve.tensor_tensor(o, o, odev[:, a, :].unsqueeze(2).broadcast_to([P, 2 * TT, P]), ALU.mult) \
                        .then_inc(o2_norm, 1)
                for a in range(2):
                    dve.wait_ge(c_hi, 2 * l + a + 1)
                    dve.tensor_tensor(op_lo[:, 8 + 2 * a:10 + 2 * a, :], c32[:, 2 * a:2 * a + 2, :],
                                      op_hi[:, 8 + 2 * a:10 + 2 * a, :].bitcast(F32), ALU.subtract).then_inc(c_ready, 1)
                for a in range(2):
                    dve.wait_ge(o2_hi, 2 * l + a + 1)
                    dve.scalar_tensor_tensor(out=op_lo[:, 12 + 2 * a:14 + 2 * a, :],
                                             in0=pg[:, 2 + a, :].rearrange("p (c t) -> p c t", c=2),
                                             scalar=sub_g[:, l:l + 1],
                                             in1=op_hi[:, 12 + 2 * a:14 + 2 * a, :].bitcast(F32),
                                             op0=ALU.mult, op1=ALU.subtract).then_inc(o2_ready, 1)
                for n in range(OUT_UNITS - 1):
                    split(U_MIX_OUT[l] + n + 2)
                residual(U_FFN[2 * l + 1] - 1, 6 + 3 * l, 1.0)
                turn(f"ffn2_{l}", COL["ffn2"] + 8 * l, U_FFN[2 * l + 1] + 1)
                swiglu(U_FFN[2 * l + 1], HG_FFN[2 * l + 1])
                residual((U_FFN + [N_UNITS])[2 * l + 2] - 1, 7 + 3 * l, 0.5, norm=l < DEPTH - 1)

        @block.tensor
        def _(pe):
            def take(u, it=None, per=0):
                pe.wait_ge(lo_ready, at(u + 1, it, per))

            def three(psum, w, x, first, last, swap=False):
                terms = ((0, 0), (1, 0), (0, 1))
                for i, (a, b) in enumerate(terms):
                    l, r = (x[b], w[a]) if swap else (w[a], x[b])
                    ins = pe.matmul(psum, l, r, start=first and i == 0, stop=last and i == 2)
                return ins

            def wslice(u, a, z):
                s = u % RING
                return w_hi[:, s, a:z], w_lo[:, s, a:z]

            def feature_chunk(u, bank, c, step=U, fresh=None):
                for k in range(KC):
                    if fresh and c == 0 and k and k % 2 == 0:
                        pe.wait_ge(xt_ready, TURN_BANK[fresh] + k // 2 + 1)
                    o = k * step + c * P
                    ins = three(bank, wslice(u, o, o + P), (op_hi[:, k, :], op_lo[:, k, :]), k == 0, k == KC - 1)
                return ins

            def token_tile(u, bank, t, c0, width, step=U):
                for k in range(KC):
                    o = k * step + c0
                    ts = slice(t * P, t * P + P)
                    ins = three(bank, wslice(u, o, o + width), (op_hi[:, k, ts], op_lo[:, k, ts]), k == 0,
                                k == KC - 1, swap=True)
                return ins

            def project(u, bank, tokens=False, it=None, per=0, fresh=None):
                take(u, it, per)
                if fresh:
                    pe.wait_ge(xt_ready, TURN_BANK[fresh] + 1)
                for c in range(2):
                    o = bank[:, c * T:(c + 1) * T]
                    ins = token_tile(u, o, c, 0, U) if tokens else feature_chunk(u, o, c, fresh=fresh)
                ins.then_inc(unit_done, 1)

            def output(u, chunk, first, last, it=None, per=0):
                take(u, it, per)

                def add(k, t, h):
                    ts = slice(t * P, t * P + P)
                    o = k * D + h * 512
                    return three(acc[:, 2 * t + h, :], wslice(u, o, o + 512),
                                 (op_hi[:, chunk + k, ts], op_lo[:, chunk + k, ts]),
                                 first and k == 0, last and k == 1, swap=True)

                if not last:
                    for k in range(2):
                        for t in range(TT):
                            for h in range(2):
                                ins = add(k, t, h)
                else:
                    for q in range(4):
                        for k in range(2):
                            ins = add(k, q // 2, q % 2)
                        if q < 3:
                            ins.then_inc(sum_done, 1)
                ins.then_inc(unit_done, 1)

            def turn_chunk(src, j, t):
                o = pg[:, j // 2 % 4, (j % 2) * T + t * P:(j % 2) * T + t * P + P]
                if src is None:
                    return pe.matmul(o, X[:, t, j * P:(j + 1) * P], diag[:, t, :], start=True, stop=True)
                return pe.transpose(o, src[:, t, j * P:(j + 1) * P], ident[:, :])

            def turn(name, src):
                n = TURNS.index(name)
                ready = NORM_AT[name]
                if name == "x":
                    pe.wait_ge(ident_in, 16)
                for t in range(TT):
                    if name == "x":
                        pe.wait_ge(x_in[t], 16)
                    elif t == 0 or NORM_PARTS[n] == 2:
                        pe.wait_ge(norm_ready, ready + t + 1)
                    for j in range(KC):
                        if NORM_PARTS[n] > 2 and t == 1 and j % 2 == 0:
                            pe.wait_ge(norm_ready, ready + 2 + j // 2)
                        ins = turn_chunk(src, j, t)
                        if t == 1 and j % 2 == 1:
                            ins.then_inc(turned, 1)

            def turn_group(g):
                pe.wait_ge(norm_ready, NORM_AT["y"] + g + 1)
                if g >= 4:
                    pe.wait_ge(xt_ready, TURN_BANK["y"] + g - 3)
                for c in range(2):
                    for t in range(TT):
                        ins = turn_chunk(xs, 2 * g + c, t)
                ins.then_inc(turned, 1)

            def mlp(u0, h0, fresh, between=None):
                project(u0, pg[:, 0, :], fresh=fresh)
                if between:
                    between()

                def groups(u1, h1, it=None):
                    for j in range(3):
                        project(u1 + 2 * j, pg[:, (1 + j) % 3, :], False, it, 6)
                        pe.wait_ge(h_ready, at(h1 + j, it, 3))
                        output(u1 + 1 + 2 * j, 8, False, False, it, 6)

                with pe.Fori(0, (G1 - 1) // 3 - 1) as it:
                    groups(u0 + 1, h0 + 1, it)
                groups(u0 + 2 * G1 - 7, h0 + G1 - 3)
                pe.wait_ge(h_ready, h0 + G1)
                output(u0 + 2 * G1 - 1, 10, False, True)

            def swiglu(u0, h0, fresh, between=None):
                project(u0, pg[:, 0, :], fresh=fresh)
                project(u0 + 1, pg[:, 1, :])
                if between:
                    between(0)

                def group(u, h, it=None):
                    pe.wait_ge(act_done, at(h, it, 1))
                    project(u, pg[:, 0, :], False, it, 3)
                    pe.wait_ge(h32_ready, at(h, it, 1))
                    project(u + 1, pg[:, 1, :], False, it, 3)
                    pe.wait_ge(h_ready, at(h, it, 1))
                    output(u + 2, 8, False, False, it, 3)

                with pe.Fori(0, G2 - 2) as it:
                    group(u0 + 2, h0 + 1, it)
                if between:
                    between(2)
                group(u0 + 3 * G2 - 4, h0 + G2 - 1)
                pe.wait_ge(h_ready, h0 + G2)
                output(u0 + 3 * G2 - 1, 10, False, True)

            def clear_sums():
                for b in range(4):
                    pe.matmul(acc[:, b, :], zeros[:, 0:1].broadcast_to([P, P]), zeros[:, 0:1].broadcast_to([P, 512]),
                              start=True, stop=False)

            def qk_sums(i):
                pe.wait_ge(qk_sq, i + 1)
                for c in range(2):
                    for t in range(TT):
                        o = c * T + t * P
                        k = (c * TT + t) * 2
                        ins = pe.matmul(acc[:, i % 2, k:k + 2], sq[:, i % 2, o:o + P], blk_const("halves")[:, ::HD],
                                        start=True, stop=True)
                ins.then_inc(qk_sum, 1)

            def qk_spreads(i):
                pe.wait_ge(qk_exp, i + 1)
                for c in range(2):
                    for t in range(TT):
                        k = (c * TT + t) * 2
                        ins = pe.matmul(acc[:, 2 + i % 2, c * T + t * P:c * T + t * P + P],
                                        hexp[:, i % 2, k * HD:(k + 2) * HD], ident[:, :], start=True, stop=True)
                ins.then_inc(qk_spread, 1)

            def o2(l, h):
                k = DH * l + h
                pe.wait_ge(mixT_ready, k + 1)
                if h >= 2:
                    pe.wait_ge(o2_evac, k - 1)
                v = V2[:, 0, h * P:h * P + P], V2[:, 1, h * P:h * P + P]
                p = [pmixT[:, k % 2, a:a + P] for a in (0, P, 2 * P)]
                pe.matmul(acc[:, h % 2, 0:P], p[0], v[0], start=True, stop=True)
                pe.matmul(acc[:, h % 2, P:T], p[1], v[0], start=True, stop=False)
                pe.matmul(acc[:, h % 2, P:T], p[2], v[1], start=False, stop=True).then_inc(o2_done, 1)

            turn("x", X)
            for n in range(A_UNITS):
                u = U_ATT + n
                if n >= 4:
                    pe.wait_ge(attn_evac, n - 3)
                bank = pg[:, n % 4, :]
                if n == 2:
                    take(u)
                    feature_chunk(u, bank[:, 0:T], 0)
                    for t in range(TT):
                        ins = token_tile(u, bank[:, T + t * P:T + t * P + P], t, P, P)
                    ins.then_inc(unit_done, 1)
                else:
                    project(u, bank, tokens=n >= 7, fresh="x" if n == 0 else None)
                if n in (1, 2):
                    i = n - 1
                    if n == 1:
                        pe.wait_ge(const_in, 16)
                    pe.wait_ge(attn_evac, i + 1)
                    pe.matmul(acc[:, i, :], att_const("rot"), q_raw[:, i, :], start=True, stop=True) \
                        .then_inc(rot_done, 1)
                if 4 <= n < 8:
                    if n == 4:
                        pe.wait_ge(bias_in, 16 * BH * 4)
                        pe.wait_ge(rope_done, 1)
                    for h in (2 * n - 8, 2 * n - 7):
                        if h >= 2:
                            pe.wait_ge(bias_ready, h - 1)
                        pe.matmul(acc[:, h % 2, :], att_const("na_flip"),
                                  na_bias[:, h, :, :].rearrange("p a n -> p (a n)"), start=True, stop=True) \
                            .then_inc(bias_flipped, 1)
                if n == 8:
                    pe.wait_ge(par_in, 16 * N_PAR)
                    pe.wait_ge(bias_ready, BH)
                    for b in range(5):
                        r = ROW_BLOCKS[b]
                        if b >= 4:
                            pe.wait_ge(par_ready, b - 3)
                        pe.transpose(acc[:, b % 4, 0:r], prow[0:r, b, :], ident[0:r, 0:r]).then_inc(par_turned, 1)
                if n == 3:
                    pe.wait_ge(attn_evac, 3)
                    for j in range(AKV):
                        pe.matmul(acc[:, 2 + j, 0:T], att_const(f"dup{j}"), k_raw, start=True, stop=True)
                        ins = pe.matmul(acc[:, 2 + j, T:2 * T], att_const(f"rdup{j}"), k_raw, start=True, stop=True)
                    ins.then_inc(rot_done, 1)
            pe.wait_ge(par_ready, 5)
            pe.wait_ge(attn_evac, A_UNITS)
            for s in range(AQ + BH + 4):
                h = s
                if h < AQ + BH:
                    if h >= 2:
                        pe.wait_ge(score_taken, h - 1)
                    p0 = (h % 2) * HD
                    ki = h // 4 if h < AQ else 2 + (h - AQ) // 2
                    for qt in range(TT):
                        ins = pe.matmul(pg[:, h % 2, qt * T:(qt + 1) * T],
                                        QT[p0:p0 + HD, h // 2, qt * P:qt * P + P], KT[p0:p0 + HD, ki, :],
                                        start=True, stop=True)
                    ins.then_inc(score_done, 1)
                h = s - 3
                if 0 <= h < AQ + BH:
                    pe.wait_ge(p_ready, h + 1)
                    if h >= 2:
                        pe.wait_ge(pt_ready, h - 1)
                    for kt in range(TT):
                        for qt in range(TT):
                            ins = pe.transpose(pg[:, 2 + h % 2, kt * T + qt * P:kt * T + qt * P + P],
                                               prob[:, h % 4, qt, kt * P:kt * P + P], ident[:, :])
                    ins.then_inc(pT_done, 1)
                h = s - 4
                if 0 <= h < AQ + BH:
                    pe.wait_ge(pt_ready, h + 1)
                    c = h // 2
                    if c >= 4 and h % 2 == 0:
                        pe.wait_ge(ot_ready, c - 3)
                    p0 = (h % 2) * HD
                    for kt in range(TT):
                        v = va[:, kt, (h // 4) * HD:(h // 4 + 1) * HD] if h < AQ \
                            else vb[:, kt, (h - AQ) * HD:(h - AQ + 1) * HD]
                        ins = pe.matmul(acc[p0:p0 + HD, c % 4, 0:T], v, probT[:, h % 2, kt, :], start=kt == 0,
                                        stop=kt == TT - 1)
                    ins.then_inc(pv_done, 1)
            pe.wait_ge(ot_ready, 8)
            for n in range(OUT_UNITS):
                output(U_ATT_OUT + n, 8 + 2 * n, n == 0, n == OUT_UNITS - 1)
            turn("ln1_0", xn)
            clear_sums()
            mlp(U_MLP[0], HG_MLP[0], "ln1_0")
            turn("ln2_0", xn)

            i = 0
            for n in range(len(SSM_COLS)):
                u = U_SSM + n
                bank = pg[:, n % 4, :]
                if n >= 4:
                    m = n - 4
                    if m < DT_AT:
                        pe.wait_ge(conv_evac, m + 1)
                    elif m == DT_AT:
                        pe.wait_ge(dt_sum, 1)
                    elif m < 17:
                        pe.wait_ge(conv_evac, m)
                    else:
                        pe.wait_ge(z_ready, m - 16)
                if n == DT_AT:
                    take(u)
                    for t in range(TT):
                        ins = token_tile(u, bank[:, t * 64:t * 64 + 64], t, 0, 64, step=64)
                    ins.then_inc(unit_done, 1)
                    continue
                project(u, bank, tokens=n >= 17, fresh="ln2_0" if n == 0 else None)
                if n == DT_AT + 1:
                    pe.wait_ge(dt_ready, 1)
                    for t in range(TT):
                        ins = pe.transpose(acc[0:64, 0, t * P:t * P + P], dt_tok[:, t, :], ident[:, :])
                    ins.then_inc(dtT_done, 1)
                if n >= 11 and n < 19:
                    j = n - 11
                    pe.wait_ge(conv_silu, j + 9)
                    if j >= 2:
                        pe.wait_ge(xs_ready, j - 1)
                    for t in range(TT):
                        for c in range(2):
                            ins = pe.transpose(acc[:, 2 + j % 2, t * U + c * P:t * U + c * P + P],
                                               xsT[:, j % 2, c, t * P:t * P + P], ident[:, :])
                    ins.then_inc(xsT_done, 1)

            def cb(g):
                if g >= 2:
                    pe.wait_ge(m_ready, GH * (g - 1))
                for st in range(TT):
                    ins = pe.matmul(acc[:, 2 + g % 2, st * T:(st + 1) * T], BT[:, g, st * P:st * P + P], CT[:, g, :],
                                    start=True, stop=True)
                ins.then_inc(cb_done, 1)

            def diff(h):
                b = h % 2
                for d in range(2):
                    o, r = pg[:, 2 * b + d, 0:384], d * SH + h
                    if h >= 2:
                        pe.wait_ge(e_ready, 2 * (h - 2) + d + 1)
                    g = g_pair[:, :, :, :].rearrange("p t a n -> p (t a n)")[:, (1 - d) * P:(4 - d) * P]
                    pe.matmul(o, select[:, r:r + 1].broadcast_to([P, P]), g, start=True, stop=False)
                    for st, a, z in ((0, 0, (2 - d) * P), (1, (2 - d) * P, 3 * P)):
                        pe.matmul(o[:, a:z], g_pair[:, st, 0, :], nselect[:, r:r + 1].broadcast_to([P, z - a]),
                                  start=False, stop=False)
                    o = o.rearrange("p (a n) -> p a n", n=P)[:, 0:3:2, :]
                    pe.matmul(o, ident_r[:, :], neg_tri[:, d:d + 1, :].broadcast_to([P, 2, P]), start=False,
                              stop=True).then_inc(diff_done, 1)

            def y(h):
                g = h // GH
                e0 = (h % GH) * HD
                pe.wait_ge(e_sum, h + 1)
                if h % GH == 0 and g >= 2:
                    pe.wait_ge(y_gated, g - 1)
                for lt, terms in enumerate((((0, 0), (4, 1)), ((1, 0), (2, 1)))):
                    for i_, (a, st) in enumerate(terms):
                        ins = pe.matmul(acc[:, g % 2, lt * U + e0:lt * U + e0 + HD], E[:, h % 4, a, :],
                                        xs[:, st, h * HD:(h + 1) * HD], start=i_ == 0, stop=i_ == 1)
                ins.then_inc(head_done, 1)

            pe.wait_ge(z_ready, Z_UNITS)
            pe.wait_ge(xs_ready, 8)
            pe.wait_ge(g_ready, 1)
            pe.wait_ge(sel_ready, 1)
            cb(0)
            diff(0)
            diff(1)
            for h in range(SH):
                if h + 2 < SH:
                    if (h + 2) % GH == 0:
                        cb((h + 2) // GH)
                    diff(h + 2)
                y(h)
            for g in range(4):
                turn_group(g)
            pe.wait_ge(y_gated, SG)
            for n in range(DI // U):
                if 1 <= n < 5:
                    turn_group(n + 3)
                pe.wait_ge(xt_ready, TURN_BANK["y"] + n + 1)
                output(U_SSM_OUT + n, 2 * n, n == 0, n == DI // U - 1)
            turn("ln1_1", xn)

            def distance_bias():
                pe.wait_ge(lam_in, 80)
                pe.wait_ge(const_in, CONST_BLK)
                pe.matmul(pg[0:DH, 3, 0:384], rel[0:BUCKETS, :], blk_const("buckets")[0:BUCKETS, :], start=True,
                          stop=True).then_inc(rel_sum, 1)

            def bias_strips(h0):
                pe.wait_ge(bias_in, 16 * (BH * 4 + DH * 2))
                if h0:
                    pe.wait_ge(bias_evac, h0)
                for h in (h0, h0 + 1):
                    pe.matmul(pg[:, 2 + h % 2, 0:384], blk_const("flip"), rbias[:, h, :], start=True, stop=True) \
                        .then_inc(bias_flipped, 1)

            clear_sums()
            mlp(U_MLP[1], HG_MLP[1], "ln1_1", distance_bias)

            for l in range(DEPTH):
                turn(f"ffn1_{l}", None)
                clear_sums()
                swiglu(U_FFN[2 * l], HG_FFN[2 * l], f"ffn1_{l}", None if l else bias_strips)
                turn(f"mix_{l}", None)
                for n in range(len(MIX_COLS)):
                    u = U_MIX[l] + n
                    m = n - 4
                    if m in (0, 1):
                        pe.wait_ge(u_ready, 4 * l + 2)
                    elif m in (2, 3):
                        pe.wait_ge(u_ready, 4 * l + 4)
                    elif m >= 4:
                        pe.wait_ge(qk_sq, 4 * l + m - 3)
                    project(u, pg[:, n % 4, :], tokens=n >= 8, fresh=f"mix_{l}" if n == 0 else None)
                    if 6 <= n:
                        qk_spreads(4 * l + n - 6)
                    if 5 <= n < 9:
                        qk_sums(4 * l + n - 5)
                pe.wait_ge(qk_ready, 4 * l + 4)
                pe.wait_ge(v_ready, 2 * l + 2)
                for s in range(2 * DH + 4):
                    i = 8 * l + s
                    if s < 2 * DH:
                        h, m = s // 2, s % 2
                        if s >= 2:
                            pe.wait_ge(sc2_taken, i - 1)
                        p0 = m * HD
                        pe.matmul(pg[:, s % 2, 0:P], Q2[p0:p0 + HD, h, 0:P], K2[p0:p0 + HD, h, 0:P], start=True,
                                  stop=True)
                        pe.matmul(pg[:, s % 2, P:384], Q2[p0:p0 + HD, h, P:T], K2[p0:p0 + HD, h, :], start=True,
                                  stop=True).then_inc(sc2_done, 1)
                    if s >= 4 and s % 2 == 0 and s < 2 * DH + 4:
                        k = DH * l + (s - 4) // 2
                        pe.wait_ge(mix_ready, k + 1)
                        if k >= 2:
                            pe.wait_ge(mixT_ready, k - 1)
                        for o, a in ((0, 0), (P, P), (2 * P, 2 * P)):
                            ins = pe.transpose(pg[:, 2 + k % 2, o:o + P], pmix[:, k % 2, a:a + P], ident[:, :])
                        ins.then_inc(mixT_done, 1)
                    if s >= 5 and s % 2 == 1:
                        o2(l, (s - 5) // 2)
                    if s == 10:
                        pe.wait_ge(cpair, l + 1)
                        for t in range(TT):
                            ins = pe.matmul(acc[:, 2, t:t + 1], osq[:, 0, t * P:(t + 1) * P], ones_m, start=True,
                                            stop=True)
                        ins.then_inc(csum, 1)
                    if s == 2 * DH + 3:
                        pe.wait_ge(crstd, l + 1)
                        for t in range(TT):
                            ins = pe.matmul(acc[:, 3, t * P:(t + 1) * P], cdev[:, t:t + 1].broadcast_to([P, P]),
                                            ident[:, :], start=True, stop=True)
                        ins.then_inc(cspread, 1)
                pe.wait_ge(o2_evac, DH * l + DH)
                for n in range(OUT_UNITS):
                    if n == 0:
                        for a in range(2):
                            pe.wait_ge(o2_norm, 2 * l + a + 1)
                            for h in (2 * a, 2 * a + 1):
                                for t in range(TT):
                                    o = (h % 2) * T + t * P
                                    ins = pe.transpose(pg[:, 2 + a, o:o + P], O2[:, h, t * P:(t + 1) * P], ident[:, :])
                            ins.then_inc(oT_done, 1)
                    pe.wait_ge(c_ready if n < 2 else o2_ready, 2 * l + n % 2 + 1)
                    output(U_MIX_OUT[l] + n, 8 + 2 * n, n == 0, n == OUT_UNITS - 1)
                turn(f"ffn2_{l}", None)
                clear_sums()
                swiglu(U_FFN[2 * l + 1], HG_FFN[2 * l + 1], f"ffn2_{l}")

_INS = ['x', 'attn_w_in', 'attn_sink', 'attn_rpb', 'attn_w_out', 'ssm_w_in', 'ssm_conv_w', 'ssm_conv_b',
        'ssm_dt_bias', 'ssm_A_log', 'ssm_D', 'ssm_norm_w', 'ssm_w_out', 'mlp_w1', 'mlp_w2', 'ln1_g', 'ln1_b',
        'ln2_g', 'ln2_b', 'rel_bias_2', 'ffn1_norm_2', 'ffn1_w_gate_2', 'ffn1_w_up_2', 'ffn1_w_down_2',
        'mix_norm_2', 'w_in_2', 'conv_w_2', 'conv_b_2', 'conv_norm_2', 'q_norm_2', 'k_norm_2', 'lambda_q1_2',
        'lambda_k1_2', 'lambda_q2_2', 'lambda_k2_2', 'subln_norm_2', 'w_out_2', 'ffn2_norm_2',
        'ffn2_w_gate_2', 'ffn2_w_up_2', 'ffn2_w_down_2']


def kernel(**inputs):
    import concourse.bacc as bacc
    from concourse.bass_utils import run_bass_kernel_spmd

    nc = bacc.Bacc("TRN2", target_bir_lowering=False, num_devices=1)
    arrays, args = {}, {}
    for name in _INS:
        a = np.ascontiguousarray(inputs[name])
        arrays["in_" + name] = a
        args[name] = nc.dram_tensor("in_" + name, a.shape, mybir.dt.from_np(a.dtype), kind="ExternalInput").ap()
    c = shape_constants()
    arrays["in_consts"] = c
    args["consts"] = nc.dram_tensor("in_consts", c.shape, F32, kind="ExternalInput").ap()
    out = nc.dram_tensor("out_x", (1, T, D), F32, kind="ExternalOutput").ap()
    two_blocks(nc, args, out)
    r = run_bass_kernel_spmd(nc, [arrays], core_ids=[0])
    return r.results[0]["out_x"]
```
